# Optimizing a Trainium2 kernel written in Bass

```python
import math
import jax, jax.numpy as jnp
from jax import lax
import numpy as np

D_MODEL = 1024
BATCH = 1
SEQ = 512
DEPTH = 2

CHUNK = 64
N_EVEN = (DEPTH + 1) // 2
N_ODD = DEPTH // 2
EPS = 1e-6
LN_EPS = 1e-5
ROPE_THETA = 10000.0

CONV_DIM = D_MODEL
CONV_WIDTH = 31
RWKV_HEAD = 64
RWKV_HEADS = D_MODEL // RWKV_HEAD
RWKV_DIM = RWKV_HEADS * RWKV_HEAD
LORA_DIM = 64
GN_EPS = 64e-5
ATT_HEADS = 16
ATT_HEAD_DIM = 128
ATT_DIM = ATT_HEADS * ATT_HEAD_DIM
IDX_HEADS = 8
IDX_HEAD_DIM = 64
TOPK_MAX = 256
Q_BLOCK = 128

EVEN_SIZES = (CONV_DIM, CONV_DIM, CONV_DIM,
              RWKV_DIM, RWKV_DIM, RWKV_DIM,
              LORA_DIM, LORA_DIM, RWKV_DIM)
EVEN_COLS = sum(EVEN_SIZES)
EVEN_OUT = CONV_DIM + RWKV_DIM
ODD_SIZES = (ATT_DIM, ATT_HEAD_DIM, ATT_HEAD_DIM,
             IDX_HEADS * IDX_HEAD_DIM, IDX_HEAD_DIM, IDX_HEADS,
             ATT_DIM)
ODD_COLS = sum(ODD_SIZES)


def split_cols(z, sizes):
    idx = np.cumsum(sizes)[:-1].tolist()
    return jnp.split(z, idx, axis=-1)

def rms_norm(x, g):
    xf = x.astype(jnp.float32)
    y = xf * lax.rsqrt(jnp.mean(xf * xf, axis=-1, keepdims=True) + EPS)
    return (y * g.astype(jnp.float32)).astype(x.dtype)

def layer_norm(x, w, b, eps):
    xf = x.astype(jnp.float32)
    mu = jnp.mean(xf, axis=-1, keepdims=True)
    var = jnp.mean(jnp.square(xf - mu), axis=-1, keepdims=True)
    y = (xf - mu) * lax.rsqrt(var + eps)
    return (y * w.astype(jnp.float32) + b.astype(jnp.float32)).astype(x.dtype)

def rope(x, pos):
    d = x.shape[-1]
    inv = ROPE_THETA ** (-jnp.arange(0, d, 2, dtype=jnp.float32) / d)
    ang = pos.astype(jnp.float32)[..., None] * inv
    cos = jnp.cos(ang)[:, :, None, :]
    sin = jnp.sin(ang)[:, :, None, :]
    xf = x.astype(jnp.float32)
    x1, x2 = jnp.split(xf, 2, axis=-1)
    out = jnp.concatenate([x1 * cos - x2 * sin, x2 * cos + x1 * sin], axis=-1)
    return out.astype(x.dtype)

def token_shift(z):
    return jnp.pad(z[:, :-1], ((0, 0), (1, 0), (0, 0)))

def conformer_conv(val, glu, conv_w, conv_vec):
    u = val * jax.nn.sigmoid(glu)
    y = lax.conv_general_dilated(u, conv_w.astype(u.dtype), window_strides=(1,),
                                 padding=[(CONV_WIDTH - 1, 0)],
                                 dimension_numbers=('NWC', 'WIO', 'NWC'),
                                 feature_group_count=CONV_DIM)
    y = y + conv_vec[0]
    y = layer_norm(y, conv_vec[1], conv_vec[2], LN_EPS)
    return jax.nn.silu(y)

def rwkv7_step(state, inp):
    r_t, w_t, k_t, v_t, kk_t, a_t = inp
    sa = jnp.einsum('bhvk,bhk->bhv', state, -kk_t)
    state = (state * w_t[:, :, None, :]
             + sa[..., None] * (kk_t * a_t)[:, :, None, :]
             + v_t[..., None] * k_t[:, :, None, :])
    y = jnp.einsum('bhvk,bhk->bhv', state, r_t)
    return state, y

def rwkv7_mix(r, k, v, wd, ad, mu_rkv, mu_lora, vec, w_up, a_up, r_k):
    B, S, _ = r.shape
    f32 = jnp.float32
    lerp = lambda z, mu: z + (token_shift(z) - z) * mu
    r = lerp(r, mu_rkv[0]).astype(f32)
    k = lerp(k, mu_rkv[1]).astype(f32)
    v = lerp(v, mu_rkv[2]).astype(f32)
    wd = lerp(wd, mu_lora[0]).astype(f32)
    ad = lerp(ad, mu_lora[1]).astype(f32)
    vec = vec.astype(f32)
    w0, a0, k_k, k_a, lnx_w, lnx_b = vec[0], vec[1], vec[2], vec[3], vec[4], vec[5]
    w_log = -jax.nn.softplus(-(w0 + jnp.tanh(wd) @ w_up.astype(f32))) - 0.5
    decay = jnp.exp(-jnp.exp(w_log))
    a = jax.nn.sigmoid(a0 + ad @ a_up.astype(f32))
    heads = lambda t: t.reshape(B, S, RWKV_HEADS, RWKV_HEAD)
    kk = heads(k * k_k)
    kk = kk / jnp.maximum(jnp.sqrt(jnp.sum(kk * kk, axis=-1, keepdims=True)), 1e-12)
    k = k * (1.0 + (a - 1.0) * k_a)
    r_h, w_h, k_h, v_h, a_h = heads(r), heads(decay), heads(k), heads(v), heads(a)
    xs = tuple(jnp.moveaxis(t, 1, 0) for t in (r_h, w_h, k_h, v_h, kk, a_h))
    state0 = jnp.zeros((B, RWKV_HEADS, RWKV_HEAD, RWKV_HEAD), f32)
    _, y = lax.scan(rwkv7_step, state0, xs)
    y = jnp.moveaxis(y, 0, 1)
    mu = jnp.mean(y, axis=-1, keepdims=True)
    var = jnp.mean(jnp.square(y - mu), axis=-1, keepdims=True)
    y = ((y - mu) * lax.rsqrt(var + GN_EPS)).reshape(B, S, RWKV_DIM) * lnx_w + lnx_b
    bonus = jnp.sum(r_h * k_h * r_k.astype(f32), axis=-1, keepdims=True) * v_h
    return y + bonus.reshape(B, S, RWKV_DIM)

def dsa_attention(q, k, v, qi, ki, wi, positions):
    B, S = positions.shape
    k_sel = min(TOPK_MAX, S // 4)
    nb = S // Q_BLOCK
    chunk_id = positions // CHUNK
    kf = ki.astype(jnp.float32)

    def to_blocks(t):
        return jnp.moveaxis(t.reshape((B, nb, Q_BLOCK) + t.shape[2:]), 1, 0)

    def block(args):
        qb, qib, wib, cqb = args
        idx_logits = jnp.einsum('bqhd,bsd->bqhs', qib.astype(jnp.float32), kf) * (IDX_HEAD_DIM ** -0.5)
        score = jnp.einsum('bqh,bqhs->bqs', wib.astype(jnp.float32) * (IDX_HEADS ** -0.5),
                           jax.nn.relu(idx_logits))
        adm = chunk_id[:, None, :] <= cqb[:, :, None]
        score = jnp.where(adm, score, -jnp.inf)
        top_val, top_idx = lax.top_k(score, k_sel)
        valid = jnp.isfinite(top_val)
        kg = jax.vmap(lambda kb, ib: kb[ib])(k, top_idx)
        vg = jax.vmap(lambda vb, ib: vb[ib])(v, top_idx)
        logits = jnp.einsum('bqhd,bqkd->bqhk', qb, kg).astype(jnp.float32) * (ATT_HEAD_DIM ** -0.5)
        logits = jnp.where(valid[:, :, None, :], logits, -jnp.inf)
        p = jax.nn.softmax(logits, axis=-1).astype(v.dtype)
        return jnp.einsum('bqhk,bqkd->bqhd', p, vg)

    o = lax.map(block, (to_blocks(q), to_blocks(qi), to_blocks(wi), to_blocks(chunk_id)))
    return jnp.moveaxis(o, 0, 1).reshape(B, S, ATT_DIM)

def first_inputs(seed: int = 0) -> dict:
    key = jax.random.key(seed)
    ks = jax.random.split(key, 24)
    nrm = lambda k, shape, s: jax.random.normal(k, shape, jnp.float32) * s
    x = nrm(ks[0], (BATCH, SEQ, D_MODEL), 1.0)
    c = nrm(ks[1], (BATCH, D_MODEL), 1.0)
    offsets = jax.random.randint(ks[2], (BATCH,), 0, 64, dtype=jnp.int32) * CHUNK
    positions = offsets[:, None] + jnp.arange(SEQ, dtype=jnp.int32)[None, :]
    ada_w = nrm(ks[3], (DEPTH, D_MODEL, 3 * D_MODEL), 0.5 * D_MODEL ** -0.5)
    ada_b = nrm(ks[4], (DEPTH, 3 * D_MODEL), 0.02)
    norm_g = 1.0 + nrm(ks[5], (DEPTH, D_MODEL), 0.05)
    final_g = 1.0 + nrm(ks[6], (D_MODEL,), 0.05)
    even_w_in = nrm(ks[7], (N_EVEN, D_MODEL, EVEN_COLS), D_MODEL ** -0.5)
    even_w_out = nrm(ks[8], (N_EVEN, EVEN_OUT, D_MODEL), EVEN_OUT ** -0.5)
    conv_w = nrm(ks[9], (N_EVEN, CONV_WIDTH, 1, CONV_DIM), CONV_WIDTH ** -0.5)
    kc = jax.random.split(ks[10], 3)
    conv_vec = jnp.stack([nrm(kc[0], (N_EVEN, CONV_DIM), 0.02),
                          1.0 + nrm(kc[1], (N_EVEN, CONV_DIM), 0.05),
                          nrm(kc[2], (N_EVEN, CONV_DIM), 0.02)], axis=1)
    rwkv_mu_rkv = jax.random.uniform(ks[11], (N_EVEN, 3, RWKV_DIM), jnp.float32)
    rwkv_mu_lora = jax.random.uniform(ks[12], (N_EVEN, 2, LORA_DIM), jnp.float32)
    kv = jax.random.split(ks[13], 6)
    rwkv_vec = jnp.stack([
        jax.random.uniform(kv[0], (N_EVEN, RWKV_DIM), jnp.float32, -4.0, 1.0),
        nrm(kv[1], (N_EVEN, RWKV_DIM), 0.1),
        0.85 + nrm(kv[2], (N_EVEN, RWKV_DIM), 0.05),
        1.0 + nrm(kv[3], (N_EVEN, RWKV_DIM), 0.05),
        1.0 + nrm(kv[4], (N_EVEN, RWKV_DIM), 0.05),
        nrm(kv[5], (N_EVEN, RWKV_DIM), 0.02)], axis=1)
    rwkv_w_up = nrm(ks[14], (N_EVEN, LORA_DIM, RWKV_DIM), 0.5 * LORA_DIM ** -0.5)
    rwkv_a_up = nrm(ks[15], (N_EVEN, LORA_DIM, RWKV_DIM), 0.5 * LORA_DIM ** -0.5)
    rwkv_r_k = nrm(ks[16], (N_EVEN, RWKV_HEADS, RWKV_HEAD), 0.1)
    odd_w_in = nrm(ks[17], (N_ODD, D_MODEL, ODD_COLS), D_MODEL ** -0.5)
    odd_w_out = nrm(ks[18], (N_ODD, ATT_DIM, D_MODEL), ATT_DIM ** -0.5)
    return {"x": x, "c": c, "positions": positions, "ada_w": ada_w, "ada_b": ada_b,
            "norm_g": norm_g, "final_g": final_g, "even_w_in": even_w_in,
            "even_w_out": even_w_out, "conv_w": conv_w, "conv_vec": conv_vec,
            "rwkv_mu_rkv": rwkv_mu_rkv, "rwkv_mu_lora": rwkv_mu_lora, "rwkv_vec": rwkv_vec,
            "rwkv_w_up": rwkv_w_up, "rwkv_a_up": rwkv_a_up, "rwkv_r_k": rwkv_r_k,
            "odd_w_in": odd_w_in, "odd_w_out": odd_w_out}

def first_block(x, c, positions, ada_w, ada_b, norm_g, final_g, even_w_in, even_w_out,
              conv_w, conv_vec, rwkv_mu_rkv, rwkv_mu_lora, rwkv_vec, rwkv_w_up, rwkv_a_up,
              rwkv_r_k, odd_w_in, odd_w_out):
    B, S, _ = x.shape
    cond = jax.nn.silu(c)
    for l in range(DEPTH):
        mod = cond @ ada_w[l] + ada_b[l]
        shift, scale, gate = jnp.split(mod, 3, axis=-1)
        h = rms_norm(x, norm_g[l]) * (1.0 + scale[:, None, :]) + shift[:, None, :]
        j = l // 2
        if l % 2 == 0:
            z = h @ even_w_in[j]
            a_val, a_glu, a_gate, r, k, v, wd, ad, b_gate = split_cols(z, EVEN_SIZES)
            ya = conformer_conv(a_val, a_glu, conv_w[j], conv_vec[j]) * jax.nn.silu(a_gate)
            yb = rwkv7_mix(r, k, v, wd, ad, rwkv_mu_rkv[j], rwkv_mu_lora[j], rwkv_vec[j],
                           rwkv_w_up[j], rwkv_a_up[j], rwkv_r_k[j]).astype(h.dtype)
            yb = yb * jax.nn.silu(b_gate)
            out = jnp.concatenate([ya, yb], axis=-1) @ even_w_out[j]
        else:
            z = h @ odd_w_in[j]
            q, k, v, qi, ki, wi, g = split_cols(z, ODD_SIZES)
            q = rope(q.reshape(B, S, ATT_HEADS, ATT_HEAD_DIM), positions)
            k = rope(k[:, :, None, :], positions)[:, :, 0, :]
            qi = rope(qi.reshape(B, S, IDX_HEADS, IDX_HEAD_DIM), positions)
            ki = rope(ki[:, :, None, :], positions)[:, :, 0, :]
            o = dsa_attention(q, k, v, qi, ki, wi, positions)
            out = (o * jax.nn.silu(g)) @ odd_w_out[j]
        x = x + gate[:, None, :] * out
    return rms_norm(x, final_g)


DEPTH_2 = 1

PLE_DIM = 256
D_MIX = D_MODEL
CONV_WIDTH_2 = D_MIX // 2
CONV_HEADS = 8
POOL_WIDTH = D_MIX - CONV_WIDTH_2
POOL_WINDOWS = (2, 4, 8, 16)
POOL_GROUP = POOL_WIDTH // len(POOL_WINDOWS)
IN_PROJ_WIDTH = 3 * CONV_WIDTH_2 + POOL_WIDTH
CONV_K = 3
PEER_HEADS = 8
PEER_QDIM = 256
PEER_HALF = PEER_QDIM // 2
N_KEYS = 128
N_EXPERTS = N_KEYS * N_KEYS
PEER_TOPK = 16
TOKEN_BLOCK = 128


def rms_norm_2(x, g):
    xf = x.astype(jnp.float32)
    y = xf * lax.rsqrt(jnp.mean(xf * xf, axis=-1, keepdims=True) + EPS)
    return (y * g.astype(jnp.float32)).astype(x.dtype)

def short_conv_mixer(b_gate, c_gate, v, conv_w):
    z = c_gate * v
    zp = jnp.pad(z, ((0, 0), (1, 1), (0, 0)))
    y = conv_w[0] * zp[:, :-2] + conv_w[1] * zp[:, 1:-1] + conv_w[2] * zp[:, 2:]
    return b_gate * y

def pool_mixer(u, pool_w, pool_scale):
    bsz, seq, _ = u.shape
    ug = u.astype(jnp.float32).reshape(bsz, seq, len(POOL_WINDOWS), POOL_GROUP)
    t = jnp.arange(seq)
    outs = []
    for g, w in enumerate(POOL_WINDOWS):
        xg = ug[:, :, g]
        cs = jnp.concatenate([jnp.zeros((bsz, 1, POOL_GROUP), jnp.float32),
                              jnp.cumsum(xg, axis=1)], axis=1)
        lo = jnp.clip(t - w // 2, 0, seq)
        hi = jnp.clip(t + w // 2, 0, seq)
        win_sum = jnp.take(cs, hi, axis=1) - jnp.take(cs, lo, axis=1)
        cnt = (hi - lo).astype(jnp.float32)[None, :, None]
        outs.append(win_sum / cnt - xg)
    pooled = jnp.stack(outs, axis=2).astype(u.dtype)
    y = jnp.einsum('bsgc,gcd->bsgd', pooled, pool_w)
    return y.reshape(bsz, seq, POOL_WIDTH) * pool_scale

def peer_block(xb, w_q, sub_keys, expert_u, expert_v):
    T = xb.shape[0]
    q = (xb @ w_q).reshape(T, PEER_HEADS, 2, PEER_HALF)
    s = jnp.einsum('thpd,hpkd->thpk', q, sub_keys)
    sv, si = lax.top_k(s, PEER_TOPK)
    cand = (sv[:, :, 0, :, None] + sv[:, :, 1, None, :]).reshape(T, PEER_HEADS, PEER_TOPK * PEER_TOPK)
    cidx = (si[:, :, 0, :, None] * N_KEYS + si[:, :, 1, None, :]).reshape(T, PEER_HEADS, PEER_TOPK * PEER_TOPK)
    top_s, pos = lax.top_k(cand, PEER_TOPK)
    eidx = jnp.take_along_axis(cidx, pos, axis=-1)
    gate = jax.nn.softmax(top_s.astype(jnp.float32), axis=-1).astype(xb.dtype)
    u = jnp.take(expert_u, eidx, axis=0)
    act = jax.nn.gelu(jnp.einsum('thkd,td->thk', u, xb))
    v = jnp.take(expert_v, eidx, axis=0)
    return jnp.einsum('thk,thkd->td', gate * act, v)

def peer_ffn(xn, w_q, sub_keys, expert_u, expert_v):
    bsz, seq, d = xn.shape
    blocks = xn.reshape(-1, TOKEN_BLOCK, d)
    out = lax.map(lambda xb: peer_block(xb, w_q, sub_keys, expert_u, expert_v), blocks)
    return out.reshape(bsz, seq, d)

def second_inputs(seed: int = 0) -> dict:
    key = jax.random.key(seed)
    ks = jax.random.split(key, 20)
    f32 = jnp.float32
    def nrm(k, shape, scale):
        return jax.random.normal(k, shape, f32) * scale
    def gain(k, shape):
        return 1.0 + 0.05 * jax.random.normal(k, shape, f32)
    return {
        "x": nrm(ks[0], (BATCH, SEQ, D_MODEL), 1.0),
        "p": nrm(ks[1], (DEPTH_2, BATCH, SEQ, PLE_DIM), 1.0),
        "g_mix": gain(ks[2], (DEPTH_2, D_MODEL)),
        "w_in": nrm(ks[3], (DEPTH_2, D_MODEL, IN_PROJ_WIDTH), D_MODEL ** -0.5),
        "conv_w": nrm(ks[4], (DEPTH_2, CONV_K, CONV_WIDTH_2), CONV_K ** -0.5),
        "pool_w": nrm(ks[5], (DEPTH_2, len(POOL_WINDOWS), POOL_GROUP, POOL_GROUP), POOL_GROUP ** -0.5),
        "pool_scale": gain(ks[6], (DEPTH_2, POOL_WIDTH)),
        "w_o": nrm(ks[7], (DEPTH_2, D_MIX, D_MODEL), D_MIX ** -0.5),
        "g_ffn": gain(ks[8], (DEPTH_2, D_MODEL)),
        "w_q": nrm(ks[9], (DEPTH_2, D_MODEL, PEER_HEADS * PEER_QDIM), D_MODEL ** -0.5),
        "sub_keys": nrm(ks[10], (DEPTH_2, PEER_HEADS, 2, N_KEYS, PEER_HALF), PEER_HALF ** -0.5),
        "expert_u": nrm(ks[11], (DEPTH_2, N_EXPERTS, D_MODEL), D_MODEL ** -0.5),
        "expert_v": nrm(ks[12], (DEPTH_2, N_EXPERTS, D_MODEL), PEER_HEADS ** -0.5),
        "g_ple": gain(ks[13], (DEPTH_2, D_MODEL)),
        "w_ple_gate": nrm(ks[14], (DEPTH_2, D_MODEL, D_MODEL), D_MODEL ** -0.5),
        "w_ple_proj": nrm(ks[15], (DEPTH_2, PLE_DIM, D_MODEL), PLE_DIM ** -0.5),
        "g_final": gain(ks[16], (D_MODEL,)),
    }

def second_block(x, p, g_mix, w_in, conv_w, pool_w, pool_scale, w_o, g_ffn, w_q, sub_keys,
              expert_u, expert_v, g_ple, w_ple_gate, w_ple_proj, g_final):
    h = x
    for i in range(DEPTH_2):
        xn = rms_norm_2(h, g_mix[i])
        proj = xn @ w_in[i]
        b_gate = proj[..., :CONV_WIDTH_2]
        c_gate = proj[..., CONV_WIDTH_2:2 * CONV_WIDTH_2]
        v_conv = proj[..., 2 * CONV_WIDTH_2:3 * CONV_WIDTH_2]
        u_pool = proj[..., 3 * CONV_WIDTH_2:]
        y_conv = short_conv_mixer(b_gate, c_gate, v_conv, conv_w[i])
        y_pool = pool_mixer(u_pool, pool_w[i], pool_scale[i])
        h = h + jnp.concatenate([y_conv, y_pool], axis=-1) @ w_o[i]
        h = h + peer_ffn(rms_norm_2(h, g_ffn[i]), w_q[i], sub_keys[i], expert_u[i], expert_v[i])
        gate = jax.nn.sigmoid(rms_norm_2(h, g_ple[i]) @ w_ple_gate[i])
        h = h + gate * (p[i] @ w_ple_proj[i])
    return rms_norm_2(h, g_final)


def setup_inputs(seed=0):
    out = dict(first_inputs(seed))
    for name, value in second_inputs(seed + 1).items():
        if name != "x":
            out[name + "_2"] = value
    return out


def reference(
    x, c, positions, ada_w, ada_b, norm_g, final_g, even_w_in, even_w_out, conv_w, conv_vec,
    rwkv_mu_rkv, rwkv_mu_lora, rwkv_vec, rwkv_w_up, rwkv_a_up, rwkv_r_k, odd_w_in, odd_w_out,
    p_2, g_mix_2, w_in_2, conv_w_2, pool_w_2, pool_scale_2, w_o_2, g_ffn_2, w_q_2, sub_keys_2,
    expert_u_2, expert_v_2, g_ple_2, w_ple_gate_2, w_ple_proj_2, g_final_2,
):
    x = first_block(
        x, c, positions, ada_w, ada_b, norm_g, final_g, even_w_in, even_w_out, conv_w, conv_vec,
        rwkv_mu_rkv, rwkv_mu_lora, rwkv_vec, rwkv_w_up, rwkv_a_up, rwkv_r_k, odd_w_in,
        odd_w_out,
    )
    return second_block(
        x, p_2, g_mix_2, w_in_2, conv_w_2, pool_w_2, pool_scale_2, w_o_2, g_ffn_2, w_q_2,
        sub_keys_2, expert_u_2, expert_v_2, g_ple_2, w_ple_gate_2, w_ple_proj_2, g_final_2,
    )


_drawn_inputs = setup_inputs


def setup_inputs(seed=0):
    import zlib

    import numpy as np

    out = dict(_drawn_inputs(seed))
    spreads = {}
    factors = {'rwkv_w_up': 2.894, 'g_ple_2': 7.796}
    for name, (base, spread) in spreads.items():
        noise = np.random.default_rng([zlib.crc32(name.encode()), seed]).standard_normal(out[name].shape)
        drawn = base * np.exp(spread * noise) if base else spread * noise
        out[name] = __import__('jax').numpy.asarray(drawn.astype(out[name].dtype))
    for name, factor in factors.items():
        out[name] = (out[name] * factor).astype(out[name].dtype)
    return out
```

```python
import math
from contextlib import ExitStack

import numpy as np

import concourse.bass as bass
from concourse import mybir

ALU = mybir.AluOpType
ACT = mybir.ActivationFunctionType
AX = mybir.AxisListType
F32 = mybir.dt.float32
BF16 = mybir.dt.bfloat16
U32 = mybir.dt.uint32
I32 = mybir.dt.int32

D = 1024
S = 512
KT = 8
CH = 4
JC = 4
TG = 64
RING = 12
TAPS = 31
NTMP = 14
TWO_PI = 2.0 * math.pi
MAGIC = 12582912.0
NEG = -1e30

VECS = [
    ("c", 8), ("norm_g0", 8), ("norm_g1", 8), ("final_g", 8), ("ada_b0", 24), ("ada_b1", 24),
    ("conv_b", 8), ("ln_w", 8), ("ln_b", 8), ("mu_r", 8), ("mu_k", 8), ("mu_v", 8), ("mu_l", 1),
    ("w0", 8), ("a0", 8), ("k_k", 8), ("k_a", 8), ("gn_w", 8), ("gn_b", 8), ("r_k", 8),
    ("conv_w", 8 * TAPS), ("g_mix", 8), ("g_ffn", 8), ("g_ple", 8), ("g_final", 8),
    ("pool_s", 4), ("conv_w2", 12), ("inv128", 1), ("inv64", 1), ("sgn128", 1), ("sgn64", 1),
]
VOFF = {}
_at = 0
for _n, _w in VECS:
    VOFF[_n] = (_at, _w)
    _at += _w
NVEC = _at


def stream_order():
    o = [("ada", m) for m in range(24)]
    for m in range(8):
        o += [("ein", m), ("ein", 8 + m), ("ein", 16 + m)]
    o += [("eout", 2 * m) for m in range(8)]
    o += [("ein", 48)]
    for m in range(8):
        o += [("ein", 24 + m), ("ein", 32 + m), ("ein", 40 + m), ("ein", 49 + m)]
    o += [("eout", 2 * m + 1) for m in range(8)]
    o += [("ada", 24 + m) for m in range(24)]
    o += [("oin", 16), ("oin", 17), ("oin", 22), ("oin", 23)]
    o += [("oin", 18 + m) for m in range(4)]
    o += [("oin", 24 + m) for m in range(16)]
    o += [("oin", m) for m in range(16)]
    for m in range(8):
        o += [("oout", 2 * m), ("oout", 2 * m + 1)]
    o += [("win", m) for m in range(16)] + [("pool", 0)] + [("wo", m) for m in range(8)]
    o += [("wq", m) for m in range(16)] + [("keys", 0), ("keys", 1)]
    n = 128 // JC
    o += [("eu", j) for j in range(JC)]
    for c in range(n):
        if c + 1 < n:
            o += [("eu", (c + 1) * JC + j) for j in range(JC)]
        o += [("ev", c * JC + j) for j in range(JC)]
    o += [("pleg", m) for m in range(8)] + [("plep", 0), ("plep", 1)]
    return o


class Eng:

    def __init__(self, sem):
        self.sem, self.n, self.q, self.seen = sem, 0, [], {}

    def wait(self, *toks):
        for t in toks:
            if t is None or not t:
                continue
            if isinstance(t, list):
                self.wait(*t)
                continue
            k, (sem, v) = t[0].name, t
            if self.seen.get(k, 0) < v:
                self.seen[k] = v
                self.q.append((sem, v))

    def __call__(self, f, *a, w=(), inc=True, **k):
        self.wait(*w)
        self.q.append((f, a, k, (self.sem, 1) if inc else None))
        if inc:
            self.n += 1
        return (self.sem, self.n)

    def dma(self, f, dst, src, sem, w=()):
        self.wait(*w)
        self.q.append((f, (dst, src), {}, (sem[0], 16)))
        sem[1] += 16
        return (sem[0], sem[1])

    def last(self):
        return (self.sem, self.n)

    def play(self, eng):
        for x in self.q:
            if len(x) == 2:
                eng.wait_ge(x[0], x[1])
            else:
                f, a, k, inc = x
                ins = f(*a, **k)
                if inc is not None:
                    ins.then_inc(inc[0], inc[1])


class Slots:

    def __init__(self, aps):
        self.free = [(ap, []) for ap in aps]

    def take(self):
        assert self.free, "no free slot"
        return self.free.pop(0)

    def give(self, slot, *toks):
        self.free.append((slot[0], list(toks)))


def build(nc, t):
    order = stream_order()
    with ExitStack() as ctx:
        def sb(name, shape, dt=F32):
            return ctx.enter_context(nc.sbuf_tensor(name, shape, dt))

        def sem(name):
            return ctx.enter_context(nc.semaphore(name))

        V, A, G, T, Y = (Eng(sem(n)) for n in ("s_dve", "s_act", "s_pool", "s_pe", "s_sp"))
        dve, act, pool, pe, sp = nc.vector, nc.scalar, nc.gpsimd, nc.tensor, nc.sync

        banks = Slots([ctx.enter_context(nc.psum_tensor(f"ps{i}", [128, 512], F32))[:, :]
                       for i in range(8)])
        xT = sb("xT", [128, KT, S])
        hT = sb("hT", [128, KT, S])
        ringt = sb("ring", [128, RING, 1024])
        vec = sb("vec", [128, NVEC])
        mod = sb("mod", [128, 2, 24])
        cond = sb("cond", [128, 8])
        gsc = sb("gsc", [128, 2, 8])
        omka = sb("omka", [128, 8])
        ident = sb("ident", [128, 128])
        ones = sb("ones", [128, 128])
        bones = sb("bones", [128, 128])
        sbtmp = sb("tmp", [128, NTMP, 512])
        ARENA = 22900
        arena = sb("arena", [128, ARENA])
        small = sb("small", [128, 8, 64])
        tmp = Slots([sbtmp[:, i, :] for i in range(NTMP)])

        def col(name, m=0):
            return vec[:, VOFF[name][0] + m:VOFF[name][0] + m + 1]

        class Arena:
            def __init__(self):
                self.at = 0

            def __call__(self, n):
                a = arena[:, self.at:self.at + n]
                self.at += n
                assert self.at <= ARENA, self.at
                return a

        def fence():
            toks = [e.last() for e in (V, A, G, T)]
            for e in (V, A, G, T, Y):
                e.wait(*toks)

        s_const = [sem("s_const"), 0]
        c_tok = Y.dma(sp.dma_start, vec[:, :], t["vec"][:, :], s_const)
        c_tok = Y.dma(sp.dma_start, ident[:, :], t["ident"][:, :], s_const)
        c_tok = Y.dma(sp.dma_start, ones[:, :], t["ones"][:, :], s_const)
        c_tok = Y.dma(sp.dma_start, bones[:, :], t["bones"][:, :], s_const)
        s_x = [sem("s_x"), 0]
        x_tok = Y.dma(sp.dma_start, xT[:, :, :], t["xT"].rearrange("(k p) s -> p k s", p=128), s_x)

        ring_sem = [[sem(f"s_w{i}"), 0] for i in range(RING)]
        st = {"loaded": 0, "used": 0, "tok": {}}

        def load_next(*w):
            n = st["loaded"]
            if n >= len(order):
                return
            name, u = order[n]
            slot = n % RING
            src = t[name][:, u, :] if name == "ev" else t[name][u]
            st["tok"][n] = Y.dma(sp.dma_start, ringt[:, slot, :], src, ring_sem[slot], w=w)
            st["loaded"] += 1

        for _ in range(RING):
            load_next()

        def unit(name, u):
            n = st["used"]
            assert order[n] == (name, u), (order[n], name, u)
            st["used"] += 1
            return ringt[:, n % RING, :].rearrange("p (k m) -> p k m", m=128), st["tok"][n]

        def proj(name, u, rhs, w=(), M=128, half=None, first=True, last=True, bank=None):
            W, tok = unit(name, u)
            b = bank or banks.take()
            T.wait(tok, *w, *([b[1]] if first else []))
            for k in range(8):
                r = T(pe.matmul, b[0][0:M, :], W[:, k, 0:M], rhs[:, k, :],
                      start=first and k == 0, stop=last and k == 7, inc=(k == 7))
            load_next(r)
            return b, r

        def rsqrt(ap, w):
            a = A(act.activation, ap, ap, ACT.Sqrt, w=[w])
            return V(dve.reciprocal, ap, ap, w=[a])

        def norm_T(src, dst, g, shift=None, w=()):
            b = banks.take()
            toks = []
            for k in range(KT):
                q = tmp.take()
                a = A(act.activation, q[0], src[:, k, :], ACT.Square, w=[w, q[1]] if not k else [q[1]])
                r = T(pe.matmul, b[0], ones[:, :], q[0], start=(k == 0), stop=(k == 7), w=[a, b[1], c_tok])
                tmp.give(q, r)
            m = tmp.take()
            v = V(dve.tensor_scalar, m[0], b[0], 1.0 / D, 1e-6, ALU.mult, ALU.add, w=[r, m[1]])
            banks.give(b, v)
            v = rsqrt(m[0], v)
            for k in range(KT):
                x = V(dve.scalar_tensor_tensor, out=dst[:, k, :], in0=src[:, k, :], scalar=g[:, k:k + 1],
                      in1=m[0], op0=ALU.mult, op1=ALU.mult, w=[v, w])
                if shift is not None:
                    x = A(act.activation, dst[:, k, :], dst[:, k, :], ACT.Identity,
                          bias=shift[:, k:k + 1], w=[x])
                toks.append(x)
            tmp.give(m, V.last())
            return toks

        def residual(b, r, m, gate=None):
            if gate is None:
                v = V(dve.tensor_tensor, xT[:, m, :], b[0], xT[:, m, :], ALU.add, w=[r])
            else:
                v = V(dve.scalar_tensor_tensor, out=xT[:, m, :], in0=b[0], scalar=gate,
                      in1=xT[:, m, :], op0=ALU.mult, op1=ALU.add, w=[r])
            banks.give(b, v)
            return v

        def modulation(l):
            b = banks.take()
            T.wait(cond_tok, b[1])
            for m in range(24):
                W, tok = unit("ada", 24 * l + m)
                for k in range(8):
                    r = T(pe.matmul, b[0][:, m:m + 1], W[:, k, :], cond[:, k:k + 1],
                          start=(k == 0), stop=(k == 7), w=[tok], inc=(k == 7))
                load_next(r)
            o = VOFF[f"ada_b{l}"][0]
            v = V(dve.tensor_tensor, mod[:, l, :], b[0][:, 0:24], vec[:, o:o + 24], ALU.add, w=[r, c_tok])
            banks.give(b, v)
            o = VOFF[f"norm_g{l}"][0]
            v = V(dve.scalar_tensor_tensor, out=gsc[:, l, :], in0=mod[:, l, 8:16], scalar=1.0,
                  in1=vec[:, o:o + 8], op0=ALU.add, op1=ALU.mult, w=[v])
            return v

        cond_tok = A(act.activation, cond[:, :], vec[:, 0:8], ACT.Silu, w=[c_tok])
        oka = VOFF["k_a"][0]
        V(dve.tensor_scalar, omka[:, :], vec[:, oka:oka + 8], -1.0, 1.0, ALU.mult, ALU.add, w=[c_tok])

        m_tok = modulation(0)
        h_toks = norm_T(xT, hT, gsc[:, 0, :], mod[:, 0, 0:8], w=[x_tok, m_tok])

        ar = Arena()
        yc = ar(4096).rearrange("p (k s) -> p k s", k=8)
        ag = ar(4096).rearrange("p (k s) -> p k s", k=8)
        us = Slots([ar(S + TAPS - 1) for _ in range(3)])
        ztoks = [V(dve.memset, u[0][:, 0:TAPS - 1], 0.0) for u in us.free]
        y_toks, ag_toks = [], []
        for m in range(8):
            bv, rv = proj("ein", m, hT, w=[h_toks])
            bg, rg = proj("ein", 8 + m, hT)
            s = tmp.take()
            a = A(act.activation, s[0], bg[0], ACT.Sigmoid, w=[rg, s[1]])
            banks.give(bg, a)
            u = us.take()
            v = V(dve.tensor_tensor, u[0][:, TAPS - 1:], bv[0], s[0], ALU.mult, w=[rv, a, u[1], ztoks])
            banks.give(bv, v)
            tmp.give(s, v)
            cw = lambda k: col("conv_w", m * TAPS + k)
            v = V(dve.tensor_scalar, yc[:, m, :], u[0][:, 0:S], cw(0), col("conv_b", m),
                  ALU.mult, ALU.add, w=[v])
            for k in range(1, TAPS):
                v = V(dve.scalar_tensor_tensor, out=yc[:, m, :], in0=u[0][:, k:k + S], scalar=cw(k),
                      in1=yc[:, m, :], op0=ALU.mult, op1=ALU.add, w=[v])
            us.give(u, v)
            y_toks.append(v)
            ba, ra = proj("ein", 16 + m, hT)
            a = A(act.activation, ag[:, m, :], ba[0], ACT.Silu, w=[ra])
            banks.give(ba, a)
            ag_toks.append(a)
        b = banks.take()
        for m in range(8):
            r = T(pe.matmul, b[0], ones[:, :], yc[:, m, :], start=(m == 0), stop=(m == 7),
                  w=[y_toks[m], b[1]])
        mu = tmp.take()
        a = A(act.activation, mu[0], b[0], ACT.Copy, scale=1.0 / D, w=[r, mu[1]])
        banks.give(b, a)
        b = banks.take()
        for m in range(8):
            v = V(dve.tensor_tensor, yc[:, m, :], yc[:, m, :], mu[0], ALU.subtract, w=[a])
            q = tmp.take()
            a2 = A(act.activation, q[0], yc[:, m, :], ACT.Square, w=[v, q[1]])
            r = T(pe.matmul, b[0], ones[:, :], q[0], start=(m == 0), stop=(m == 7), w=[a2, b[1]])
            tmp.give(q, r)
        v = V(dve.tensor_scalar, mu[0], b[0], 1.0 / D, 1e-5, ALU.mult, ALU.add, w=[r, v])
        banks.give(b, v)
        v = vr = rsqrt(mu[0], v)
        ya_toks = []
        for m in range(8):
            v = V(dve.tensor_tensor, yc[:, m, :], yc[:, m, :], mu[0], ALU.mult, w=[vr])
            a = A(act.activation, yc[:, m, :], yc[:, m, :], ACT.Silu, scale=col("ln_w", m),
                  bias=col("ln_b", m), w=[v])
            ya_toks.append(G(pool.tensor_tensor, yc[:, m, :], yc[:, m, :], ag[:, m, :], ALU.mult,
                             w=[a, ag_toks[m]]))
        tmp.give(mu, v)
        for m in range(8):
            b, r = proj("eout", 2 * m, yc, w=[ya_toks])
            residual(b, r, m, gate=mod[:, 0, 16 + m:17 + m])
        fence()

        ar = Arena()
        yb = ar(4096).rearrange("p (k s) -> p k s", k=8)
        zs = Slots([ar(S + 1) for _ in range(3)])
        wl = ar(512)
        lup = ar(1024)
        msk = ar(512).bitcast(U32)
        lvl = ar(7 * 128).rearrange("p (l n) -> p l n", l=7)
        PP = ar(CH * 129).rearrange("p (c n) -> p c n", c=CH)
        d1 = ar(512)
        sm = ar(16)

        def pair_set():
            return {"KR": ar(1024).rearrange("p (c a n) -> p c a n", c=CH, a=2), "Be": ar(512), "Kh": ar(512),
                    "bon": ar(512), "gs": ar(512), "dd": ar(CH), "Vt": ar(512).rearrange("p (c n) -> p c n", c=CH),
                    "Bt": ar(512).rearrange("p (c n) -> p c n", c=CH),
                    "Kt": ar(512).rearrange("p (c n) -> p c n", c=CH)}
        sets = Slots([pair_set()])
        AB = ar(2048).rearrange("p (e c a n) -> p e c a n", e=2, c=CH, a=2)
        AK = ar(2048).rearrange("p (e c a n) -> p e c a n", e=2, c=CH, a=2)
        X = ar(1024).rearrange("p (e c n) -> p e c n", e=2, c=CH)
        XT = ar(1024).rearrange("p (e c n) -> p e c n", e=2, c=CH)
        P1 = ar(1024).rearrange("p (e c n) -> p e c n", e=2, c=CH)
        Sbd = ar(128)
        Su = ar(128)
        x1n = ar(128)
        SA = ar(128)
        s_rc = [sem("s_rc"), 0]
        Y.dma(sp.dma_start, msk, t["msk"][:, :], s_rc)
        Y.dma(sp.dma_start, lup, t["lup"][:, :], s_rc)
        rc_tok = Y.dma(sp.dma_start, lvl, t["lvl"].rearrange("l p n -> p l n"), s_rc)
        V(dve.memset, AB, 0.0)
        V(dve.memset, AK, 0.0)
        z0 = [V(dve.memset, d1, 0.0)] + [V(dve.memset, z[0][:, 0:1], 0.0) for z in zs.free]

        def shifted(name, u, mu_col, out, w=()):
            b, r = proj(name, u, hT)
            z = zs.take()
            a = A(act.activation, z[0][:, 1:], b[0], ACT.Copy, w=[r, z[1], z0])
            banks.give(b, a)
            d = tmp.take()
            g = G(pool.tensor_tensor, d[0], z[0][:, 0:S], z[0][:, 1:], ALU.subtract, w=[a, d[1]])
            v = V(dve.scalar_tensor_tensor, out=out, in0=d[0], scalar=mu_col, in1=z[0][:, 1:],
                  op0=ALU.mult, op1=ALU.add, w=[g, w])
            tmp.give(d, v)
            zs.give(z, v)
            return v

        v = shifted("ein", 48, col("mu_l"), wl)
        wl_tok = A(act.activation, wl[0:64, :], wl[0:64, :], ACT.Tanh, w=[v])

        def prep(c, out):
            s = sets.take()
            d = s[0]
            out["s"] = s
            sw = s[1]
            k = tmp.take()
            r_ = tmp.take()
            v_ = tmp.take()
            tr = shifted("ein", 24 + c, col("mu_r", c), r_[0], w=[r_[1]])
            yield
            tk = shifted("ein", 32 + c, col("mu_k", c), k[0], w=[k[1]])
            yield
            tv = shifted("ein", 40 + c, col("mu_v", c), v_[0], w=[v_[1]])
            yield
            bg, rg = proj("ein", 49 + c, hT)
            tg = A(act.activation, d["gs"], bg[0], ACT.Silu, w=[rg, sw])
            banks.give(bg, tg)
            yield
            b1 = banks.take()
            r1 = T(pe.matmul, b1[0], lup[0:64, c * 128:(c + 1) * 128], wl[0:64, :], start=True, stop=True,
                   w=[b1[1], wl_tok, rc_tok])
            b2 = banks.take()
            r2 = T(pe.matmul, b2[0], lup[64:128, c * 128:(c + 1) * 128], wl[64:128, :], start=True, stop=True,
                   w=[b2[1]])
            wd = tmp.take()
            aa = tmp.take()
            a = A(act.activation, wd[0], b1[0], ACT.Sigmoid, bias=col("w0", c), w=[r1, wd[1]])
            banks.give(b1, a)
            ta = A(act.activation, aa[0], b2[0], ACT.Sigmoid, bias=col("a0", c), w=[r2, aa[1]])
            banks.give(b2, ta)
            sq = tmp.take()
            a2 = A(act.activation, sq[0], k[0], ACT.Square, scale=col("k_k", c), w=[tk, sq[1]])
            b = banks.take()
            r = T(pe.matmul, b[0], bones[:, :], sq[0], start=True, stop=True, w=[a2, b[1]])
            tw = A(act.activation, wd[0], wd[0], ACT.Exp, scale=-math.exp(-0.5), w=[a])
            yield
            v = V(dve.tensor_scalar, sq[0], b[0], 1e-24, None, ALU.max, w=[r])
            banks.give(b, v)
            v = rsqrt(sq[0], v)
            kk = tmp.take()
            v = V(dve.scalar_tensor_tensor, out=kk[0], in0=k[0], scalar=col("k_k", c), in1=sq[0],
                  op0=ALU.mult, op1=ALU.mult, w=[v, kk[1]])
            tmp.give(sq, v)
            tkk = v
            k2 = tmp.take()
            v = V(dve.tensor_scalar, k2[0], aa[0], col("k_a", c), omka[:, c:c + 1], ALU.mult, ALU.add,
                  w=[ta, k2[1]])
            tk2 = V(dve.tensor_tensor, k2[0], k2[0], k[0], ALU.mult, w=[v])
            tmp.give(k, tk2)
            tb = G(pool.tensor_tensor, aa[0], aa[0], kk[0], ALU.mult, w=[tkk, v])
            yield
            w4 = wd[0].rearrange("p (c n) -> p c n", c=CH)
            v = V(dve.tensor_copy, d1.rearrange("p (c n) -> p c n", c=CH)[:, :, 0:1], w4[:, :, 0:1], w=[tw, z0])
            v = V(dve.memset, w4[:, :, 0:1], 0.0, w=[v])
            pw = tmp.take()
            v = V(dve.tensor_tensor_scan, pw[0], wd[0], d1, 0.0, ALU.mult, ALU.add, w=[v, pw[1]])
            tmp.give(wd, v)
            p4 = pw[0].rearrange("p (c n) -> p c n", c=CH)
            v2 = V(dve.reciprocal, PP[:, :, 0:1], p4[:, :, 63:64], w=[v])
            v = V(dve.tensor_tensor, PP[:, :, 1:129], p4, PP[:, :, 0:1].broadcast_to([128, CH, 128]), ALU.mult,
                  w=[v2])
            vd = V(dve.tensor_tensor, d["dd"][:, 0:3], PP[:, 0:3, 128:129].rearrange("p c n -> p (c n)"),
                   p4[:, 1:4, 63:64].rearrange("p c n -> p (c n)"), ALU.mult, w=[v, sw])
            pi4 = pw[0].rearrange("p (c n) -> p c n", c=CH)
            vi = V(dve.reciprocal, pi4, PP[:, :, 1:129], w=[vd])
            yield
            KR = d["KR"]
            f4 = lambda ap: ap.rearrange("p (c n) -> p c n", c=CH)
            g1 = G(pool.tensor_tensor, KR[:, :, 0, :], f4(kk[0]), PP[:, :, 0:128], ALU.mult, w=[v, tkk, sw])
            g2 = V(dve.tensor_tensor, KR[:, :, 1, :], f4(r_[0]), PP[:, :, 1:129], ALU.mult, w=[v, tr, sw])
            tmp.give(kk, g1)
            out["PPfree"] = [g1, g2]
            V.wait(g1)
            vB = V(dve.tensor_tensor, d["Be"], aa[0], pw[0], ALU.mult, w=[tb, vi, sw])
            vK = V(dve.tensor_tensor, d["Kh"], k2[0], pw[0], ALU.mult, w=[tk2, vi, sw])
            tmp.give(aa, vB)
            tmp.give(pw, vK)
            v = V(dve.scalar_tensor_tensor, out=r_[0], in0=r_[0], scalar=col("r_k", c), in1=k2[0],
                  op0=ALU.mult, op1=ALU.mult, w=[g2])
            tmp.give(k2, v)
            b = banks.take()
            r = T(pe.matmul, b[0], bones[:, :], r_[0], start=True, stop=True, w=[v, b[1]])
            yield
            tmp.give(r_, r)
            vb = V(dve.tensor_tensor, d["bon"], b[0], v_[0], ALU.mult, w=[r, tv, sw])
            banks.give(b, vb)
            tt = []
            for src, dst, tk_ in ((v_[0], "Vt", tv), (d["Be"], "Bt", vB), (d["Kh"], "Kt", vK)):
                b = banks.take()
                T.wait(tk_, b[1])
                for q in range(CH):
                    r = T(pe.transpose, b[0][:, q * 128:(q + 1) * 128], src[:, q * 128:(q + 1) * 128],
                          ident[:, :], inc=(q == 3))
                a = A(act.activation, d[dst], b[0], ACT.Copy, w=[r, sw])
                banks.give(b, a)
                if dst == "Vt":
                    tmp.give(v_, r, vb)
                tt.append(a)
                yield
            out["tok"] = [g1, g2, vB, vK, vb, tg, vd] + tt

        st2 = {"ab": [], "y": []}

        def solve(c, inp):
            s = inp["s"]
            d = s[0]
            KR, Be, Kh = d["KR"], d["Be"], d["Kh"]
            T.wait(inp["tok"])
            ev = []
            for e in range(2):
                p = slice(64 * e, 64 * e + 64)
                for dst, lhs in ((AB, Be), (AK, Kh)):
                    for cc in range(0, CH, 2):
                        b = banks.take()
                        T.wait(b[1])
                        for q in range(2):
                            r = T(pe.matmul, b[0][:, q * 256:(q + 1) * 256],
                                  lhs[p, (cc + q) * 128:(cc + q + 1) * 128],
                                  KR[p, cc + q, :, :].rearrange("p a n -> p (a n)"),
                                  start=True, stop=True, inc=(q == 1))
                        v = V(dve.copy_predicated, dst[:, e, cc:cc + 2, :, :].rearrange("p c a n -> p (c a n)"),
                              msk, b[0], w=[r, rc_tok, st2["ab"]])
                        banks.give(b, v)
                        ev.append(v)
                    yield
            toks = {}
            for e in range(2):
                g = G(pool.tensor_tensor, XT[:, e, :, :], AB[:, e, :, 0, :],
                      lvl[:, 0:1, :].broadcast_to([128, CH, 128]), ALU.mult, w=[ev, st2["ab"]])
                g = G(pool.tensor_tensor, XT[:, e, :, :], XT[:, e, :, :],
                      ident[:, :].rearrange("p (o n) -> p o n", o=1).broadcast_to([128, CH, 128]), ALU.add, w=[g])
                b = banks.take()
                T.wait(b[1], g)
                for q in range(CH):
                    r = T(pe.transpose, b[0][:, q * 128:(q + 1) * 128], XT[:, e, q, :], ident[:, :], inc=(q == 3))
                a = A(act.activation, X[:, e, :, :].rearrange("p c n -> p (c n)"), b[0], ACT.Copy, w=[r])
                banks.give(b, a)
                toks[e] = [g, a]
            yield
            for l in range(1, 7):
                p1 = {}
                for e in range(2):
                    b = banks.take()
                    T.wait(b[1], toks[e], ev)
                    for q in range(CH):
                        r = T(pe.matmul, b[0][:, q * 128:(q + 1) * 128], AB[:, e, q, 0, :], X[:, e, q, :],
                              start=True, stop=True, inc=(q == 3))
                    v = V(dve.tensor_tensor, P1[:, e, :, :], b[0].rearrange("p (c n) -> p c n", c=CH),
                          lvl[:, l:l + 1, :].broadcast_to([128, CH, 128]), ALU.mult, w=[r])
                    banks.give(b, v)
                    p1[e] = v
                yield
                for e in range(2):
                    b3 = banks.take()
                    T.wait(b3[1], p1[e])
                    for q in range(CH):
                        r3 = T(pe.matmul, b3[0][:, q * 128:(q + 1) * 128], P1[:, e, q, :], XT[:, e, q, :],
                               start=True, stop=True, inc=(q == 3))
                    r2 = None
                    if l < 6:
                        b2 = banks.take()
                        T.wait(b2[1])
                        for q in range(CH):
                            r2 = T(pe.matmul, b2[0][:, q * 128:(q + 1) * 128], XT[:, e, q, :], P1[:, e, q, :],
                                   start=True, stop=True, inc=(q == 3))
                        xf = X[:, e, :, :].rearrange("p c n -> p (c n)")
                        v2 = V(dve.tensor_tensor, xf, xf, b2[0], ALU.subtract, w=[r2])
                        banks.give(b2, v2)
                    xf = XT[:, e, :, :].rearrange("p c n -> p (c n)")
                    v = V(dve.tensor_tensor, xf, xf, b3[0], ALU.subtract, w=[r3, r2])
                    banks.give(b3, v)
                    toks[e] = [v]
                yield
            ts = V(dve.memset, Sbd, 0.0, w=[st2["y"]])
            by = banks.take()
            T.wait(by[1])
            for q in range(CH):
                b = banks.take()
                T.wait(b[1], ts, toks[0], toks[1])
                for e in range(2):
                    xe = b[0][:, 64 * e:64 * e + 64]
                    T(pe.matmul, xe, KR[:, q, 0, :], Sbd[:, 64 * e:64 * e + 64], start=True, stop=False, inc=False)
                    r = T(pe.matmul, xe, AK[:, e, q, 0, :], d["Vt"][:, q, 64 * e:64 * e + 64],
                          start=False, stop=True, inc=(e == 1))
                a = A(act.activation, x1n, b[0][:, 0:128], ACT.Copy, scale=-1.0, w=[r, st2["y"]])
                banks.give(b, a)
                yield
                b = banks.take()
                T.wait(b[1], a)
                for e in range(2):
                    r = T(pe.matmul, b[0][:, 64 * e:64 * e + 64], XT[:, e, q, :], x1n[:, 64 * e:64 * e + 64],
                          start=True, stop=True, inc=(e == 1))
                a = A(act.activation, SA, b[0][:, 0:128], ACT.Copy, w=[r, st2["y"]])
                banks.give(b, a)
                yield
                yo = by[0][:, q * 128:(q + 1) * 128]
                T.wait(a)
                b = None
                if q < CH - 1:
                    b = banks.take()
                    T.wait(b[1])
                    T(pe.matmul, b[0][:, 0:128], d["Bt"][:, q, :], SA, start=True, stop=False, inc=False)
                    r = T(pe.matmul, b[0][:, 0:128], d["Kt"][:, q, :], d["Vt"][:, q, :], start=False, stop=True)
                    v = V(dve.tensor_tensor, Su, b[0][:, 0:128], Sbd, ALU.add, w=[r, ts])
                    banks.give(b, v)
                for e in range(2):
                    ye = yo[64 * e:64 * e + 64, :]
                    T(pe.matmul, ye, Sbd[:, 64 * e:64 * e + 64], KR[:, q, 1, :], start=True, stop=False, inc=False)
                    T(pe.matmul, ye, SA[:, 64 * e:64 * e + 64], AB[:, e, q, 1, :], start=False, stop=False,
                      inc=False)
                    ry = T(pe.matmul, ye, d["Vt"][:, q, 64 * e:64 * e + 64], AK[:, e, q, 1, :], start=False,
                           stop=True, inc=(e == 1))
                st2["y"] = [ry]
                if q < CH - 1:
                    ts = V(dve.scalar_tensor_tensor, out=Sbd, in0=Su, scalar=d["dd"][:, q:q + 1], in1=bones[:, :],
                           op0=ALU.mult, op1=ALU.mult, w=[v, ry])
                yield
            st2["ab"] = [ry]
            y = tmp.take()
            a = A(act.activation, y[0], by[0], ACT.Copy, w=[ry, y[1]])
            banks.give(by, a)
            b = banks.take()
            r = T(pe.matmul, b[0], bones[:, :], y[0], start=True, stop=True, w=[a, b[1]])
            v = V(dve.scalar_tensor_tensor, out=y[0], in0=b[0], scalar=-1.0 / 64, in1=y[0], op0=ALU.mult,
                  op1=ALU.add, w=[r])
            banks.give(b, v)
            yield
            q = tmp.take()
            a = A(act.activation, q[0], y[0], ACT.Square, w=[v, q[1]])
            b = banks.take()
            r = T(pe.matmul, b[0], bones[:, :], q[0], start=True, stop=True, w=[a, b[1]])
            yield
            v = V(dve.tensor_scalar, q[0], b[0], 1.0 / 64, 64e-5, ALU.mult, ALU.add, w=[r])
            banks.give(b, v)
            v = rsqrt(q[0], v)
            v = V(dve.scalar_tensor_tensor, out=y[0], in0=y[0], scalar=col("gn_w", c), in1=q[0], op0=ALU.mult,
                  op1=ALU.mult, w=[v])
            v = V(dve.scalar_tensor_tensor, out=y[0], in0=y[0], scalar=col("gn_b", c), in1=d["bon"], op0=ALU.add,
                  op1=ALU.add, w=[v])
            g = G(pool.tensor_tensor, yb[:, c, :], y[0], d["gs"], ALU.mult, w=[v])
            tmp.give(y, g)
            tmp.give(q, v)
            yb_toks.append(g)
            sets.give(s, ry, g, v)

        yb_toks = []

        def run(*gens):
            gens = list(gens)
            while gens:
                for g in list(gens):
                    try:
                        next(g)
                    except StopIteration:
                        gens.remove(g)

        for c in range(8):
            o = {}
            run(prep(c, o))
            run(solve(c, o))
        for m in range(8):
            b, r = proj("eout", 2 * m + 1, yb, w=[yb_toks])
            residual(b, r, m, gate=mod[:, 0, 16 + m:17 + m])

        m_tok = modulation(1)
        h_toks = norm_T(xT, hT, gsc[:, 1, :], mod[:, 1, 0:8], w=[m_tok, V.last()])
        fence()
        ar = Arena()
        og = ar(8192).rearrange("p (k s) -> p k s", k=16)
        tabs = {}
        posf = ar(512)
        posi = tmp.take()
        s_p = [sem("s_p"), 0]
        ptok = Y.dma(sp.dma_start, posi[0].bitcast(I32), t["positions"].partition_broadcast(128), s_p,
                     w=[posi[1]])
        pcol = ar(4)
        pcr = ar(4)
        ptok2 = Y.dma(sp.dma_start, pcr.bitcast(I32), t["pcol"][:, :], s_p)
        v = V(dve.tensor_copy, posf, posi[0].bitcast(I32), w=[ptok2])
        C1 = 6.28125
        C2 = float(np.float32(np.round((TWO_PI - C1) * 2 ** 21) / 2 ** 21))
        C3 = float(TWO_PI - C1 - C2)
        for nm, inv, sgn in (("128", "inv128", "sgn128"), ("64", "inv64", "sgn64")):
            ang, n, cosT, sinT = tmp.take(), tmp.take(), ar(512), ar(512)
            v = V(dve.tensor_scalar, ang[0], posf, col(inv), None, ALU.mult, w=[v, ang[1]])
            v = V(dve.tensor_scalar, n[0], ang[0], 1.0 / TWO_PI, None, ALU.mult, w=[v, n[1]])
            v = V(dve.tensor_scalar, n[0], n[0], MAGIC, None, ALU.add, w=[v])
            v = V(dve.tensor_scalar, n[0], n[0], -MAGIC, None, ALU.add, w=[v])
            for cst in (C1, C2, C3):
                v = V(dve.scalar_tensor_tensor, out=ang[0], in0=n[0], scalar=-cst, in1=ang[0],
                      op0=ALU.mult, op1=ALU.add, w=[v])
            v = V(dve.tensor_scalar, ang[0], ang[0], 3.1415925, -3.1415925, ALU.min, ALU.max, w=[v])
            a = A(act.activation, sinT, ang[0], ACT.Sin, w=[v])
            vs = V(dve.tensor_scalar, sinT, sinT, col(sgn), None, ALU.mult, w=[a])
            v = V(dve.tensor_scalar, ang[0], ang[0], math.pi / 2, None, ALU.add, w=[a])
            v = V(dve.tensor_scalar, n[0], ang[0], math.pi, -TWO_PI, ALU.is_gt, ALU.mult, w=[v])
            v = V(dve.tensor_tensor, ang[0], ang[0], n[0], ALU.add, w=[v])
            v = V(dve.tensor_scalar, ang[0], ang[0], 3.1415925, -3.1415925, ALU.min, ALU.max, w=[v])
            a = A(act.activation, cosT, ang[0], ACT.Sin, w=[v])
            tmp.give(ang, a)
            tmp.give(n, v)
            tabs[nm] = (cosT, sinT, [a, vs])
        cidr = ar(512)
        v = V(dve.tensor_scalar, posi[0].bitcast(I32), posi[0].bitcast(I32), 6, None,
              ALU.arith_shift_right, w=[v])
        v = V(dve.tensor_copy, cidr, posi[0].bitcast(I32), w=[v])
        tmp.give(posi, v)
        v = V(dve.tensor_scalar, pcr.bitcast(I32), pcr.bitcast(I32), 6, None, ALU.arith_shift_right, w=[v, ptok2])
        cid_tok = V(dve.tensor_copy, pcol, pcr.bitcast(I32), w=[v])

        def rope(b, r, tab, out, w=()):
            cosT, sinT, tt = tabs[tab]
            h = int(tab) // 2
            m, n = tmp.take(), tmp.take()
            v1 = V(dve.tensor_tensor, m[0], b[0], cosT, ALU.mult, w=[r, m[1], tt])
            V.wait(n[1])
            for p in range(0, 128, h):
                q = p + h if (p // h) % 2 == 0 else p - h
                v2 = V(dve.tensor_tensor, n[0][p:p + h, :], b[0][q:q + h, :], sinT[q:q + h, :], ALU.mult)
            banks.give(b, v2)
            g = G(pool.tensor_tensor, out, m[0], n[0], ALU.add, w=[v1, v2, w])
            tmp.give(m, g)
            tmp.give(n, g)
            return g

        kT = ar(512)
        b, r = proj("oin", 16, hT, w=[h_toks])
        k_tok = rope(b, r, "128", kT)
        W, tok = unit("oin", 17)
        b = banks.take()
        T.wait(tok, b[1])
        for q in range(4):
            for k in range(8):
                r = T(pe.matmul, b[0][:, q * 128:(q + 1) * 128], hT[:, k, q * 128:(q + 1) * 128], W[:, k, :],
                      start=(k == 0), stop=(k == 7), inc=(k == 7))
        load_next(r)
        Vs = ar(512).rearrange("p (s n) -> p s n", s=4)
        v_tok = A(act.activation, Vs.rearrange("p s n -> p (s n)"), b[0], ACT.Copy, w=[r])
        banks.give(b, v_tok)
        kiT = ar(512)
        b, r = proj("oin", 22, hT)
        ki_tok = rope(b, r, "64", kiT)
        W, tok = unit("oin", 23)
        b = banks.take()
        T.wait(tok, b[1])
        for q in range(4):
            for k in range(8):
                r = T(pe.matmul, b[0][:, q * 8:q * 8 + 8], hT[:, k, q * 128:(q + 1) * 128], W[:, k, 0:8],
                      start=(k == 0), stop=(k == 7), inc=(k == 7))
        load_next(r)
        wi = ar(32)
        wi_tok = A(act.activation, wi, b[0][:, 0:32], ACT.Copy, scale=8.0 ** -0.5, w=[r])
        banks.give(b, wi_tok)
        qi = ar(2048).rearrange("p (k s) -> p k s", k=4)
        qi_toks = []
        for m in range(4):
            b, r = proj("oin", 18 + m, hT)
            qi_toks.append(rope(b, r, "64", qi[:, m, :]))
        selb = ar(2048).rearrange("p (b s) -> p b s", b=4)
        m8 = ar(8)
        sel_toks = []
        gate_units = list(range(16))
        og_toks = {}

        def gate_proj():
            if gate_units:
                m = gate_units.pop(0)
                b, r = proj("oin", 24 + m, hT)
                og_toks[m] = A(act.activation, og[:, m, :], b[0], ACT.Silu, w=[r])
                banks.give(b, og_toks[m])

        m8_free = []
        for blk in range(4):
            acc, val = tmp.take(), tmp.take()
            v = None
            for h in range(8):
                e = h % 2
                b = banks.take()
                r = T(pe.matmul, b[0], qi[64 * e:64 * e + 64, h // 2, blk * 128:(blk + 1) * 128],
                      kiT[64 * e:64 * e + 64, :], start=True, stop=True, w=[b[1], qi_toks, ki_tok])
                x = tmp.take()
                a = A(act.activation, x[0], b[0], ACT.Relu, scale=0.125, w=[r, x[1]])
                banks.give(b, a)
                wc = wi[:, blk * 8 + h:blk * 8 + h + 1]
                if h == 0:
                    v = V(dve.tensor_scalar, acc[0], x[0], wc, None, ALU.mult, w=[a, wi_tok, acc[1]])
                else:
                    v = V(dve.scalar_tensor_tensor, out=acc[0], in0=x[0], scalar=wc, in1=acc[0],
                          op0=ALU.mult, op1=ALU.add, w=[a, v])
                tmp.give(x, v)
            v2 = V(dve.tensor_scalar, val[0], cidr, pcol[:, blk:blk + 1], None, ALU.is_le, w=[cid_tok, val[1]])
            v = V(dve.tensor_tensor, acc[0], acc[0], val[0], ALU.mult, w=[v, v2])
            x = tmp.take()
            v2 = V(dve.tensor_scalar, x[0], val[0], -1.0, -NEG, ALU.add, ALU.mult, w=[v2, x[1]])
            v = V(dve.tensor_tensor, acc[0], acc[0], x[0], ALU.add, w=[v, v2])
            cur = acc[0]
            for i in range(16):
                v = V(dve.max, m8, cur, w=[v, m8_free])
                v = V(dve.match_replace, x[0], m8, cur, -3e38, w=[v])
                cur = x[0]
            v = V(dve.tensor_tensor, x[0], x[0], acc[0], ALU.not_equal, w=[v])
            v = V(dve.tensor_tensor, x[0], x[0], val[0], ALU.mult, w=[v])
            v = V(dve.tensor_scalar, selb[:, blk, :], x[0], -1.0, -NEG, ALU.add, ALU.mult, w=[v])
            sel_toks.append(v)
            tmp.give(acc, v)
            tmp.give(val, v)
            tmp.give(x, v)
            for _ in range(4):
                gate_proj()

        SC = 128 ** -0.5
        qTs = Slots([ar(512) for _ in range(2)])
        PTs = Slots([ar(2048).rearrange("p (s q) -> p s q", s=4)])
        sms = Slots([small[:, i, 0:4] for i in range(8)])

        def q_part(h, out):
            b, r = proj("oin", h, hT)
            qT = qTs.take()
            out["q"] = (qT, rope(b, r, "128", qT[0], w=[qT[1]]))

        def attend(h, inp):
            qT, q_tok = inp["q"]
            PT = PTs.take()
            evs = []
            Ps = []
            for blk in range(4):
                b = banks.take()
                r = T(pe.matmul, b[0], qT[0][:, blk * 128:(blk + 1) * 128], kT, start=True, stop=True,
                      w=[b[1], q_tok, k_tok])
                p, c4 = tmp.take(), sms.take()
                v = V(dve.tensor_tensor_reduce, out=p[0], in0=b[0], in1=selb[:, blk, :], scale=1.0,
                      scalar=-3e38, op0=ALU.add, op1=ALU.max, accum_out=c4[0][:, 0:1],
                      w=[r, p[1], c4[1], sel_toks[blk]])
                banks.give(b, v)
                v = V(dve.tensor_scalar, c4[0][:, 1:2], c4[0][:, 0:1], -SC, None, ALU.mult, w=[v])
                a = A(act.activation, p[0], p[0], ACT.Exp, scale=SC, bias=c4[0][:, 1:2],
                      accum_out=c4[0][:, 2:3], w=[v])
                Ps.append((p, c4, a))
            qTs.give(qT, r)
            yield
            for blk in range(4):
                p, c4, a = Ps[blk]
                v = V(dve.reciprocal, c4[0][:, 3:4], c4[0][:, 2:3], w=[a])
                g = G(pool.tensor_scalar, p[0], p[0], c4[0][:, 3:4], None, ALU.mult, w=[v])
                sms.give(c4, g)
                b = banks.take()
                T.wait(b[1], g)
                for s in range(4):
                    r = T(pe.transpose, b[0][:, s * 128:(s + 1) * 128], p[0][:, s * 128:(s + 1) * 128],
                          ident[:, :], inc=(s == 3))
                tmp.give(p, r)
                dst = PT[0][:, :, blk * 128:(blk + 1) * 128]
                srcb = b[0].rearrange("p (s q) -> p s q", s=4)
                if blk % 2:
                    e = V(dve.tensor_copy, dst, srcb, w=[r, PT[1]])
                else:
                    e = A(act.activation, dst, srcb, ACT.Copy, w=[r, PT[1]])
                banks.give(b, e)
                evs.append(e)
            yield
            b = banks.take()
            T.wait(b[1], evs, v_tok)
            for s in range(4):
                r = T(pe.matmul, b[0], Vs[:, s, :], PT[0][:, s, :], start=(s == 0), stop=(s == 3), inc=(s == 3))
            PTs.give(PT, r)
            v = V(dve.tensor_tensor, og[:, h, :], b[0], og[:, h, :], ALU.mult, w=[r, og_toks[h]])
            banks.give(b, v)
            og_toks[h] = v

        nxt = {}
        q_part(0, nxt)
        for h in range(16):
            cur, nxt = nxt, {}
            g = attend(h, cur)
            next(g)
            if h < 15:
                q_part(h + 1, nxt)
            run(g)
        for m in range(8):
            b, r = proj("oout", 2 * m, og[:, 0:8, :], last=False, w=[og_toks[h] for h in range(16)])
            b, r = proj("oout", 2 * m + 1, og[:, 8:16, :], first=False, bank=b)
            residual(b, r, m, gate=mod[:, 1, 16 + m:17 + m])
        fence()
        o = VOFF["final_g"][0]
        f_toks = norm_T(xT, xT, vec[:, o:o + 8], w=[V.last()])

        o = VOFF["g_mix"][0]
        h_toks = norm_T(xT, hT, vec[:, o:o + 8], w=f_toks)
        ar = Arena()
        ym = ar(4096).rearrange("p (k s) -> p k s", k=8)
        PADL = 16
        zp = [ar(S + 2 * PADL) for _ in range(3)]
        icnt = ar(2048).rearrange("p (g s) -> p g s", g=4)
        s_ic = [sem("s_ic"), 0]
        ic_tok = Y.dma(sp.dma_start, icnt, t["icnt"].rearrange("g s -> (g s)").partition_broadcast(128), s_ic)
        v = None
        for z in zp:
            v = V(dve.memset, z, 0.0, w=[v])
        zt = v
        ymt = {}
        cc = {}
        for m in range(4):
            q = tmp.take()
            b, r = proj("win", m, hT, w=[h_toks])
            a = A(act.activation, ym[:, m, :], b[0], ACT.Copy, w=[r])
            banks.give(b, a)
            ymt[m] = a
            tmp.give(q)
        for m in range(4):
            cc[m] = tmp.take()
            b, r = proj("win", 4 + m, hT)
            a = A(act.activation, cc[m][0], b[0], ACT.Copy, w=[r, cc[m][1]])
            banks.give(b, a)
            cc[m] = (cc[m], a)
        for m in range(4):
            b, r = proj("win", 8 + m, hT)
            z = zp[0]
            cs, a = cc[m]
            v = V(dve.tensor_tensor, z[:, 1:S + 1], b[0], cs[0], ALU.mult, w=[r, a, zt])
            banks.give(b, v)
            w3 = lambda i: col("conv_w2", m * 3 + i)
            v = V(dve.tensor_scalar, cs[0], z[:, 0:S], w3(0), None, ALU.mult, w=[v])
            v = V(dve.scalar_tensor_tensor, out=cs[0], in0=z[:, 1:S + 1], scalar=w3(1), in1=cs[0],
                  op0=ALU.mult, op1=ALU.add, w=[v])
            zt = v = V(dve.scalar_tensor_tensor, out=cs[0], in0=z[:, 2:S + 2], scalar=w3(2), in1=cs[0],
                       op0=ALU.mult, op1=ALU.add, w=[v])
            ymt[m] = V(dve.tensor_tensor, ym[:, m, :], ym[:, m, :], cs[0], ALU.mult, w=[v, ymt[m]])
            tmp.give(cs, ymt[m])
        xg = {}
        pl = []
        v = zt
        for g in range(4):
            w = 2 << g
            b, r = proj("win", 12 + g, hT)
            z, z2 = zp[1], zp[2]
            u = tmp.take()
            v = V(dve.tensor_copy, z[:, PADL:PADL + S], b[0], w=[r, v])
            a = A(act.activation, u[0], b[0], ACT.Copy, w=[v, u[1]])
            banks.give(b, v, a)
            src, dst, n = z, z2, 1
            while n < w:
                L = S + 2 * PADL
                v = V(dve.tensor_tensor, dst[:, n:L], src[:, n:L], src[:, 0:L - n], ALU.add, w=[v])
                v = V(dve.tensor_copy, dst[:, 0:n], src[:, 0:n], w=[v])
                src, dst, n = dst, src, 2 * n
            o = PADL + w // 2 - 1
            p = tmp.take()
            v = V(dve.tensor_tensor, p[0], src[:, o:o + S], icnt[:, g, :], ALU.mult, w=[v, ic_tok, p[1]])
            pt = V(dve.tensor_tensor, p[0], p[0], u[0], ALU.subtract, w=[v, a])
            tmp.give(u, pt)
            v = V(dve.memset, z, 0.0, w=[pt])
            v = V(dve.memset, z2, 0.0, w=[v])
            pl.append((p, pt))
        W, tok = unit("pool", 0)
        for g in range(4):
            p, pt = pl[g]
            b = banks.take()
            r = T(pe.matmul, b[0], W[:, g, :], p[0], start=True, stop=True, w=[tok, pt, b[1]])
            tmp.give(p, r)
            ymt[4 + g] = A(act.activation, ym[:, 4 + g, :], b[0], ACT.Copy, scale=col("pool_s", g), w=[r])
            banks.give(b, ymt[4 + g])
        load_next(r)
        for m in range(8):
            b, r = proj("wo", m, ym, w=[ymt[i] for i in range(8)])
            v = residual(b, r, m)
        o = VOFF["g_ffn"][0]
        h_toks = norm_T(xT, hT, vec[:, o:o + 8], w=[v])
        fence()

        ar = Arena()
        iT, jT, gT = ar(512), ar(512), [ar(512) for _ in range(3)]
        base = ar.at
        qh = ar(8192).rearrange("p (k s) -> p k s", k=16)
        q_toks = []
        for m in range(16):
            b, r = proj("wq", m, hT, w=[h_toks])
            if m % 2:
                q_toks.append(V(dve.tensor_copy, qh[:, m, :], b[0], w=[r]))
            else:
                q_toks.append(A(act.activation, qh[:, m, :], b[0], ACT.Copy, w=[r]))
            banks.give(b, q_toks[-1])
        K0, kt0 = unit("keys", 0)
        K1, kt1 = unit("keys", 1)
        ss = ar(2048)
        cand = ar(2048)
        sv = ar(256).rearrange("p (h k) -> p h k", k=16)
        sx = ar(256).bitcast(U32).rearrange("p (h k) -> p h k", k=16)
        sxf = ar(256).rearrange("p (h k) -> p h k", k=16)
        tv = ar(128).rearrange("p (h k) -> p h k", k=16)
        px = ar(128).bitcast(U32).rearrange("p (h k) -> p h k", k=16)
        ph = ar(128).bitcast(U32)
        hif = ar(128)
        lof = ar(128)
        ijg = ar(384)
        io16 = ar(16)
        s16 = ar(256)
        io_tok = Y.dma(sp.dma_start, io16, t["iota16"].partition_broadcast(128), s_ic)
        v = None
        fin = []
        for blk in range(4):
            bs = [banks.take() for _ in range(4)]
            T.wait(*[b[1] for b in bs], q_toks, kt0, kt1)
            for hp in range(16):
                W = K0 if hp < 8 else K1
                r = T(pe.matmul, bs[hp // 4][0][:, (hp % 4) * 128:(hp % 4 + 1) * 128],
                      qh[:, hp, blk * 128:(blk + 1) * 128], W[:, hp % 8, :], start=True, stop=True,
                      inc=(hp % 4 == 3))
            if blk == 3:
                load_next(r)
                load_next(r)
            at = []
            for i in range(4):
                at.append(A(act.activation, ss[:, i * 512:(i + 1) * 512], bs[i][0], ACT.Copy, w=[r, v]))
                banks.give(bs[i], at[-1])

            def top16(src, vals, idx, w):
                v = V(dve.max, vals[:, 0:8], src, w=w)
                v = V(dve.max_index, idx[:, 0:8], vals[:, 0:8], src, w=[v])
                v = V(dve.match_replace, src, vals[:, 0:8], src, -3e38, w=[v])
                v = V(dve.max, vals[:, 8:16], src, w=[v])
                return V(dve.max_index, idx[:, 8:16], vals[:, 8:16], src, w=[v])

            for hp in range(16):
                v = top16(ss[:, hp * 128:(hp + 1) * 128], sv[:, hp, :], sx[:, hp, :], [at, v])
            v = V(dve.tensor_copy, sxf, sx, w=[v])
            sv4 = sv.rearrange("p (h two) k -> p h two k", two=2)
            sx4 = sxf.rearrange("p (h two) k -> p h two k", two=2)
            c4 = cand.rearrange("p (h a b) -> p h a b", h=8, a=16)
            for h in range(8):
                v = V(dve.tensor_tensor, c4[:, h, :, :],
                      sv4[:, h, 0, :].rearrange("p (a o) -> p a o", o=1).broadcast_to([128, 16, 16]),
                      sv4[:, h, 1:2, :].broadcast_to([128, 16, 16]), ALU.add, w=[v])
            for h in range(8):
                v = top16(cand[:, h * 256:(h + 1) * 256], tv[:, h, :], px[:, h, :], [v])
            pxf = px.rearrange("p h k -> p (h k)")
            v = V(dve.tensor_scalar, ph, pxf, 4, None, ALU.logical_shift_right, w=[v])
            v = V(dve.tensor_copy, hif, ph, w=[v])
            v = V(dve.tensor_scalar, ph, pxf, 15, None, ALU.bitwise_and, w=[v])
            v = V(dve.tensor_copy, lof, ph, w=[v])
            for half, src in ((0, hif), (1, lof)):
                oh = cand.rearrange("p (n a) -> p n a", a=16)
                v = V(dve.tensor_tensor, oh, src.rearrange("p (n o) -> p n o", o=1).broadcast_to([128, 128, 16]),
                      io16.rearrange("p (o a) -> p o a", o=1).broadcast_to([128, 128, 16]), ALU.is_equal,
                      w=[v, io_tok])
                oh4 = cand.rearrange("p (h k a) -> p h k a", h=8, k=16)
                for h in range(8):
                    v = V(dve.tensor_tensor, oh4[:, h, :, :], oh4[:, h, :, :],
                          sx4[:, h, half:half + 1, :].broadcast_to([128, 16, 16]), ALU.mult, w=[v])
                v = V(dve.tensor_reduce, ijg[:, half * 128:(half + 1) * 128], oh, AX.X, ALU.add, w=[v, fin])
            gt = ijg[:, 256:384].rearrange("p (h k) -> p h k", k=16)
            v = V(dve.tensor_tensor, gt, tv, tv[:, :, 0:1].broadcast_to([128, 8, 16]), ALU.subtract, w=[v])
            a = A(act.activation, gt, gt, ACT.Exp, w=[v])
            s8 = s16[:, 0:8]
            v = V(dve.tensor_reduce, s8, gt, AX.X, ALU.add, w=[a])
            v = V(dve.reciprocal, s8, s8, w=[v])
            v = V(dve.tensor_tensor, gt, gt, s8.rearrange("p (h o) -> p h o", o=1).broadcast_to([128, 8, 16]),
                  ALU.mult, w=[v])
            b = banks.take()
            T.wait(b[1], v)
            for i in range(3):
                r = T(pe.transpose, b[0][:, i * 128:(i + 1) * 128], ijg[:, i * 128:(i + 1) * 128], ident[:, :],
                      inc=(i == 2))
            fin = [r]
            for i, dst in enumerate((iT, jT, gT[0])):
                a = A(act.activation, dst[:, blk * 128:(blk + 1) * 128], b[0][:, i * 128:(i + 1) * 128],
                      ACT.Copy, w=[r])
            banks.give(b, a)
        pb = ar(256).bitcast(BF16)
        v = V(dve.tensor_copy, pb, gT[0], w=[a, v])
        v = V(dve.tensor_copy, gT[1], pb, w=[v])
        v = V(dve.tensor_tensor, gT[2], gT[0], gT[1], ALU.subtract, w=[v])
        v = V(dve.tensor_copy, gT[0], gT[1], w=[v])
        v = V(dve.tensor_copy, pb, gT[2], w=[v])
        v = V(dve.tensor_copy, gT[1], pb, w=[v])
        split_tok = V(dve.tensor_tensor, gT[2], gT[2], gT[1], ALU.subtract, w=[v])
        fence()
        ar.at = base
        iob = ar(64).bitcast(BF16)
        s_io = [sem("s_io"), 0]
        iob_tok = Y.dma(sp.dma_start, iob, t["iotab"][:, :], s_io)
        ohs = Slots([ar(256).bitcast(BF16).rearrange("p (a n) -> p a n", a=4) for _ in range(6)])
        stages = Slots([(ar(128 * TG), [sem(f"s_st{i}"), 0]) for i in range(2)])
        gd_toks = []
        for blk in range(S // TG):
            stg = stages.take()
            sview = stg[0][0].rearrange("p (j t) -> p j t", t=TG)
            e = None
            for t4 in range(TG // 4):
                b = banks.take()
                T.wait(b[1])
                for q in range(4):
                    tk = blk * TG + t4 * 4 + q
                    o = ohs.take()
                    V(dve.tensor_scalar, o[0][:, 0, :], iob, iT[:, tk:tk + 1], None, ALU.is_equal,
                      w=[o[1], split_tok, iob_tok])
                    for m in range(3):
                        v = V(dve.tensor_scalar, o[0][:, 1 + m, :], iob, jT[:, tk:tk + 1], gT[m][:, tk:tk + 1],
                              ALU.is_equal, ALU.mult)
                    T.wait(v)
                    for m in range(3):
                        r = T(pe.matmul, b[0][:, q * 128:(q + 1) * 128], o[0][:, 0, :], o[0][:, 1 + m, :],
                              start=(m == 0), stop=(m == 2), inc=(m == 2))
                    ohs.give(o, r)
                e = A(act.activation, sview[:, :, t4 * 4:t4 * 4 + 4].rearrange("p j t -> p t j"),
                      b[0].rearrange("p (t j) -> p t j", t=4), ACT.Copy, w=[r, stg[1]])
                banks.give(b, e)
            tk = Y.dma(sp.dma_start, t["gd"][:, blk, :, :].rearrange("c p n -> p c n"),
                       stg[0][0].rearrange("p (c n) -> p c n", n=JC * TG), stg[0][1], w=[e])
            gd_toks.append(tk)
            stages.give(stg, tk)
        fence()
        Y.wait(*gd_toks)
        ar.at = base
        NC = 128 // JC
        gch = [(ar(JC * S), [sem(f"s_g{i}"), 0]) for i in range(2)]
        agb = [ar(JC * S).rearrange("p (j s) -> p j s", j=JC) for _ in range(2)]
        gfree = [[], []]
        afree = [[], []]
        gl = {}

        def load_g(c):
            g, sm_ = gch[c % 2]
            gl[c] = Y.dma(sp.dma_start, g.rearrange("p (b n) -> p b n", n=JC * TG),
                          t["gd"][c].rearrange("b p n -> p b n"), sm_, w=[gfree[c % 2]])

        load_g(0)
        load_g(1)
        ag_t = {}

        def z_part(c):
            g = gch[c % 2][0].rearrange("p (b j t) -> p j b t", j=JC, t=TG)
            toks = []
            for j in range(JC):
                b, r = proj("eu", c * JC + j, hT)
                x = tmp.take()
                a = A(act.activation, x[0], b[0], ACT.Gelu_apprx_tanh, w=[r, x[1]])
                banks.give(b, a)
                v = V(dve.tensor_tensor, agb[c % 2][:, j, :].rearrange("p (b t) -> p b t", t=TG),
                      x[0].rearrange("p (b t) -> p b t", t=TG), g[:, j, :, :], ALU.mult,
                      w=[a, gl[c], afree[c % 2]])
                tmp.give(x, v)
                toks.append(v)
            gfree[c % 2] = [v]
            ag_t[c] = toks

        def v_part(c):
            us_ = [unit("ev", c * JC + j) for j in range(JC)]
            for dt in range(8):
                b = banks.take()
                T.wait(b[1])
                for j in range(JC):
                    r = T(pe.matmul, b[0], us_[j][0][:, dt, :], agb[c % 2][:, j, :], start=(j == 0),
                          stop=(j == JC - 1), inc=(j == JC - 1), w=[us_[j][1], ag_t[c][j]])
                vv = residual(b, r, dt)
            for j in range(JC):
                load_next(r)
            afree[c % 2] = [r]
            return vv

        z_part(0)
        for c in range(NC):
            if c + 1 < NC:
                z_part(c + 1)
                if c + 2 < NC:
                    load_g(c + 2)
            vlast = v_part(c)

        o = VOFF["g_ple"][0]
        h_toks = norm_T(xT, hT, vec[:, o:o + 8], w=[vlast])
        fence()
        ar = Arena()
        gp = ar(4096).rearrange("p (k s) -> p k s", k=8)
        pT = ar(1024).rearrange("p (k s) -> p k s", k=2)
        p_tok = Y.dma(sp.dma_start, pT, t["pT"].rearrange("(k p) s -> p k s", p=128), s_ic)
        gp_t = []
        for m in range(8):
            b, r = proj("pleg", m, hT, w=[h_toks])
            gp_t.append(A(act.activation, gp[:, m, :], b[0], ACT.Sigmoid, w=[r]))
            banks.give(b, gp_t[-1])
        for u in range(2):
            W, tok = unit("plep", u)
            for i in range(4):
                m = 4 * u + i
                b = banks.take()
                T.wait(tok, b[1], p_tok)
                for k in range(2):
                    r = T(pe.matmul, b[0], W[:, 2 * i + k, :], pT[:, k, :], start=(k == 0), stop=(k == 1),
                          inc=(k == 1))
                v = V(dve.tensor_tensor, gp[:, m, :], b[0], gp[:, m, :], ALU.mult, w=[r, gp_t[m]])
                banks.give(b, v)
                v = V(dve.tensor_tensor, xT[:, m, :], xT[:, m, :], gp[:, m, :], ALU.add, w=[v])
            load_next(r)
        o = VOFF["g_final"][0]
        f_toks = norm_T(xT, xT, vec[:, o:o + 8], w=[v])
        s_out = [sem("s_out"), 0]
        o_tok = Y.dma(sp.dma_start, t["out"].rearrange("(k p) s -> p k s", p=128), xT[:, :, :], s_out, w=f_toks)
        Y.wait(o_tok)
        assert st["used"] == len(order)

        block = ctx.enter_context(nc.Block())

        @block.sync
        def _(eng):
            Y.play(eng)

        @block.scalar
        def _(eng):
            A.play(eng)

        @block.vector
        def _(eng):
            V.play(eng)

        @block.gpsimd
        def _(eng):
            G.play(eng)

        @block.tensor
        def _(eng):
            T.play(eng)


def _cols(v):
    return np.ascontiguousarray(np.asarray(v).reshape(-1, 128).T)


def _units(w, starts=None):
    w = np.asarray(w)
    K, N = w.shape
    starts = range(0, N, 128) if starts is None else starts
    out = []
    for s in starts:
        for kh in range(0, K, 1024):
            out.append(w[kh:kh + 1024, s:s + 128].reshape(8, 128, 128).transpose(1, 0, 2).reshape(128, 1024))
    return np.ascontiguousarray(np.stack(out))


def _constants():
    i = np.arange(128)
    strict = (i[:, None] < i[None, :])
    incl = (i[:, None] <= i[None, :])
    m = np.concatenate([strict, incl], 1).astype(np.uint32)
    lvl = np.zeros((7, 128, 128), np.float32)
    for l in range(7):
        s = 1 << l
        lvl[l] = ((i[:, None] // s) % 2 == 1) & (i[None, :] // s == i[:, None] // s - 1)
    lvl[0] = -lvl[0].T
    icnt = np.zeros((4, S), np.float32)
    tt = np.arange(S)
    for g, w in enumerate((2, 4, 8, 16)):
        icnt[g] = 1.0 / (np.clip(tt + w // 2, 0, S) - np.clip(tt - w // 2, 0, S))
    return {
        "ident": np.eye(128, dtype=np.float32), "ones": np.ones((128, 128), np.float32),
        "bones": np.kron(np.eye(2), np.ones((64, 64))).astype(np.float32),
        "msk": np.concatenate([m, m], 1), "lvl": lvl, "icnt": icnt,
        "iota16": np.arange(16, dtype=np.float32),
    }


def kernel(x, c, positions, ada_w, ada_b, norm_g, final_g, even_w_in, even_w_out, conv_w, conv_vec,
           rwkv_mu_rkv, rwkv_mu_lora, rwkv_vec, rwkv_w_up, rwkv_a_up, rwkv_r_k, odd_w_in, odd_w_out,
           p_2, g_mix_2, w_in_2, conv_w_2, pool_w_2, pool_scale_2, w_o_2, g_ffn_2, w_q_2, sub_keys_2,
           expert_u_2, expert_v_2, g_ple_2, w_ple_gate_2, w_ple_proj_2, g_final_2):
    import ml_dtypes
    import concourse.bacc as bacc
    from concourse.bass_utils import run_bass_kernel_spmd

    a = np.asarray
    f = {}
    f.update(_constants())
    f["iotab"] = np.tile(np.arange(128, dtype=np.float32), (128, 1)).astype(ml_dtypes.bfloat16)
    f["xT"] = np.ascontiguousarray(a(x)[0].T)
    f["positions"] = np.ascontiguousarray(a(positions)[0])
    f["pcol"] = np.ascontiguousarray(a(positions)[0].reshape(4, 128).T)
    q = np.arange(128)
    inv = lambda d: (np.float32(10000.0) ** (-np.arange(0, d, 2, dtype=np.float32) / np.float32(d))).astype(np.float32)
    v = {
        "c": _cols(c), "norm_g0": _cols(a(norm_g)[0]), "norm_g1": _cols(a(norm_g)[1]), "final_g": _cols(final_g),
        "ada_b0": _cols(a(ada_b)[0]), "ada_b1": _cols(a(ada_b)[1]),
        "conv_b": _cols(a(conv_vec)[0, 0]), "ln_w": _cols(a(conv_vec)[0, 1]), "ln_b": _cols(a(conv_vec)[0, 2]),
        "mu_r": _cols(a(rwkv_mu_rkv)[0, 0]), "mu_k": _cols(a(rwkv_mu_rkv)[0, 1]), "mu_v": _cols(a(rwkv_mu_rkv)[0, 2]),
        "mu_l": a(rwkv_mu_lora)[0].reshape(128, 1), "r_k": _cols(a(rwkv_r_k)[0]),
        "conv_w": a(conv_w)[0, :, 0, :].reshape(TAPS, 8, 128).transpose(2, 1, 0).reshape(128, 8 * TAPS),
        "g_mix": _cols(a(g_mix_2)[0]), "g_ffn": _cols(a(g_ffn_2)[0]), "g_ple": _cols(a(g_ple_2)[0]),
        "g_final": _cols(g_final_2), "pool_s": _cols(a(pool_scale_2)[0]),
        "conv_w2": a(conv_w_2)[0].reshape(3, 4, 128).transpose(2, 1, 0).reshape(128, 12),
        "inv128": inv(128)[q % 64][:, None], "inv64": inv(64)[q % 32][:, None],
        "sgn128": np.where(q % 128 < 64, 1.0, -1.0).astype(np.float32)[:, None],
        "sgn64": np.where(q % 64 < 32, 1.0, -1.0).astype(np.float32)[:, None],
    }
    for i, n in enumerate(("w0", "a0", "k_k", "k_a", "gn_w", "gn_b")):
        v[n] = _cols(a(rwkv_vec)[0, i])
    f["vec"] = np.ascontiguousarray(np.concatenate([v[n] for n, _ in VECS], 1))
    f["lup"] = np.ascontiguousarray(np.concatenate([a(rwkv_w_up)[0], a(rwkv_a_up)[0]], 0))
    f["ada"] = np.concatenate([_units(a(ada_w)[0]), _units(a(ada_w)[1])])
    f["ein"] = _units(a(even_w_in)[0])
    f["eout"] = _units(a(even_w_out)[0])
    w = a(odd_w_in)[0]
    ki, wi = w[:, 2816:2880], w[:, 2880:2888]
    pad = np.zeros((D, 120), w.dtype)
    f["oin"] = _units(np.concatenate([w[:, 0:2816], ki, ki, wi, pad, w[:, 2888:]], 1))
    f["oout"] = _units(a(odd_w_out)[0])
    f["win"] = _units(a(w_in_2)[0])
    pw = a(pool_w_2)[0].transpose(1, 0, 2).reshape(128, 512)
    f["pool"] = np.ascontiguousarray(np.concatenate([pw, np.zeros_like(pw)], 1))[None]
    f["wo"] = _units(a(w_o_2)[0])
    f["wq"] = _units(a(w_q_2)[0])
    sk = a(sub_keys_2)[0].reshape(2, 8, 128, 128)
    f["keys"] = np.ascontiguousarray(sk.transpose(0, 3, 1, 2).reshape(2, 128, 1024))
    f["eu"] = np.ascontiguousarray(
        a(expert_u_2)[0].reshape(128, 128, 8, 128).transpose(1, 3, 2, 0)).reshape(128, 128, 1024)
    f["ev"] = np.ascontiguousarray(a(expert_v_2)[0]).reshape(128, 128, 1024)
    f["pleg"] = _units(a(w_ple_gate_2)[0])
    wp = a(w_ple_proj_2)[0].reshape(2, 128, 2, 4, 128)
    f["plep"] = np.ascontiguousarray(wp.transpose(2, 1, 3, 0, 4)).reshape(2, 128, 1024)
    f["pT"] = np.ascontiguousarray(a(p_2)[0, 0].T)

    nc = bacc.Bacc("TRN2", target_bir_lowering=False, num_devices=1)
    t = {k: nc.dram_tensor(f"in_{k}", list(z.shape), mybir.dt.from_np(z.dtype), kind="ExternalInput").ap()
         for k, z in f.items()}
    t["out"] = nc.dram_tensor("out_0", [D, S], F32, kind="ExternalOutput").ap()
    t["gd"] = nc.dram_tensor("gd", [128 // JC, S // TG, 128, JC * TG], F32, kind="Internal").ap()
    build(nc, t)
    r = run_bass_kernel_spmd(nc, [{f"in_{k}": z for k, z in f.items()}], core_ids=[0])
    return np.ascontiguousarray(r.results[0]["out_0"].T)[None]
```

```python
import math
from contextlib import ExitStack

import numpy as np

import concourse.bass as bass
from concourse import mybir

ALU = mybir.AluOpType
ACT = mybir.ActivationFunctionType
AX = mybir.AxisListType
F32 = mybir.dt.float32
F32R = mybir.dt.float32r
BF16 = mybir.dt.bfloat16
U32 = mybir.dt.uint32
I32 = mybir.dt.int32

D = 1024
S = 512
KT = 8
CH = 4
JC = 4
TG = 64
RING = 3
TAPS = 31
NTMP = 12
NSP = 3
NUNITS = 48 + 57 + 16 + 40 + 16 + 16 + 1 + 8 + 16 + 256 + 8 + 2
TWO_PI = 2.0 * math.pi
MAGIC = 12582912.0
NEG = -1e30

VECS = [
    ("c", 8), ("norm_g0", 8), ("norm_g1", 8), ("final_g", 8), ("ada_b0", 24), ("ada_b1", 24),
    ("conv_b", 8), ("ln_w", 8), ("ln_b", 8), ("mu_r", 8), ("mu_k", 8), ("mu_v", 8), ("mu_l", 1),
    ("w0", 8), ("a0", 8), ("k_k", 8), ("k_a", 8), ("gn_w", 8), ("gn_b", 8), ("r_k", 8),
    ("conv_w", 8 * TAPS), ("g_mix", 8), ("g_ffn", 8), ("g_ple", 8), ("g_final", 8),
    ("pool_s", 4), ("conv_w2", 12), ("inv128", 1), ("inv64", 1), ("sgn128", 1), ("sgn64", 1),
]
VOFF = {}
_at = 0
for _n, _w in VECS:
    VOFF[_n] = (_at, _w)
    _at += _w
NVEC = _at


class Eng:

    def __init__(self, sem):
        self.sem, self.n, self.q, self.seen = sem, 0, [], {}

    def wait(self, *toks):
        for t in toks:
            if t is None or not t:
                continue
            if isinstance(t, list):
                self.wait(*t)
                continue
            k, (sem, v) = t[0].name, t
            if self.seen.get(k, 0) < v:
                self.seen[k] = v
                self.q.append((sem, v))

    def __call__(self, f, *a, w=(), inc=True, **k):
        self.wait(*w)
        self.q.append((f, a, k, (self.sem, 1) if inc else None))
        if inc:
            self.n += 1
        return (self.sem, self.n)

    def dma(self, f, dst, src, sem, w=()):
        self.wait(*w)
        self.q.append((f, (dst, src), {}, (sem[0], 16)))
        sem[1] += 16
        return (sem[0], sem[1])

    def last(self):
        return (self.sem, self.n)

    def play(self, eng):
        for x in self.q:
            if len(x) == 2:
                eng.wait_ge(x[0], x[1])
            else:
                f, a, k, inc = x
                if "unit" in k:
                    a, k = (a[0], a[1](k["unit"])), {}
                ins = f(*a, **k)
                if inc is not None:
                    ins.then_inc(inc[0], inc[1])


class Slots:

    def __init__(self, aps):
        self.free = [(ap, []) for ap in aps]

    def take(self):
        assert self.free, "no free slot"
        return self.free.pop(0)

    def give(self, slot, *toks):
        self.free.append((slot[0], list(toks)))


def build(nc, t):
    order = []
    with ExitStack() as ctx:
        def sb(name, shape, dt=F32):
            return ctx.enter_context(nc.sbuf_tensor(name, shape, dt))

        def sem(name):
            return ctx.enter_context(nc.semaphore(name))

        V, A, G, T, Y = (Eng(sem(n)) for n in ("s_dve", "s_act", "s_pool", "s_pe", "s_sp"))
        dve, act, pool, pe, sp = nc.vector, nc.scalar, nc.gpsimd, nc.tensor, nc.sync

        banks = Slots([ctx.enter_context(nc.psum_tensor(f"ps{i}", [128, 512], F32))[:, :]
                       for i in range(8)])
        xT = sb("xT", [128, KT, S])
        hT = sb("hT", [128, 2, KT, S], F32R)
        wsp = sb("wsp", [128, NSP, 2, 1024], F32R)
        wsl = [Slots([wsp[:, i, :, :] for i in range(NSP)])]
        ringt = sb("ring", [128, RING, 1024])
        vec = sb("vec", [128, NVEC])
        mod = sb("mod", [128, 2, 24])
        cond = sb("cond", [128, 8])
        gsc = sb("gsc", [128, 2, 8])
        omka = sb("omka", [128, 8])
        ident = sb("ident", [128, 128])
        ones = sb("ones", [128, 128])
        bones = sb("bones", [128, 128])
        small = sb("small", [128, 8, 64])
        tmp = Slots([])

        def col(name, m=0):
            return vec[:, VOFF[name][0] + m:VOFF[name][0] + m + 1]

        class Phase:

            count = 0

            def __init__(self, ntmp):
                Phase.count += 1
                self.ctx, self.id, self.n, self.ntmp = ExitStack(), Phase.count, 0, ntmp

            def __call__(self, n, dt=F32):
                self.n += 1
                nm = f"p{self.id}_{self.n}"
                return self.ctx.enter_context(nc.sbuf_tensor(nm, [128, n], dt))[:, :]

            def temps(self):
                tmp.free = [(self(512), []) for _ in range(self.ntmp)]

            def leave(self, quiet=True):
                if quiet:
                    fence()
                self.ctx.close()

        def fence():
            toks = [e.last() for e in (V, A, G, T)]
            for e in (V, A, G, T, Y):
                e.wait(*toks)

        s_const = [sem("s_const"), 0]
        c_tok = Y.dma(sp.dma_start, vec[:, :], t["vec"][:, :], s_const)
        c_tok = Y.dma(sp.dma_start, ident[:, :], t["ident"][:, :], s_const)
        c_tok = Y.dma(sp.dma_start, ones[:, :], t["ones"][:, :], s_const)
        c_tok = Y.dma(sp.dma_start, bones[:, :], t["bones"][:, :], s_const)
        s_x = [sem("s_x"), 0]
        ring_sem = [[sem(f"s_w{i}"), 0] for i in range(RING)]
        st = {"loaded": 0, "used": 0, "split": 0, "hl": {}, "tok": {}, "ahead": 1, "pool": False}

        def source(n):
            name, u = order[n]
            return t[name][:, u, :] if name == "ev" else t[name][u]

        def load_next(*w):
            n = st["loaded"]
            if n >= NUNITS:
                return
            slot = n % RING
            Y.wait(*w)
            s_, v_ = ring_sem[slot]
            Y.q.append((sp.dma_start, (ringt[:, slot, :], source), {"unit": n}, (s_, 16)))
            ring_sem[slot][1] += 16
            st["tok"][n] = (s_, v_ + 16)
            st["loaded"] += 1

        for _ in range(RING):
            load_next()
        x_tok = Y.dma(sp.dma_start, xT[:, :, :], t["xT"].rearrange("(k p) s -> p k s", p=128), s_x)

        def unit(name, u):
            n = st["used"]
            assert n == st["split"], "split ahead"
            order.append((name, u))
            st["used"] += 1
            st["split"] += 1
            return ringt[:, n % RING, :].rearrange("p (k m) -> p k m", m=128), st["tok"][n]

        def split_next():
            n = st["split"]
            if n >= NUNITS:
                return
            hl = wsl[0].take()
            raw = ringt[:, n % RING, :]
            a = A(act.activation, hl[0][:, 0, :], raw, ACT.Copy, w=[st["tok"][n], hl[1]])
            E, e = (G, pool) if st["pool"] else (V, dve)
            v = E(e.tensor_tensor, hl[0][:, 1, :], raw, hl[0][:, 0, :].bitcast(F32), ALU.subtract, w=[a])
            load_next(a, v)
            st["hl"][n] = (hl, v)
            st["split"] += 1

        def unit_hl(name, u, nxt=True):
            n = st["used"]
            if st["split"] == n:
                split_next()
            order.append((name, u))
            st["used"] += 1
            while nxt and st["split"] <= n + st["ahead"] and st["split"] < NUNITS:
                split_next()
            hl, v = st["hl"].pop(n)
            return hl, hl[0].rearrange("p a (k m) -> p a k m", m=128), v

        def mm3(out, W, R, first=True, last=True, inc=True):
            T(pe.matmul, out, W[0], R[0], start=first, stop=False, inc=False)
            T(pe.matmul, out, W[0], R[1], start=False, stop=False, inc=False)
            return T(pe.matmul, out, W[1], R[0], start=False, stop=last, inc=inc)

        def split(src, hi, lo, w):
            a = A(act.activation, hi, src, ACT.Copy, w=w)
            return V(dve.tensor_tensor, lo, src, hi.bitcast(F32), ALU.subtract, w=[a])

        def proj_steps(name, u, rhs, out):
            hl, W, tok = unit_hl(name, u)
            b = banks.take()
            T.wait(tok, b[1])
            for k in range(8):
                r = mm3(b[0], (W[:, 0, k, :], W[:, 1, k, :]), (rhs[:, 0, k, :], rhs[:, 1, k, :]),
                        first=(k == 0), last=(k == 7), inc=(k == 7))
                if k in (1, 3, 5):
                    yield
            wsl[0].give(hl, r)
            out[:] = [b, r]

        def proj(name, u, rhs, w=(), first=True, last=True, bank=None, nxt=True):
            hl, W, tok = unit_hl(name, u, nxt)
            b = bank or banks.take()
            T.wait(tok, *w, *([b[1]] if first else []))
            for k in range(8):
                r = mm3(b[0], (W[:, 0, k, :], W[:, 1, k, :]), (rhs[:, 0, k, :], rhs[:, 1, k, :]),
                        first=first and k == 0, last=last and k == 7, inc=(k == 7))
            wsl[0].give(hl, r)
            return b, r

        def rsqrt(ap, w):
            a = A(act.activation, ap, ap, ACT.Sqrt, w=[w])
            return V(dve.reciprocal, ap, ap, w=[a])

        def norm_T(src, dst, g, shift=None, w=()):
            h_free = T.last()
            b = banks.take()
            toks = []
            for k in range(KT):
                q = tmp.take()
                a = A(act.activation, q[0], src[:, k, :], ACT.Square, w=[w, q[1]] if not k else [q[1]])
                r = T(pe.matmul, b[0], ones[:, :], q[0], start=(k == 0), stop=(k == 7), w=[a, b[1], c_tok])
                tmp.give(q, r)
            m = tmp.take()
            v = V(dve.tensor_scalar, m[0], b[0], 1.0 / D, 1e-6, ALU.mult, ALU.add, w=[r, m[1]])
            banks.give(b, v)
            v = rsqrt(m[0], v)
            if dst is None:
                for k in range(KT):
                    toks.append(V(dve.scalar_tensor_tensor, out=src[:, k, :], in0=src[:, k, :],
                                  scalar=g[:, k:k + 1], in1=m[0], op0=ALU.mult, op1=ALU.mult, w=[v, w]))
                tmp.give(m, toks[-1])
                return toks
            for k in range(KT):
                x = tmp.take()
                v2 = V(dve.scalar_tensor_tensor, out=x[0], in0=src[:, k, :], scalar=g[:, k:k + 1],
                       in1=m[0], op0=ALU.mult, op1=ALU.mult, w=[v, w, x[1]])
                if shift is None:
                    v2 = split(x[0], dst[:, 0, k, :], dst[:, 1, k, :], [v2, h_free])
                else:
                    a = A(act.activation, dst[:, 0, k, :], x[0], ACT.Identity, bias=shift[:, k:k + 1],
                          w=[v2, h_free])
                    v2 = V(dve.scalar_tensor_tensor, out=dst[:, 1, k, :], in0=x[0], scalar=shift[:, k:k + 1],
                           in1=dst[:, 0, k, :].bitcast(F32), op0=ALU.add, op1=ALU.subtract, w=[a])
                tmp.give(x, v2)
                toks.append(v2)
            tmp.give(m, v2)
            return toks

        def residual(b, r, m, gate=None):
            if gate is None:
                v = V(dve.tensor_tensor, xT[:, m, :], b[0], xT[:, m, :], ALU.add, w=[r])
            else:
                v = V(dve.scalar_tensor_tensor, out=xT[:, m, :], in0=b[0], scalar=gate,
                      in1=xT[:, m, :], op0=ALU.mult, op1=ALU.add, w=[r])
            banks.give(b, v)
            return v

        row = small[:, :, :].rearrange("p a n -> p (a n)")
        rfree = [[]]

        def modulation(l):
            bc = banks.take()
            T.wait(cond_tok, bc[1])
            for g in range(6):
                b = banks.take()
                T.wait(b[1])
                for kp in range(4):
                    n = st["used"]
                    _, tok = unit("ada", 24 * l + 4 * g + kp)
                    W = ringt[:, n % RING, :].rearrange("p (i n) -> p i n", i=2)
                    for i in range(2):
                        k = 2 * kp + i
                        r = T(pe.matmul, b[0][0:1, :], cond[:, k:k + 1], W[:, i, :], start=(k == 0),
                              stop=(k == 7), w=[tok], inc=(i == 1))
                    load_next(r)
                a = A(act.activation, row[0:1, :], b[0][0:1, :], ACT.Copy, w=[r, rfree[0]])
                banks.give(b, a)
                T.wait(a)
                for i in range(4):
                    m = 4 * g + i
                    r = T(pe.matmul, bc[0][:, m:m + 1], row[0:1, i * 128:(i + 1) * 128], ones[0:1, 0:1],
                          start=True, stop=True, inc=(i == 3))
                rfree[0] = [r]
            b = bc
            o = VOFF[f"ada_b{l}"][0]
            v = V(dve.tensor_tensor, mod[:, l, :], b[0][:, 0:24], vec[:, o:o + 24], ALU.add, w=[r, c_tok])
            banks.give(b, v)
            o = VOFF[f"norm_g{l}"][0]
            v = V(dve.scalar_tensor_tensor, out=gsc[:, l, :], in0=mod[:, l, 8:16], scalar=1.0,
                  in1=vec[:, o:o + 8], op0=ALU.add, op1=ALU.mult, w=[v])
            return v

        cond_tok = A(act.activation, cond[:, :], vec[:, 0:8], ACT.Silu, w=[c_tok])
        oka = VOFF["k_a"][0]
        V(dve.tensor_scalar, omka[:, :], vec[:, oka:oka + 8], -1.0, 1.0, ALU.mult, ALU.add, w=[c_tok])

        m_tok = modulation(0)
        ar0 = Phase(0)
        yc = ar0(4096).rearrange("p (k s) -> p k s", k=8)
        ar = Phase(11)
        ar.temps()
        h_toks = norm_T(xT, hT, gsc[:, 0, :], mod[:, 0, 0:8], w=[x_tok, m_tok])

        us = Slots([ar(S + TAPS - 1) for _ in range(2)])
        zs = Slots([ar(S + 1) for _ in range(2)])
        yb = xT
        yb_w = h_toks
        wl = ar(512)
        lup = ar(1024)
        msk = ar(512, U32)
        lvl = ar(128).rearrange("p (l n) -> p l n", l=1)
        lvh = ar(6 * 64).rearrange("p (l n) -> p l n", l=6)
        PP = ar(CH * 129).rearrange("p (c n) -> p c n", c=CH)
        d1 = ar(512)

        def chunked(ap):
            return ap.rearrange("p (c n) -> p c n", c=CH)

        Bes, Khs = Slots([ar(512)]), Slots([ar(512)])
        bons = Slots([ar(512) for _ in range(2)])
        sets = Slots([{"KR": ar(1024).rearrange("p (c a n) -> p c a n", c=CH, a=2), "dd": ar(CH),
                       "Vt": chunked(ar(512)), "Bt": chunked(ar(512)), "Kt": chunked(ar(512))}
                      for _ in range(2)])
        AB = ar(2048).rearrange("p (e c a n) -> p e c a n", e=2, c=CH, a=2)
        AK = ar(2048).rearrange("p (e c a n) -> p e c a n", e=2, c=CH, a=2)
        X = ar(1024).rearrange("p (e c n) -> p e c n", e=2, c=CH)
        XT = ar(1024).rearrange("p (e c n) -> p e c n", e=2, c=CH)
        P1 = ar(512).rearrange("p (e c n) -> p e c n", e=2, c=CH)
        Sbd = ar(128)
        Su = ar(128)
        x1n = ar(128)
        SA = ar(128)
        s_rc = [sem("s_rc"), 0]
        Y.dma(sp.dma_start, msk, t["msk"][:, :], s_rc)
        Y.dma(sp.dma_start, lup, t["lup"][:, :], s_rc)
        Y.dma(sp.dma_start, lvh.rearrange("p l n -> p (l n)"), t["lvh"][:, :], s_rc)
        rc_tok = Y.dma(sp.dma_start, lvl.rearrange("p l n -> p (l n)"), t["lvl"][:, :], s_rc)
        V(dve.memset, AB, 0.0)
        V(dve.memset, AK, 0.0)
        z0 = ([V(dve.memset, d1, 0.0)] + [V(dve.memset, z[0][:, 0:1], 0.0) for z in zs.free]
              + [V(dve.memset, u[0][:, 0:TAPS - 1], 0.0) for u in us.free])
        y_toks = []

        def conv(m):
            o = []
            yield from proj_steps("ein", m, hT, o)
            bv, rv = o
            yield
            yield from proj_steps("ein", 8 + m, hT, o)
            bg, rg = o
            s = tmp.take()
            a = A(act.activation, s[0], bg[0], ACT.Sigmoid, w=[rg, s[1]])
            banks.give(bg, a)
            u = us.take()
            v = V(dve.tensor_tensor, u[0][:, TAPS - 1:], bv[0], s[0], ALU.mult, w=[rv, a, u[1], z0])
            banks.give(bv, v)
            tmp.give(s, v)
            yield
            cw = lambda k: col("conv_w", m * TAPS + k)
            v = V(dve.tensor_scalar, yc[:, m, :], u[0][:, 0:S], cw(0), col("conv_b", m),
                  ALU.mult, ALU.add, w=[v])
            for k in range(1, TAPS):
                v = V(dve.scalar_tensor_tensor, out=yc[:, m, :], in0=u[0][:, k:k + S], scalar=cw(k),
                      in1=yc[:, m, :], op0=ALU.mult, op1=ALU.add, w=[v])
                yield
            us.give(u, v)
            y_toks.append(v)

        def shifted(name, u, mu_col, out, res, w=()):
            o = []
            yield from proj_steps(name, u, hT, o)
            b, r = o
            z = zs.take()
            a = A(act.activation, z[0][:, 1:], b[0], ACT.Copy, w=[r, z[1], z0])
            banks.give(b, a)
            d = tmp.take()
            g = G(pool.tensor_tensor, d[0], z[0][:, 0:S], z[0][:, 1:], ALU.subtract, w=[a, d[1]])
            v = V(dve.scalar_tensor_tensor, out=out, in0=d[0], scalar=mu_col, in1=z[0][:, 1:],
                  op0=ALU.mult, op1=ALU.add, w=[g, w])
            tmp.give(d, v)
            zs.give(z, v)
            res.append(v)

        res = []
        for _ in shifted("ein", 48, col("mu_l"), wl, res):
            pass
        v = res[0]
        wl_tok = A(act.activation, wl[0:64, :], wl[0:64, :], ACT.Tanh, w=[v])

        def prep(c, out):
            s = sets.take()
            d = s[0]
            out["s"] = s
            sw = s[1]
            k = tmp.take()
            r_ = tmp.take()
            v_ = tmp.take()
            res = []
            yield from shifted("ein", 24 + c, col("mu_r", c), r_[0], res, w=[r_[1]])
            tr = res[0]
            yield
            res = []
            yield from shifted("ein", 32 + c, col("mu_k", c), k[0], res, w=[k[1]])
            tk = res[0]
            yield
            res = []
            yield from shifted("ein", 40 + c, col("mu_v", c), v_[0], res, w=[v_[1]])
            tv = res[0]
            yield
            b1 = banks.take()
            r1 = T(pe.matmul, b1[0], lup[0:64, c * 128:(c + 1) * 128], wl[0:64, :], start=True, stop=True,
                   w=[b1[1], wl_tok, rc_tok])
            b2 = banks.take()
            r2 = T(pe.matmul, b2[0], lup[64:128, c * 128:(c + 1) * 128], wl[64:128, :], start=True, stop=True,
                   w=[b2[1]])
            wd = tmp.take()
            aa = tmp.take()
            a = A(act.activation, wd[0], b1[0], ACT.Sigmoid, bias=col("w0", c), w=[r1, wd[1]])
            banks.give(b1, a)
            ta = A(act.activation, aa[0], b2[0], ACT.Sigmoid, bias=col("a0", c), w=[r2, aa[1]])
            banks.give(b2, ta)
            sq = tmp.take()
            a2 = A(act.activation, sq[0], k[0], ACT.Square, scale=col("k_k", c), w=[tk, sq[1]])
            b = banks.take()
            r = T(pe.matmul, b[0], bones[:, :], sq[0], start=True, stop=True, w=[a2, b[1]])
            tw = A(act.activation, wd[0], wd[0], ACT.Exp, scale=-math.exp(-0.5), w=[a])
            yield
            v = V(dve.tensor_scalar, sq[0], b[0], 1e-24, None, ALU.max, w=[r])
            banks.give(b, v)
            vr = A(act.activation, sq[0], sq[0], ACT.Sqrt, w=[v])
            for i in range(CH):
                v = V(dve.reciprocal, chunked(sq[0])[:, i, :], chunked(sq[0])[:, i, :], w=[vr])
                yield
            kk = tmp.take()
            v = V(dve.scalar_tensor_tensor, out=kk[0], in0=k[0], scalar=col("k_k", c), in1=sq[0],
                  op0=ALU.mult, op1=ALU.mult, w=[v, kk[1]])
            tmp.give(sq, v)
            tkk = v
            k2 = tmp.take()
            v = V(dve.tensor_scalar, k2[0], aa[0], col("k_a", c), omka[:, c:c + 1], ALU.mult, ALU.add,
                  w=[ta, k2[1]])
            tk2 = V(dve.tensor_tensor, k2[0], k2[0], k[0], ALU.mult, w=[v])
            tmp.give(k, tk2)
            tb = G(pool.tensor_tensor, aa[0], aa[0], kk[0], ALU.mult, w=[tkk, v])
            yield
            w4 = wd[0].rearrange("p (c n) -> p c n", c=CH)
            v = V(dve.tensor_copy, d1.rearrange("p (c n) -> p c n", c=CH)[:, :, 0:1], w4[:, :, 0:1], w=[tw, z0])
            v = V(dve.memset, w4[:, :, 0:1], 0.0, w=[v])
            pw = tmp.take()
            v = V(dve.tensor_tensor_scan, pw[0], wd[0], d1, 0.0, ALU.mult, ALU.add, w=[v, pw[1]])
            tmp.give(wd, v)
            p4 = pw[0].rearrange("p (c n) -> p c n", c=CH)
            v2 = V(dve.reciprocal, PP[:, :, 0:1], p4[:, :, 63:64], w=[v])
            v = V(dve.tensor_tensor, PP[:, :, 1:129], p4, PP[:, :, 0:1].broadcast_to([128, CH, 128]), ALU.mult,
                  w=[v2])
            vd = V(dve.tensor_tensor, d["dd"][:, 0:3], PP[:, 0:3, 128:129].rearrange("p c n -> p (c n)"),
                   p4[:, 1:4, 63:64].rearrange("p c n -> p (c n)"), ALU.mult, w=[v, sw])
            pi4 = pw[0].rearrange("p (c n) -> p c n", c=CH)
            for q in range(CH):
                vi = V(dve.reciprocal, pi4[:, q, :], PP[:, q, 1:129], w=[vd])
                yield
            KR = d["KR"]
            f4 = lambda ap: ap.rearrange("p (c n) -> p c n", c=CH)
            g1 = G(pool.tensor_tensor, KR[:, :, 0, :], f4(kk[0]), PP[:, :, 0:128], ALU.mult, w=[v, tkk, sw])
            g2 = V(dve.tensor_tensor, KR[:, :, 1, :], f4(r_[0]), PP[:, :, 1:129], ALU.mult, w=[v, tr, sw])
            tmp.give(kk, g1)
            out["PPfree"] = [g1, g2]
            V.wait(g1)
            Be, Kh, bon = Bes.take(), Khs.take(), bons.take()
            out["b"] = (Be, Kh, bon)
            vB = V(dve.tensor_tensor, Be[0], aa[0], pw[0], ALU.mult, w=[tb, vi, Be[1]])
            vK = V(dve.tensor_tensor, Kh[0], k2[0], pw[0], ALU.mult, w=[tk2, vi, Kh[1]])
            tmp.give(aa, vB)
            tmp.give(pw, vK)
            v = V(dve.scalar_tensor_tensor, out=r_[0], in0=r_[0], scalar=col("r_k", c), in1=k2[0],
                  op0=ALU.mult, op1=ALU.mult, w=[g2])
            tmp.give(k2, v)
            b = banks.take()
            r = T(pe.matmul, b[0], bones[:, :], r_[0], start=True, stop=True, w=[v, b[1]])
            yield
            tmp.give(r_, r)
            vb = V(dve.tensor_tensor, bon[0], b[0], v_[0], ALU.mult, w=[r, tv, bon[1]])
            banks.give(b, vb)
            tt = []
            for src, dst, tk_ in ((v_[0], "Vt", tv), (Be[0], "Bt", vB), (Kh[0], "Kt", vK)):
                b = banks.take()
                T.wait(tk_, b[1])
                for q in range(CH):
                    r = T(pe.transpose, b[0][:, q * 128:(q + 1) * 128], src[:, q * 128:(q + 1) * 128],
                          ident[:, :], inc=(q == 3))
                a = A(act.activation, d[dst].rearrange("p c n -> p (c n)"), b[0], ACT.Copy, w=[r, sw])
                banks.give(b, a)
                if dst == "Vt":
                    tmp.give(v_, r, vb)
                tt.append(a)
                yield
            out["tok"] = [g1, g2, vB, vK, vd] + tt
            out["bon"] = vb

        st2 = {"ab": [], "y": []}

        def solve(c, inp):
            s = inp["s"]
            d = s[0]
            KR = d["KR"]
            sBe, sKh, bon = inp["b"]
            Be, Kh = sBe[0], sKh[0]
            T.wait(inp["tok"])
            ev = []
            for e in range(2):
                p = slice(64 * e, 64 * e + 64)
                for dst, lhs in ((AB, Be), (AK, Kh)):
                    for cc in range(0, CH, 2):
                        b = banks.take()
                        T.wait(b[1])
                        for q in range(2):
                            r = T(pe.matmul, b[0][:, q * 256:(q + 1) * 256],
                                  lhs[p, (cc + q) * 128:(cc + q + 1) * 128],
                                  KR[p, cc + q, :, :].rearrange("p a n -> p (a n)"),
                                  start=True, stop=True, inc=(q == 1))
                        v = V(dve.copy_predicated, dst[:, e, cc:cc + 2, :, :].rearrange("p c a n -> p (c a n)"),
                              msk, b[0], w=[r, rc_tok, st2["ab"]])
                        banks.give(b, v)
                        ev.append(v)
                    yield
            Bes.give(sBe, r)
            Khs.give(sKh, r)
            toks = {}

            def turn(e, w):
                b = banks.take()
                T.wait(b[1], w)
                for q in range(CH):
                    r = T(pe.transpose, b[0][:, q * 128:(q + 1) * 128], src[:, e, q, :], ident[:, :], inc=(q == 3))
                a = A(act.activation, dst[:, e, :, :].rearrange("p c n -> p (c n)"), b[0], ACT.Copy, w=[r])
                banks.give(b, a)
                return a

            src, dst = XT, X
            for e in range(2):
                g = G(pool.tensor_tensor, XT[:, e, :, :], AB[:, e, :, 0, :],
                      lvl[:, 0:1, :].broadcast_to([128, CH, 128]), ALU.mult, w=[ev, st2["ab"]])
                g = G(pool.tensor_tensor, XT[:, e, :, :], XT[:, e, :, :],
                      ident[:, :].rearrange("p (o n) -> p o n", o=1).broadcast_to([128, CH, 128]), ALU.add, w=[g])
                toks[e] = g
            yield
            for e in range(2):
                toks[e] = [toks[e], turn(e, toks[e])]
            yield
            src, dst = X, XT
            for l in range(1, 7):
                n = 1 << l
                even = lambda ap: ap.rearrange("p c (b two s) -> p c b two s", two=2, s=n)[:, :, :, 0, :]
                p1 = {}
                for e in range(2):
                    b = banks.take()
                    T.wait(b[1], toks[e], ev)
                    for q in range(CH):
                        r = T(pe.matmul, b[0][:, q * 64:(q + 1) * 64], AB[:, e, q, 0, :],
                              even(X[:, e, q:q + 1, :]).rearrange("p o b s -> p (o b) s"),
                              start=True, stop=True, inc=(q == 3))
                    v = V(dve.tensor_tensor, P1[:, e, :, :], b[0][:, 0:256].rearrange("p (c n) -> p c n", c=CH),
                          lvh[:, l - 1:l, :].broadcast_to([128, CH, 64]), ALU.mult, w=[r])
                    banks.give(b, v)
                    p1[e] = v
                yield
                for e in range(2):
                    b = banks.take()
                    T.wait(b[1], p1[e])
                    for q in range(CH):
                        r = T(pe.matmul, b[0][:, q * 64:(q + 1) * 64], XT[:, e, q, :], P1[:, e, q, :],
                              start=True, stop=True, inc=(q == 3))
                    for q in range(CH):
                        xe = even(X[:, e, q:q + 1, :]).rearrange("p o b s -> p (o b) s")
                        v = V(dve.tensor_tensor, xe, xe,
                              b[0][:, q * 64:(q + 1) * 64].rearrange("p (b s) -> p b s", s=n), ALU.subtract, w=[r])
                    banks.give(b, v)
                    p1[e] = v
                yield
                for e in range(2):
                    toks[e] = [turn(e, p1[e])]
                yield
            ts = V(dve.memset, Sbd, 0.0, w=[st2["y"]])
            by = banks.take()
            T.wait(by[1])
            for q in range(CH):
                b = banks.take()
                T.wait(b[1], ts, toks[0], toks[1])
                for e in range(2):
                    xe = b[0][:, 64 * e:64 * e + 64]
                    T(pe.matmul, xe, KR[:, q, 0, :], Sbd[:, 64 * e:64 * e + 64], start=True, stop=False, inc=False)
                    r = T(pe.matmul, xe, AK[:, e, q, 0, :], d["Vt"][:, q, 64 * e:64 * e + 64],
                          start=False, stop=True, inc=(e == 1))
                a = A(act.activation, x1n, b[0][:, 0:128], ACT.Copy, scale=-1.0, w=[r, st2["y"]])
                banks.give(b, a)
                yield
                b = banks.take()
                T.wait(b[1], a)
                for e in range(2):
                    r = T(pe.matmul, b[0][:, 64 * e:64 * e + 64], XT[:, e, q, :], x1n[:, 64 * e:64 * e + 64],
                          start=True, stop=True, inc=(e == 1))
                a = A(act.activation, SA, b[0][:, 0:128], ACT.Copy, w=[r, st2["y"]])
                banks.give(b, a)
                yield
                yo = by[0][:, q * 128:(q + 1) * 128]
                T.wait(a)
                b = None
                if q < CH - 1:
                    b = banks.take()
                    T.wait(b[1])
                    T(pe.matmul, b[0][:, 0:128], d["Bt"][:, q, :], SA, start=True, stop=False, inc=False)
                    r = T(pe.matmul, b[0][:, 0:128], d["Kt"][:, q, :], d["Vt"][:, q, :], start=False, stop=True)
                    v = V(dve.tensor_tensor, Su, b[0][:, 0:128], Sbd, ALU.add, w=[r, ts])
                    banks.give(b, v)
                for e in range(2):
                    ye = yo[64 * e:64 * e + 64, :]
                    T(pe.matmul, ye, Sbd[:, 64 * e:64 * e + 64], KR[:, q, 1, :], start=True, stop=False, inc=False)
                    T(pe.matmul, ye, SA[:, 64 * e:64 * e + 64], AB[:, e, q, 1, :], start=False, stop=False,
                      inc=False)
                    ry = T(pe.matmul, ye, d["Vt"][:, q, 64 * e:64 * e + 64], AK[:, e, q, 1, :], start=False,
                           stop=True, inc=(e == 1))
                st2["y"] = [ry]
                if q < CH - 1:
                    ts = V(dve.scalar_tensor_tensor, out=Sbd, in0=Su, scalar=d["dd"][:, q:q + 1], in1=bones[:, :],
                           op0=ALU.mult, op1=ALU.mult, w=[v, ry])
                yield
            st2["ab"] = [ry]
            y = tmp.take()
            a = A(act.activation, y[0], by[0], ACT.Copy, w=[ry, y[1]])
            banks.give(by, a)
            b = banks.take()
            r = T(pe.matmul, b[0], bones[:, :], y[0], start=True, stop=True, w=[a, b[1]])
            v = V(dve.scalar_tensor_tensor, out=y[0], in0=b[0], scalar=-1.0 / 64, in1=y[0], op0=ALU.mult,
                  op1=ALU.add, w=[r])
            banks.give(b, v)
            yield
            q = tmp.take()
            a = A(act.activation, q[0], y[0], ACT.Square, w=[v, q[1]])
            b = banks.take()
            r = T(pe.matmul, b[0], bones[:, :], q[0], start=True, stop=True, w=[a, b[1]])
            gs = tmp.take()
            o = []
            yield from proj_steps("ein", 49 + c, hT, o)
            bg, rg = o
            tg = A(act.activation, gs[0], bg[0], ACT.Silu, w=[rg, gs[1]])
            banks.give(bg, tg)
            yield
            v = V(dve.tensor_scalar, q[0], b[0], 1.0 / 64, 64e-5, ALU.mult, ALU.add, w=[r])
            banks.give(b, v)
            vr = A(act.activation, q[0], q[0], ACT.Sqrt, w=[v])
            for i in range(CH):
                v = V(dve.reciprocal, chunked(q[0])[:, i, :], chunked(q[0])[:, i, :], w=[vr])
                yield
            v = V(dve.scalar_tensor_tensor, out=y[0], in0=y[0], scalar=col("gn_w", c), in1=q[0], op0=ALU.mult,
                  op1=ALU.mult, w=[v])
            v = V(dve.scalar_tensor_tensor, out=y[0], in0=y[0], scalar=col("gn_b", c), in1=bon[0], op0=ALU.add,
                  op1=ALU.add, w=[v, inp["bon"]])
            bons.give(bon, v)
            g = G(pool.tensor_tensor, yb[:, c, :], y[0], gs[0], ALU.mult, w=[v, tg, yb_w])
            tmp.give(gs, g)
            tmp.give(y, g)
            tmp.give(q, v)
            yb_toks.append(g)
            sets.give(s, ry, g, v)

        yb_toks = []

        def run(*gens):
            live = [[0.0, i, 1.0 / n, g] for i, (g, n) in enumerate(gens)]
            while live:
                x = min(live)
                try:
                    next(x[3])
                    x[0] += x[2]
                except StopIteration:
                    live.remove(x)

        o = {}
        st["pool"] = True
        run((prep(0, o), 26), (conv(0), 37))
        for c in range(8):
            o2 = {}
            gens = [(solve(c, o), 48)]
            if c < 7:
                gens += [(prep(c + 1, o2), 26), (conv(c + 1), 37)]
            run(*gens)
            o = o2

        st["pool"] = False
        b = banks.take()
        for m in range(8):
            r = T(pe.matmul, b[0], ones[:, :], yc[:, m, :], start=(m == 0), stop=(m == 7),
                  w=[y_toks[m], b[1]])
        mu = tmp.take()
        a = A(act.activation, mu[0], b[0], ACT.Copy, scale=1.0 / D, w=[r, mu[1]])
        banks.give(b, a)
        b = banks.take()
        for m in range(8):
            v = V(dve.tensor_tensor, yc[:, m, :], yc[:, m, :], mu[0], ALU.subtract, w=[a])
            q = tmp.take()
            a2 = A(act.activation, q[0], yc[:, m, :], ACT.Square, w=[v, q[1]])
            r = T(pe.matmul, b[0], ones[:, :], q[0], start=(m == 0), stop=(m == 7), w=[a2, b[1]])
            tmp.give(q, r)
        v = V(dve.tensor_scalar, mu[0], b[0], 1.0 / D, 1e-5, ALU.mult, ALU.add, w=[r, v])
        banks.give(b, v)
        vr = rsqrt(mu[0], v)
        ya_toks = []
        for m in range(8):
            ba, ra = proj("ein", 16 + m, hT)
            ag = tmp.take()
            a = A(act.activation, ag[0], ba[0], ACT.Silu, w=[ra, ag[1]])
            banks.give(ba, a)
            v = V(dve.tensor_tensor, yc[:, m, :], yc[:, m, :], mu[0], ALU.mult, w=[vr])
            a = A(act.activation, yc[:, m, :], yc[:, m, :], ACT.Silu, scale=col("ln_w", m),
                  bias=col("ln_b", m), w=[v])
            ya_toks.append(V(dve.tensor_tensor, yc[:, m, :], yc[:, m, :], ag[0], ALU.mult, w=[a]))
            tmp.give(ag, ya_toks[-1])
        tmp.give(mu, v)
        hf = T.last()
        ar.leave()
        ar = Phase(8)
        ar.temps()
        xr = ar(4096).rearrange("p (k s) -> p k s", k=8)
        x_tok = Y.dma(sp.dma_start, xr, t["xT"].rearrange("(k p) s -> p k s", p=128), s_x)
        h_toks = [split(yc[:, k, :], hT[:, 0, k, :], hT[:, 1, k, :], [hf, ya_toks[k]]) for k in range(8)]
        for m in range(8):
            b, r = proj("eout", 2 * m, hT, w=[h_toks])
            v = V(dve.scalar_tensor_tensor, out=xr[:, m, :], in0=b[0], scalar=mod[:, 0, 16 + m:17 + m],
                  in1=xr[:, m, :], op0=ALU.mult, op1=ALU.add, w=[r, x_tok])
            banks.give(b, v)
        h_toks = [split(yb[:, k, :], hT[:, 0, k, :], hT[:, 1, k, :], [r, yb_toks[k]]) for k in range(8)]
        for m in range(8):
            b, r = proj("eout", 2 * m + 1, hT, w=[h_toks], nxt=(m < 7))
            v = V(dve.scalar_tensor_tensor, out=xT[:, m, :], in0=b[0], scalar=mod[:, 0, 16 + m:17 + m],
                  in1=xr[:, m, :], op0=ALU.mult, op1=ALU.add, w=[r, h_toks])
            banks.give(b, v)

        m_tok = modulation(1)
        h_toks = norm_T(xT, hT, gsc[:, 1, :], mod[:, 1, 0:8], w=[m_tok, V.last()])
        ar.leave()
        ar0.leave(False)
        ar = Phase(14)
        ar.temps()
        og = ar(8192).rearrange("p (k s) -> p k s", k=16)
        tabs = {}
        posf = ar(512)
        posi = tmp.take()
        s_p = [sem("s_p"), 0]
        ptok = Y.dma(sp.dma_start, posi[0].bitcast(I32), t["positions"].partition_broadcast(128), s_p,
                     w=[posi[1]])
        pcol = ar(4)
        pcr = ar(4)
        ptok2 = Y.dma(sp.dma_start, pcr.bitcast(I32), t["pcol"][:, :], s_p)
        v = V(dve.tensor_copy, posf, posi[0].bitcast(I32), w=[ptok2])
        C1 = 6.28125
        C2 = float(np.float32(np.round((TWO_PI - C1) * 2 ** 21) / 2 ** 21))
        C3 = float(TWO_PI - C1 - C2)
        for nm, inv, sgn in (("128", "inv128", "sgn128"), ("64", "inv64", "sgn64")):
            ang, n, cosT, sinT = tmp.take(), tmp.take(), ar(512), ar(512)
            v = V(dve.tensor_scalar, ang[0], posf, col(inv), None, ALU.mult, w=[v, ang[1]])
            v = V(dve.tensor_scalar, n[0], ang[0], 1.0 / TWO_PI, None, ALU.mult, w=[v, n[1]])
            v = V(dve.tensor_scalar, n[0], n[0], MAGIC, None, ALU.add, w=[v])
            v = V(dve.tensor_scalar, n[0], n[0], -MAGIC, None, ALU.add, w=[v])
            for cst in (C1, C2, C3):
                v = V(dve.scalar_tensor_tensor, out=ang[0], in0=n[0], scalar=-cst, in1=ang[0],
                      op0=ALU.mult, op1=ALU.add, w=[v])
            v = V(dve.tensor_scalar, ang[0], ang[0], 3.1415925, -3.1415925, ALU.min, ALU.max, w=[v])
            a = A(act.activation, sinT, ang[0], ACT.Sin, w=[v])
            vs = V(dve.tensor_scalar, sinT, sinT, col(sgn), None, ALU.mult, w=[a])
            v = V(dve.tensor_scalar, ang[0], ang[0], math.pi / 2, None, ALU.add, w=[a])
            v = V(dve.tensor_scalar, n[0], ang[0], math.pi, -TWO_PI, ALU.is_gt, ALU.mult, w=[v])
            v = V(dve.tensor_tensor, ang[0], ang[0], n[0], ALU.add, w=[v])
            v = V(dve.tensor_scalar, ang[0], ang[0], 3.1415925, -3.1415925, ALU.min, ALU.max, w=[v])
            a = A(act.activation, cosT, ang[0], ACT.Sin, w=[v])
            tmp.give(ang, a)
            tmp.give(n, v)
            tabs[nm] = (cosT, sinT, [a, vs])
        cidr = ar(512)
        v = V(dve.tensor_scalar, posi[0].bitcast(I32), posi[0].bitcast(I32), 6, None,
              ALU.arith_shift_right, w=[v])
        v = V(dve.tensor_copy, cidr, posi[0].bitcast(I32), w=[v])
        tmp.give(posi, v)
        v = V(dve.tensor_scalar, pcr.bitcast(I32), pcr.bitcast(I32), 6, None, ALU.arith_shift_right, w=[v, ptok2])
        cid_tok = V(dve.tensor_copy, pcol, pcr.bitcast(I32), w=[v])

        def rope(b, r, tab, out, w=()):
            cosT, sinT, tt = tabs[tab]
            h = int(tab) // 2
            m, n = tmp.take(), tmp.take()
            v1 = V(dve.tensor_tensor, m[0], b[0], cosT, ALU.mult, w=[r, m[1], tt])
            V.wait(n[1])
            for p in range(0, 128, h):
                q = p + h if (p // h) % 2 == 0 else p - h
                v2 = V(dve.tensor_tensor, n[0][p:p + h, :], b[0][q:q + h, :], sinT[q:q + h, :], ALU.mult)
            banks.give(b, v2)
            g = G(pool.tensor_tensor, out, m[0], n[0], ALU.add, w=[v1, v2, w])
            tmp.give(m, g)
            tmp.give(n, g)
            return g

        kT = ar(512)
        b, r = proj("oin", 16, hT, w=[h_toks])
        k_tok = rope(b, r, "128", kT)
        hl, W, tok = unit_hl("oin", 17)
        b = banks.take()
        T.wait(tok, b[1])
        for q in range(4):
            for k in range(8):
                r = mm3(b[0][:, q * 128:(q + 1) * 128],
                        [hT[:, i, k, q * 128:(q + 1) * 128] for i in range(2)], [W[:, i, k, :] for i in range(2)],
                        first=(k == 0), last=(k == 7), inc=(k == 7))
        wsl[0].give(hl, r)
        Vs = ar(512).rearrange("p (s n) -> p s n", s=4)
        v_tok = A(act.activation, Vs.rearrange("p s n -> p (s n)"), b[0], ACT.Copy, w=[r])
        banks.give(b, v_tok)
        kiT = ar(512)
        b, r = proj("oin", 22, hT)
        ki_tok = rope(b, r, "64", kiT)
        hl, W, tok = unit_hl("oin", 23)
        b = banks.take()
        T.wait(tok, b[1])
        for q in range(4):
            for k in range(8):
                r = mm3(b[0][:, q * 8:q * 8 + 8],
                        [hT[:, i, k, q * 128:(q + 1) * 128] for i in range(2)], [W[:, i, k, 0:8] for i in range(2)],
                        first=(k == 0), last=(k == 7), inc=(k == 7))
        wsl[0].give(hl, r)
        wi = ar(32)
        wi_tok = A(act.activation, wi, b[0][:, 0:32], ACT.Copy, scale=8.0 ** -0.5, w=[r])
        banks.give(b, wi_tok)
        qi = ar(2048).rearrange("p (k s) -> p k s", k=4)
        qi_toks = []
        for m in range(4):
            b, r = proj("oin", 18 + m, hT)
            qi_toks.append(rope(b, r, "64", qi[:, m, :]))
        selb = ar(2048).rearrange("p (b s) -> p b s", b=4)
        m8 = ar(8)
        sel_toks = []
        gate_units = list(range(16))
        og_toks = {}

        def gate_proj():
            if gate_units:
                m = gate_units.pop(0)
                b, r = proj("oin", 24 + m, hT)
                og_toks[m] = A(act.activation, og[:, m, :], b[0], ACT.Silu, w=[r])
                banks.give(b, og_toks[m])

        m8_free = []
        for blk in range(4):
            acc, val = tmp.take(), tmp.take()
            v = None
            for h in range(8):
                e = h % 2
                b = banks.take()
                r = T(pe.matmul, b[0], qi[64 * e:64 * e + 64, h // 2, blk * 128:(blk + 1) * 128],
                      kiT[64 * e:64 * e + 64, :], start=True, stop=True, w=[b[1], qi_toks, ki_tok])
                x = tmp.take()
                a = A(act.activation, x[0], b[0], ACT.Relu, scale=0.125, w=[r, x[1]])
                banks.give(b, a)
                wc = wi[:, blk * 8 + h:blk * 8 + h + 1]
                if h == 0:
                    v = V(dve.tensor_scalar, acc[0], x[0], wc, None, ALU.mult, w=[a, wi_tok, acc[1]])
                else:
                    v = V(dve.scalar_tensor_tensor, out=acc[0], in0=x[0], scalar=wc, in1=acc[0],
                          op0=ALU.mult, op1=ALU.add, w=[a, v])
                tmp.give(x, v)
            v2 = V(dve.tensor_scalar, val[0], cidr, pcol[:, blk:blk + 1], None, ALU.is_le, w=[cid_tok, val[1]])
            v = V(dve.tensor_tensor, acc[0], acc[0], val[0], ALU.mult, w=[v, v2])
            x = tmp.take()
            v2 = V(dve.tensor_scalar, x[0], val[0], -1.0, -NEG, ALU.add, ALU.mult, w=[v2, x[1]])
            v = V(dve.tensor_tensor, acc[0], acc[0], x[0], ALU.add, w=[v, v2])
            cur = acc[0]
            for i in range(16):
                v = V(dve.max, m8, cur, w=[v, m8_free])
                v = V(dve.match_replace, x[0], m8, cur, -3e38, w=[v])
                cur = x[0]
            v = V(dve.tensor_tensor, x[0], x[0], acc[0], ALU.not_equal, w=[v])
            v = V(dve.tensor_tensor, x[0], x[0], val[0], ALU.mult, w=[v])
            v = V(dve.tensor_scalar, selb[:, blk, :], x[0], -1.0, -NEG, ALU.add, ALU.mult, w=[v])
            sel_toks.append(v)
            tmp.give(acc, v)
            tmp.give(val, v)
            tmp.give(x, v)
            for _ in range(4):
                gate_proj()

        SC = 128 ** -0.5
        qTs = Slots([ar(512) for _ in range(2)])
        PTs = Slots([ar(2048).rearrange("p (s q) -> p s q", s=4) for _ in range(2)])
        sms = Slots([small[:, i, 0:4] for i in range(8)])

        def q_part(h, out):
            b, r = proj("oin", h, hT)
            qT = qTs.take()
            out["q"] = (qT, rope(b, r, "128", qT[0], w=[qT[1]]))

        def attend(h, inp):
            qT, q_tok = inp["q"]
            PT = PTs.take()
            evs = []
            Ps = []
            for blk in range(4):
                b = banks.take()
                r = T(pe.matmul, b[0], qT[0][:, blk * 128:(blk + 1) * 128], kT, start=True, stop=True,
                      w=[b[1], q_tok, k_tok])
                p, c4 = tmp.take(), sms.take()
                v = V(dve.tensor_tensor_reduce, out=p[0], in0=b[0], in1=selb[:, blk, :], scale=1.0,
                      scalar=-3e38, op0=ALU.add, op1=ALU.max, accum_out=c4[0][:, 0:1],
                      w=[r, p[1], c4[1], sel_toks[blk]])
                banks.give(b, v)
                v = V(dve.tensor_scalar, c4[0][:, 1:2], c4[0][:, 0:1], -SC, None, ALU.mult, w=[v])
                a = A(act.activation, p[0], p[0], ACT.Exp, scale=SC, bias=c4[0][:, 1:2],
                      accum_out=c4[0][:, 2:3], w=[v])
                Ps.append((p, c4, a))
            qTs.give(qT, r)
            yield
            for blk in range(4):
                p, c4, a = Ps[blk]
                v = V(dve.reciprocal, c4[0][:, 3:4], c4[0][:, 2:3], w=[a])
                g = G(pool.tensor_scalar, p[0], p[0], c4[0][:, 3:4], None, ALU.mult, w=[v])
                sms.give(c4, g)
                b = banks.take()
                T.wait(b[1], g)
                for s in range(4):
                    r = T(pe.transpose, b[0][:, s * 128:(s + 1) * 128], p[0][:, s * 128:(s + 1) * 128],
                          ident[:, :], inc=(s == 3))
                tmp.give(p, r)
                dst = PT[0][:, :, blk * 128:(blk + 1) * 128]
                srcb = b[0].rearrange("p (s q) -> p s q", s=4)
                if blk % 2:
                    e = V(dve.tensor_copy, dst, srcb, w=[r, PT[1]])
                else:
                    e = A(act.activation, dst, srcb, ACT.Copy, w=[r, PT[1]])
                banks.give(b, e)
                evs.append(e)
            yield
            b = banks.take()
            T.wait(b[1], evs, v_tok)
            for s in range(4):
                r = T(pe.matmul, b[0], Vs[:, s, :], PT[0][:, s, :], start=(s == 0), stop=(s == 3), inc=(s == 3))
            PTs.give(PT, r)
            v = V(dve.tensor_tensor, og[:, h, :], b[0], og[:, h, :], ALU.mult, w=[r, og_toks[h]])
            banks.give(b, v)
            og_toks[h] = v

        nxt = {}
        q_part(0, nxt)
        old = None
        for h in range(16):
            g = attend(h, nxt)
            next(g)
            if old:
                next(old)
            nxt = {}
            if h < 15:
                q_part(h + 1, nxt)
            if old:
                next(old, None)
            old = g
        next(old)
        next(old, None)
        for half in range(2):
            h_toks = [split(og[:, 8 * half + k, :], hT[:, 0, k, :], hT[:, 1, k, :], [T.last(), og_toks[8 * half + k]])
                      for k in range(8)]
            for m in range(8):
                b, r = proj("oout", 2 * m + half, hT, w=[h_toks])
                v = residual(b, r, m, gate=mod[:, 1, 16 + m:17 + m])
        ar.leave()
        ar = Phase(14)
        ar.temps()
        o = VOFF["final_g"][0]
        f_toks = norm_T(xT, None, vec[:, o:o + 8], w=[V.last()])

        o = VOFF["g_mix"][0]
        h_toks = norm_T(xT, hT, vec[:, o:o + 8], w=f_toks)
        ym = ar(4096).rearrange("p (k s) -> p k s", k=8)
        PADL = 16
        zp = [ar(S + 2 * PADL) for _ in range(3)]
        icnt = ar(2048).rearrange("p (g s) -> p g s", g=4)
        s_ic = [sem("s_ic"), 0]
        ic_tok = Y.dma(sp.dma_start, icnt, t["icnt"].rearrange("g s -> (g s)").partition_broadcast(128), s_ic)
        v = None
        for z in zp:
            v = V(dve.memset, z, 0.0, w=[v])
        zt = v
        ymt = {}
        cc = {}
        for m in range(4):
            q = tmp.take()
            b, r = proj("win", m, hT, w=[h_toks])
            a = A(act.activation, ym[:, m, :], b[0], ACT.Copy, w=[r])
            banks.give(b, a)
            ymt[m] = a
            tmp.give(q)
        for m in range(4):
            cc[m] = tmp.take()
            b, r = proj("win", 4 + m, hT)
            a = A(act.activation, cc[m][0], b[0], ACT.Copy, w=[r, cc[m][1]])
            banks.give(b, a)
            cc[m] = (cc[m], a)
        for m in range(4):
            b, r = proj("win", 8 + m, hT)
            z = zp[0]
            cs, a = cc[m]
            v = V(dve.tensor_tensor, z[:, 1:S + 1], b[0], cs[0], ALU.mult, w=[r, a, zt])
            banks.give(b, v)
            w3 = lambda i: col("conv_w2", m * 3 + i)
            v = V(dve.tensor_scalar, cs[0], z[:, 0:S], w3(0), None, ALU.mult, w=[v])
            v = V(dve.scalar_tensor_tensor, out=cs[0], in0=z[:, 1:S + 1], scalar=w3(1), in1=cs[0],
                  op0=ALU.mult, op1=ALU.add, w=[v])
            zt = v = V(dve.scalar_tensor_tensor, out=cs[0], in0=z[:, 2:S + 2], scalar=w3(2), in1=cs[0],
                       op0=ALU.mult, op1=ALU.add, w=[v])
            ymt[m] = V(dve.tensor_tensor, ym[:, m, :], ym[:, m, :], cs[0], ALU.mult, w=[v, ymt[m]])
            tmp.give(cs, ymt[m])
        xg = {}
        pl = []
        v = zt
        for g in range(4):
            w = 2 << g
            b, r = proj("win", 12 + g, hT, nxt=(g < 3))
            z, z2 = zp[1], zp[2]
            u = tmp.take()
            v = V(dve.tensor_copy, z[:, PADL:PADL + S], b[0], w=[r, v])
            a = A(act.activation, u[0], b[0], ACT.Copy, w=[v, u[1]])
            banks.give(b, v, a)
            src, dst, n = z, z2, 1
            while n < w:
                L = S + 2 * PADL
                v = V(dve.tensor_tensor, dst[:, n:L], src[:, n:L], src[:, 0:L - n], ALU.add, w=[v])
                v = V(dve.tensor_copy, dst[:, 0:n], src[:, 0:n], w=[v])
                src, dst, n = dst, src, 2 * n
            o = PADL + w // 2 - 1
            p = tmp.take()
            v = V(dve.tensor_tensor, p[0], src[:, o:o + S], icnt[:, g, :], ALU.mult, w=[v, ic_tok, p[1]])
            pt = V(dve.tensor_tensor, p[0], p[0], u[0], ALU.subtract, w=[v, a])
            tmp.give(u, pt)
            v = V(dve.memset, z, 0.0, w=[pt])
            v = V(dve.memset, z2, 0.0, w=[v])
            pl.append((p, pt))
        W, tok = unit("pool", 0)
        for g in range(4):
            p, pt = pl[g]
            b = banks.take()
            r = T(pe.matmul, b[0], W[:, g, :], p[0], start=True, stop=True, w=[tok, pt, b[1]])
            tmp.give(p, r)
            ymt[4 + g] = A(act.activation, ym[:, 4 + g, :], b[0], ACT.Copy, scale=col("pool_s", g), w=[r])
            banks.give(b, ymt[4 + g])
        load_next(r)
        h_toks = [split(ym[:, k, :], hT[:, 0, k, :], hT[:, 1, k, :], [r, ymt[k]]) for k in range(8)]
        for m in range(8):
            b, r = proj("wo", m, hT, w=[h_toks])
            v = residual(b, r, m)
        o = VOFF["g_ffn"][0]
        h_toks = norm_T(xT, hT, vec[:, o:o + 8], w=[v])
        ar.leave()

        ar0 = Phase(0)
        gT, rT = ar0(512), ar0(512)
        ixT = [ar0(512, BF16) for _ in range(5)]
        ar = Phase(4)
        ar.temps()
        ksb = ar(2048).rearrange("p (u k m) -> p u k m", u=2, k=8)
        s_ks = [sem("s_ks"), 0]
        ks_tok = Y.dma(sp.dma_start, ksb.rearrange("p u k m -> p u (k m)"), t["keys"].rearrange("u p n -> p u n"), s_ks)
        cand = ar(2048)
        sv_ = ar(1024).rearrange("p (b h k) -> p b h k", b=4, k=16)
        sx_ = ar(1024, U32).rearrange("p (b h k) -> p b h k", b=4, k=16)
        sxf = ar(256).rearrange("p (h k) -> p h k", k=16)
        tv = ar(128).rearrange("p (h k) -> p h k", k=16)
        px = ar(128, U32).rearrange("p (h k) -> p h k", k=16)
        ph = ar(128, U32)
        hif = ar(128)
        lof = ar(128)
        ijg = ar(384)
        io16 = ar(16)
        s16 = ar(256)
        io_tok = Y.dma(sp.dma_start, io16, t["iota16"].partition_broadcast(128), s_ic)
        v = None
        fin, gcand = [], []
        def top16(n, src, vals, idx, w):
            a, b = slice(0, 8), slice(8, 16)
            one = [V(dve.max, vals[:, i, a], src(i), w=w) for i in range(n)]
            for i in range(n):
                V(dve.max_index, idx[:, i, a], vals[:, i, a], src(i), w=[one[i]])
            one = [V(dve.match_replace, src(i), vals[:, i, a], src(i), -3e38, w=[V.last()] if not i else [])
                   for i in range(n)]
            one = [V(dve.max, vals[:, i, b], src(i), w=[one[i]]) for i in range(n)]
            for i in range(n):
                v = V(dve.max_index, idx[:, i, b], vals[:, i, b], src(i), w=[one[i]])
            return v

        for hp in range(16):
            b, r = proj("wq", hp, hT, w=[h_toks], nxt=(hp < 15))
            q = tmp.take()
            a = A(act.activation, q[0], b[0], ACT.Copy, w=[r, q[1]])
            banks.give(b, a)
            b = banks.take()
            T.wait(a, b[1], ks_tok)
            for blk in range(4):
                r = T(pe.matmul, b[0][:, blk * 128:(blk + 1) * 128], q[0][:, blk * 128:(blk + 1) * 128],
                      ksb[:, hp // 8, hp % 8, :], start=True, stop=True, inc=(blk == 3))
            tmp.give(q, r)
            x = tmp.take()
            a = A(act.activation, x[0], b[0], ACT.Copy, w=[r, x[1]])
            banks.give(b, a)
            v = top16(4, lambda i: x[0][:, i * 128:(i + 1) * 128], sv_[:, :, hp, :], sx_[:, :, hp, :], [a])
            tmp.give(x, v)
        st["ahead"] = 4
        for blk in range(4):
            sv, sx = sv_[:, blk, :, :], sx_[:, blk, :, :]
            v = V(dve.tensor_copy, sxf, sx, w=[v])
            sv4 = sv.rearrange("p (h two) k -> p h two k", two=2)
            sx4 = sxf.rearrange("p (h two) k -> p h two k", two=2)
            c4 = cand.rearrange("p (h a b) -> p h a b", h=8, a=16)
            for h in range(8):
                v = V(dve.tensor_tensor, c4[:, h, :, :],
                      sv4[:, h, 0, :].rearrange("p (a o) -> p a o", o=1).broadcast_to([128, 16, 16]),
                      sv4[:, h, 1:2, :].broadcast_to([128, 16, 16]), ALU.add, w=[gcand])
            v = top16(8, lambda i: cand[:, i * 256:(i + 1) * 256], tv, px, [v])
            pxf = px.rearrange("p h k -> p (h k)")
            v = V(dve.tensor_scalar, ph, pxf, 4, None, ALU.logical_shift_right, w=[v])
            v = V(dve.tensor_copy, hif, ph, w=[v])
            v = V(dve.tensor_scalar, ph, pxf, 15, None, ALU.bitwise_and, w=[v])
            v = V(dve.tensor_copy, lof, ph, w=[v])
            for half, src in ((0, hif), (1, lof)):
                oh = cand.rearrange("p (n a) -> p n a", a=16)
                v = V(dve.tensor_tensor, oh, src.rearrange("p (n o) -> p n o", o=1).broadcast_to([128, 128, 16]),
                      io16.rearrange("p (o a) -> p o a", o=1).broadcast_to([128, 128, 16]), ALU.is_equal,
                      w=[v, io_tok])
                oh4 = cand.rearrange("p (h k a) -> p h k a", h=8, k=16)
                v0 = v
                for h in range(8):
                    v = V(dve.tensor_tensor, oh4[:, h, :, :], oh4[:, h, :, :],
                          sx4[:, h, half:half + 1, :].broadcast_to([128, 16, 16]), ALU.mult, w=[v0])
                v = V(dve.tensor_reduce, ijg[:, half * 128:(half + 1) * 128], oh, AX.X, ALU.add, w=[v, fin])
            gt = ijg[:, 256:384].rearrange("p (h k) -> p h k", k=16)
            v = V(dve.tensor_tensor, gt, tv, tv[:, :, 0:1].broadcast_to([128, 8, 16]), ALU.subtract, w=[v])
            a = A(act.activation, gt, gt, ACT.Exp, w=[v])
            s8 = s16[:, 0:8]
            v = V(dve.tensor_reduce, s8, gt, AX.X, ALU.add, w=[a])
            v = V(dve.reciprocal, s8, s8, w=[v])
            v = V(dve.tensor_tensor, gt, gt, s8.rearrange("p (h o) -> p h o", o=1).broadcast_to([128, 8, 16]),
                  ALU.mult, w=[v])
            b = banks.take()
            T.wait(b[1], v)
            for i in range(3):
                r = T(pe.transpose, b[0][:, i * 128:(i + 1) * 128], ijg[:, i * 128:(i + 1) * 128], ident[:, :],
                      inc=(i == 2))
            fin = [r]
            for i, o in enumerate((ixT[0], ixT[1], gT)):
                a = A(act.activation, o[:, blk * 128:(blk + 1) * 128], b[0][:, i * 128:(i + 1) * 128],
                      ACT.Copy, w=[r])
            banks.give(b, a)
        v = V(dve.tensor_copy, ixT[2], gT, w=[a, v])
        v = V(dve.tensor_tensor, rT, gT, ixT[2], ALU.subtract, w=[v])
        v = V(dve.tensor_copy, ixT[3], rT, w=[v])
        v = V(dve.tensor_tensor, rT, rT, ixT[3], ALU.subtract, w=[v])
        split_tok = V(dve.tensor_copy, ixT[4], rT, w=[v])
        ar.leave()
        ar = Phase(0)
        TB = 16
        iom = ar(128 * TB, BF16).rearrange("p (n t) -> p n t", t=TB)
        s_io = [sem("s_io"), 0]
        io_tok = Y.dma(sp.dma_start, iom.rearrange("p n t -> p (n t)"), t["iom"].partition_broadcast(128), s_io)
        ohs = Slots([[ar(128 * TB, BF16).rearrange("p (n t) -> p n t", t=TB) for _ in range(5)] for _ in range(2)])
        stages = Slots([(ar(128 * TG), [sem(f"s_st{i}"), 0]) for i in range(2)])
        gd_toks = []

        def spread(ix, t0):
            return ix[:, t0:t0 + TB].rearrange("p (o t) -> p o t", o=1).broadcast_to([128, 128, TB])

        for blk in range(S // TG):
            stg = stages.take()
            sview = stg[0][0].rearrange("p (j t) -> p j t", t=TG)
            for tb in range(TG // TB):
                t0 = blk * TG + tb * TB
                o = ohs.take()
                oi, oj, g1, g2, g3 = o[0]
                V(dve.tensor_tensor, oi, iom, spread(ixT[0], t0), ALU.is_equal, w=[o[1], split_tok, io_tok])
                v = V(dve.tensor_tensor, oj, iom, spread(ixT[1], t0), ALU.is_equal)
                v1 = V(dve.tensor_tensor, g1, oj, spread(ixT[2], t0), ALU.mult, w=[v])
                V(dve.tensor_tensor, g2, oj, spread(ixT[3], t0), ALU.mult)
                v = V(dve.tensor_tensor, g3, oj, spread(ixT[4], t0), ALU.mult)
                T.wait(v)
                for t4 in range(TB // 4):
                    b = banks.take()
                    T.wait(b[1])
                    for q in range(4):
                        tk = t4 * 4 + q
                        for m, gm in enumerate((g1, g2, g3)):
                            r = T(pe.matmul, b[0][:, q * 128:(q + 1) * 128], oi[:, :, tk], gm[:, :, tk],
                                  start=(m == 0), stop=(m == 2), inc=(m == 2))
                    at_ = tb * TB + t4 * 4
                    e = A(act.activation, sview[:, :, at_:at_ + 4].rearrange("p j t -> p t j"),
                          b[0].rearrange("p (t j) -> p t j", t=4), ACT.Copy, w=[r, stg[1]])
                    banks.give(b, e)
                ohs.give(o, r)
            tk = Y.dma(sp.dma_start, t["gd"][:, blk, :, :].rearrange("c p n -> p c n"),
                       stg[0][0].rearrange("p (c n) -> p c n", n=JC * TG), stg[0][1], w=[e])
            gd_toks.append(tk)
            stages.give(stg, tk)
        ar.leave()
        ar0.leave(False)
        Y.wait(*gd_toks)
        ar = Phase(5)
        ar.temps()
        more = ar(5 * 2048, F32R).rearrange("p (i a n) -> p i a n", i=5, a=2)
        keep = wsl[0].free
        wsl[0].free = keep + [(more[:, i, :, :], []) for i in range(5)]
        NC = 128 // JC
        gch = [(ar(JC * S), [sem(f"s_g{i}"), 0]) for i in range(2)]
        agb = [ar(2 * JC * S, F32R).rearrange("p (a j s) -> p a j s", a=2, j=JC) for _ in range(2)]
        gfree = [[], []]
        afree = [[], []]
        gl = {}

        def load_g(c):
            g, sm_ = gch[c % 2]
            gl[c] = Y.dma(sp.dma_start, g.rearrange("p (b n) -> p b n", n=JC * TG),
                          t["gd"][c].rearrange("b p n -> p b n"), sm_, w=[gfree[c % 2]])

        load_g(0)
        load_g(1)
        ag_t = {}

        def z_part(c):
            g = gch[c % 2][0].rearrange("p (b j t) -> p j b t", j=JC, t=TG)
            toks = []
            for j in range(JC):
                b, r = proj("eu", c * JC + j, hT)
                x, y = tmp.take(), tmp.take()
                a = A(act.activation, x[0], b[0], ACT.Gelu_apprx_tanh, w=[r, x[1]])
                banks.give(b, a)
                v = V(dve.tensor_tensor, y[0].rearrange("p (b t) -> p b t", t=TG),
                      x[0].rearrange("p (b t) -> p b t", t=TG), g[:, j, :, :], ALU.mult, w=[a, gl[c], y[1]])
                tmp.give(x, v)
                hi, lo = agb[c % 2][:, 0, j, :], agb[c % 2][:, 1, j, :]
                a = A(act.activation, hi, y[0], ACT.Copy, w=[v, afree[c % 2]])
                p = G(pool.tensor_tensor, lo, y[0], hi.bitcast(F32), ALU.subtract, w=[a])
                tmp.give(y, p)
                toks.append(p)
                yield
            gfree[c % 2] = [v]
            ag_t[c] = toks

        def v_part(c):
            us_ = []
            for j in range(JC):
                us_.append(unit_hl("ev", c * JC + j, nxt=False))
            for dt in range(8):
                b = banks.take()
                T.wait(b[1])
                for j in range(JC):
                    T.wait(us_[j][2], ag_t[c][j])
                    W = us_[j][1]
                    r = mm3(b[0], (W[:, 0, dt, :], W[:, 1, dt, :]),
                            (agb[c % 2][:, 0, j, :], agb[c % 2][:, 1, j, :]),
                            first=(j == 0), last=(j == JC - 1), inc=(j == JC - 1))
                vv = residual(b, r, dt)
                if dt % 2 == 0 and c < NC - 1 and st["split"] < st["used"] + 4:
                    split_next()
            for j in range(JC):
                wsl[0].give(us_[j][0], r)
            afree[c % 2] = [r]
            return vv

        run((z_part(0), 4))
        for c in range(NC):
            if c + 1 < NC:
                run((z_part(c + 1), 4))
                if c + 2 < NC:
                    load_g(c + 2)
            vlast = v_part(c)

        st["ahead"] = 1
        o = VOFF["g_ple"][0]
        h_toks = norm_T(xT, hT, vec[:, o:o + 8], w=[vlast])
        ar.leave()
        ar = Phase(8)
        ar.temps()
        wsl[0].free = [x for x in wsl[0].free if x[0].tensor.name == "wsp"]
        gp = ar(4096).rearrange("p (k s) -> p k s", k=8)
        pT = ar(1024).rearrange("p (k s) -> p k s", k=2)
        p_tok = Y.dma(sp.dma_start, pT, t["pT"].rearrange("(k p) s -> p k s", p=128), s_ic)
        gp_t = []
        for m in range(8):
            b, r = proj("pleg", m, hT, w=[h_toks], nxt=(m < 7))
            gp_t.append(A(act.activation, gp[:, m, :], b[0], ACT.Sigmoid, w=[r]))
            banks.give(b, gp_t[-1])
        for u in range(2):
            W, tok = unit("plep", u)
            for i in range(4):
                m = 4 * u + i
                b = banks.take()
                T.wait(tok, b[1], p_tok)
                for k in range(2):
                    r = T(pe.matmul, b[0], W[:, 2 * i + k, :], pT[:, k, :], start=(k == 0), stop=(k == 1),
                          inc=(k == 1))
                v = V(dve.tensor_tensor, gp[:, m, :], b[0], gp[:, m, :], ALU.mult, w=[r, gp_t[m]])
                banks.give(b, v)
                v = V(dve.tensor_tensor, xT[:, m, :], xT[:, m, :], gp[:, m, :], ALU.add, w=[v])
            load_next(r)
        o = VOFF["g_final"][0]
        f_toks = norm_T(xT, None, vec[:, o:o + 8], w=[v])
        s_out = [sem("s_out"), 0]
        o_tok = Y.dma(sp.dma_start, t["out"].rearrange("(k p) s -> p k s", p=128), xT[:, :, :], s_out, w=f_toks)
        Y.wait(o_tok)
        assert st["used"] == len(order)

        ctx.callback(ar.ctx.close)
        block = ctx.enter_context(nc.Block())

        @block.sync
        def _(eng):
            Y.play(eng)

        @block.scalar
        def _(eng):
            A.play(eng)

        @block.vector
        def _(eng):
            V.play(eng)

        @block.gpsimd
        def _(eng):
            G.play(eng)

        @block.tensor
        def _(eng):
            T.play(eng)


def _cols(v):
    return np.ascontiguousarray(np.asarray(v).reshape(-1, 128).T)


def _units(w, starts=None):
    w = np.asarray(w)
    K, N = w.shape
    starts = range(0, N, 128) if starts is None else starts
    out = []
    for s in starts:
        for kh in range(0, K, 1024):
            out.append(w[kh:kh + 1024, s:s + 128].reshape(8, 128, 128).transpose(1, 0, 2).reshape(128, 1024))
    return np.ascontiguousarray(np.stack(out))


def _constants():
    i = np.arange(128)
    strict = (i[:, None] < i[None, :])
    incl = (i[:, None] <= i[None, :])
    m = np.concatenate([strict, incl], 1).astype(np.uint32)
    lvl = np.zeros((7, 128, 128), np.float32)
    for l in range(7):
        s = 1 << l
        lvl[l] = ((i[:, None] // s) % 2 == 1) & (i[None, :] // s == i[:, None] // s - 1)
    lvh = np.concatenate([lvl[l].reshape(128, -1, 2, 1 << l)[:, :, 0, :].reshape(128, 64) for l in range(1, 7)], 1)
    lvl = -lvl[0].T
    icnt = np.zeros((4, S), np.float32)
    tt = np.arange(S)
    for g, w in enumerate((2, 4, 8, 16)):
        icnt[g] = 1.0 / (np.clip(tt + w // 2, 0, S) - np.clip(tt - w // 2, 0, S))
    return {
        "ident": np.eye(128, dtype=np.float32), "ones": np.ones((128, 128), np.float32),
        "bones": np.kron(np.eye(2), np.ones((64, 64))).astype(np.float32),
        "msk": np.concatenate([m, m], 1), "lvl": np.ascontiguousarray(lvl), "lvh": np.ascontiguousarray(lvh), "icnt": icnt,
        "iota16": np.arange(16, dtype=np.float32),
    }


def kernel(x, c, positions, ada_w, ada_b, norm_g, final_g, even_w_in, even_w_out, conv_w, conv_vec,
           rwkv_mu_rkv, rwkv_mu_lora, rwkv_vec, rwkv_w_up, rwkv_a_up, rwkv_r_k, odd_w_in, odd_w_out,
           p_2, g_mix_2, w_in_2, conv_w_2, pool_w_2, pool_scale_2, w_o_2, g_ffn_2, w_q_2, sub_keys_2,
           expert_u_2, expert_v_2, g_ple_2, w_ple_gate_2, w_ple_proj_2, g_final_2):
    import ml_dtypes
    import concourse.bacc as bacc
    from concourse.bass_utils import run_bass_kernel_spmd

    a = np.asarray
    f = {}
    f.update(_constants())
    f["iom"] = np.repeat(np.arange(128), 16).astype(ml_dtypes.bfloat16)
    f["xT"] = np.ascontiguousarray(a(x)[0].T)
    f["positions"] = np.ascontiguousarray(a(positions)[0])
    f["pcol"] = np.ascontiguousarray(a(positions)[0].reshape(4, 128).T)
    q = np.arange(128)
    inv = lambda d: (np.float32(10000.0) ** (-np.arange(0, d, 2, dtype=np.float32) / np.float32(d))).astype(np.float32)
    v = {
        "c": _cols(c), "norm_g0": _cols(a(norm_g)[0]), "norm_g1": _cols(a(norm_g)[1]), "final_g": _cols(final_g),
        "ada_b0": _cols(a(ada_b)[0]), "ada_b1": _cols(a(ada_b)[1]),
        "conv_b": _cols(a(conv_vec)[0, 0]), "ln_w": _cols(a(conv_vec)[0, 1]), "ln_b": _cols(a(conv_vec)[0, 2]),
        "mu_r": _cols(a(rwkv_mu_rkv)[0, 0]), "mu_k": _cols(a(rwkv_mu_rkv)[0, 1]), "mu_v": _cols(a(rwkv_mu_rkv)[0, 2]),
        "mu_l": a(rwkv_mu_lora)[0].reshape(128, 1), "r_k": _cols(a(rwkv_r_k)[0]),
        "conv_w": a(conv_w)[0, :, 0, :].reshape(TAPS, 8, 128).transpose(2, 1, 0).reshape(128, 8 * TAPS),
        "g_mix": _cols(a(g_mix_2)[0]), "g_ffn": _cols(a(g_ffn_2)[0]), "g_ple": _cols(a(g_ple_2)[0]),
        "g_final": _cols(g_final_2), "pool_s": _cols(a(pool_scale_2)[0]),
        "conv_w2": a(conv_w_2)[0].reshape(3, 4, 128).transpose(2, 1, 0).reshape(128, 12),
        "inv128": inv(128)[q % 64][:, None], "inv64": inv(64)[q % 32][:, None],
        "sgn128": np.where(q % 128 < 64, 1.0, -1.0).astype(np.float32)[:, None],
        "sgn64": np.where(q % 64 < 32, 1.0, -1.0).astype(np.float32)[:, None],
    }
    for i, n in enumerate(("w0", "a0", "k_k", "k_a", "gn_w", "gn_b")):
        v[n] = _cols(a(rwkv_vec)[0, i])
    f["vec"] = np.ascontiguousarray(np.concatenate([v[n] for n, _ in VECS], 1))
    f["lup"] = np.ascontiguousarray(np.concatenate([a(rwkv_w_up)[0], a(rwkv_a_up)[0]], 0))
    f["ada"] = np.ascontiguousarray(
        a(ada_w).reshape(2, 4, 2, 128, 6, 512).transpose(0, 4, 1, 3, 2, 5)).reshape(48, 128, 1024)
    f["ein"] = _units(a(even_w_in)[0])
    f["eout"] = _units(a(even_w_out)[0])
    w = a(odd_w_in)[0]
    ki, wi = w[:, 2816:2880], w[:, 2880:2888]
    pad = np.zeros((D, 120), w.dtype)
    f["oin"] = _units(np.concatenate([w[:, 0:2816], ki, ki, wi, pad, w[:, 2888:]], 1))
    f["oout"] = _units(a(odd_w_out)[0])
    f["win"] = _units(a(w_in_2)[0])
    pw = a(pool_w_2)[0].transpose(1, 0, 2).reshape(128, 512)
    f["pool"] = np.ascontiguousarray(np.concatenate([pw, np.zeros_like(pw)], 1))[None]
    f["wo"] = _units(a(w_o_2)[0])
    f["wq"] = _units(a(w_q_2)[0])
    sk = a(sub_keys_2)[0].reshape(2, 8, 128, 128)
    f["keys"] = np.ascontiguousarray(sk.transpose(0, 3, 1, 2).reshape(2, 128, 1024))
    f["eu"] = np.ascontiguousarray(
        a(expert_u_2)[0].reshape(128, 128, 8, 128).transpose(1, 3, 2, 0)).reshape(128, 128, 1024)
    f["ev"] = np.ascontiguousarray(a(expert_v_2)[0]).reshape(128, 128, 1024)
    f["pleg"] = _units(a(w_ple_gate_2)[0])
    wp = a(w_ple_proj_2)[0].reshape(2, 128, 2, 4, 128)
    f["plep"] = np.ascontiguousarray(wp.transpose(2, 1, 3, 0, 4)).reshape(2, 128, 1024)
    f["pT"] = np.ascontiguousarray(a(p_2)[0, 0].T)

    nc = bacc.Bacc("TRN2", target_bir_lowering=False, num_devices=1)
    t = {k: nc.dram_tensor(f"in_{k}", list(z.shape), mybir.dt.from_np(z.dtype), kind="ExternalInput").ap()
         for k, z in f.items()}
    t["out"] = nc.dram_tensor("out_0", [D, S], F32, kind="ExternalOutput").ap()
    t["gd"] = nc.dram_tensor("gd", [128 // JC, S // TG, 128, JC * TG], F32, kind="Internal").ap()
    build(nc, t)
    r = run_bass_kernel_spmd(nc, [{f"in_{k}": z for k, z in f.items()}], core_ids=[0])
    return np.ascontiguousarray(r.results[0]["out_0"].T)[None]
```

```python
import itertools
import math
from contextlib import ExitStack

import numpy as np

import concourse.bass as bass
from concourse import mybir

ALU = mybir.AluOpType
ACT = mybir.ActivationFunctionType
AX = mybir.AxisListType
F32 = mybir.dt.float32
F32R = mybir.dt.float32r
BF16 = mybir.dt.bfloat16
U32 = mybir.dt.uint32
I32 = mybir.dt.int32

D = 1024
S = 512
KT = 8
CH = 4
JC = 4
TG = 64
RING = 3
UNSPLIT = [193, 474, 475, 484]
TAPS = 31
NPRE = 13
NTMP = 12
PATIENCE = 1.13e-4
NSP = 3
NUNITS = 48 + 57 + 16 + 40 + 16 + 16 + 1 + 8 + 16 + 256 + 8 + 2
TWO_PI = 2.0 * math.pi
MAGIC = 12582912.0
NEG = -1e30

VECS = [
    ("c", 8), ("norm_g0", 8), ("norm_g1", 8), ("final_g", 8), ("ada_b0", 24), ("ada_b1", 24),
    ("conv_b", 8), ("ln_w", 8), ("ln_b", 8), ("mu_r", 8), ("mu_k", 8), ("mu_v", 8), ("mu_l", 1),
    ("w0", 8), ("a0", 8), ("k_k", 8), ("k_a", 8), ("gn_w", 8), ("gn_b", 8), ("r_k", 8),
    ("conv_w", 8 * TAPS), ("g_mix", 8), ("g_ffn", 8), ("g_ple", 8), ("g_final", 8),
    ("pool_s", 4), ("conv_w2", 12), ("inv128", 1), ("inv64", 1), ("sgn128", 1), ("sgn64", 1),
]
VOFF = {}
_at = 0
for _n, _w in VECS:
    VOFF[_n] = (_at, _w)
    _at += _w
NVEC = _at


WHEN = {}
EST = {"latest": 0.0}


def _estimate(name, kind, a, k):
    out = k["out"] if "out" in k else a[0]
    n = 1
    for d in out.shape[1:]:
        n *= d
    if name == "s_pe":
        one = kind == "transpose" or a[1].dtype in (F32R, BF16)
        return n * 0.417 * (1 if one else 4)
    if name == "s_pool":
        return 100 + 2.2 * n
    if name == "s_act":
        return 150 + 0.9 * n
    return 60 + n * (6.3 if kind == "reciprocal" else 1.1)


class Eng:

    def __init__(self, sem):
        self.sem, self.n, self.q, self.seen = sem, 0, [], {}
        self.t = 0.0

    def wait(self, *toks):
        for t in toks:
            if t is None or not t:
                continue
            if isinstance(t, list):
                self.wait(*t)
                continue
            k, (sem, v) = t[0].name, t
            self.t = max(self.t, WHEN.get((k, v), 0.0))
            if self.seen.get(k, 0) < v:
                self.seen[k] = v
                self.q.append((sem, v))

    def __call__(self, f, *a, w=(), inc=True, **k):
        self.wait(*w)
        self.q.append((f, a, k, (self.sem, 1) if inc else None))
        self.t += _estimate(self.sem.name, f.__name__, a, k)
        if inc:
            self.n += 1
            WHEN[(self.sem.name, self.n)] = self.t + 100
            EST["latest"] = max(EST["latest"], self.t + 100)
        return (self.sem, self.n)

    def dma(self, f, dst, src, sem, w=()):
        self.wait(*w)
        self.q.append((f, (dst, src), {}, (sem[0], 16)))
        sem[1] += 16
        WHEN[(sem[0].name, sem[1])] = self.t + 4000
        return (sem[0], sem[1])

    def last(self):
        return (self.sem, self.n)

    def play(self, eng):
        for x in self.q:
            if len(x) == 2:
                eng.wait_ge(x[0], x[1])
            else:
                f, a, k, inc = x
                if "unit" in k:
                    a, k = (a[0], a[1](k["unit"])), {}
                ins = f(*a, **k)
                if inc is not None:
                    ins.then_inc(inc[0], inc[1])


class Slots:

    def __init__(self, aps):
        self.free = [(ap, []) for ap in aps]

    def take(self):
        assert self.free, "no free slot"
        return self.free.pop(0)

    def give(self, slot, *toks):
        self.free.append((slot[0], list(toks)))


def build(nc, t):
    order = []
    with ExitStack() as ctx:
        def sb(name, shape, dt=F32):
            return ctx.enter_context(nc.sbuf_tensor(name, shape, dt))

        def sem(name):
            return ctx.enter_context(nc.semaphore(name))

        V, A, G, T, Y = (Eng(sem(n)) for n in ("s_dve", "s_act", "s_pool", "s_pe", "s_sp"))
        dve, act, pool, pe, sp = nc.vector, nc.scalar, nc.gpsimd, nc.tensor, nc.sync

        banks = Slots([ctx.enter_context(nc.psum_tensor(f"ps{i}", [128, 512], F32))[:, :]
                       for i in range(8)])
        xT = sb("xT", [128, KT, S])
        hT = sb("hT", [128, 2, KT, S], F32R)
        wsp = sb("wsp", [128, NSP, 2, 1024], F32R)
        wsl = [Slots([wsp[:, i, :, :] for i in range(NSP)])]
        ringt = sb("ring", [128, RING, 1024])
        vec = sb("vec", [128, NVEC])
        mod = sb("mod", [128, 2, 24])
        cond = sb("cond", [128, 8])
        gsc = sb("gsc", [128, 2, 8])
        omka = sb("omka", [128, 8])
        ident = sb("ident", [128, 128])
        ones = sb("ones", [128, 128])
        bones = sb("bones", [128, 128])
        small = sb("small", [128, 8, 64])
        msum = sb("msum", [128, 512])
        tmp = Slots([])

        def col(name, m=0):
            return vec[:, VOFF[name][0] + m:VOFF[name][0] + m + 1]

        class Phase:

            count = 0

            def __init__(self, ntmp):
                Phase.count += 1
                self.ctx, self.id, self.n, self.ntmp = ExitStack(), Phase.count, 0, ntmp

            def __call__(self, n, dt=F32):
                self.n += 1
                nm = f"p{self.id}_{self.n}"
                return self.ctx.enter_context(nc.sbuf_tensor(nm, [128, n], dt))[:, :]

            def temps(self):
                tmp.free = [(self(512), []) for _ in range(self.ntmp)]

            def leave(self, quiet=True):
                if quiet:
                    fence()
                self.ctx.close()

        def fence():
            toks = [e.last() for e in (V, A, G, T)]
            for e in (V, A, G, T, Y):
                e.wait(*toks)

        s_const = [sem("s_const"), 0]
        c_tok = Y.dma(sp.dma_start, vec[:, :], t["vec"][:, :], s_const)
        c_tok = Y.dma(sp.dma_start, ident[:, :], t["ident"][:, :], s_const)
        c_tok = Y.dma(sp.dma_start, ones[:, :], t["ones"][:, :], s_const)
        c_tok = Y.dma(sp.dma_start, bones[:, :], t["bones"][:, :], s_const)
        s_x = [sem("s_x"), 0]
        ring_sem = [[sem(f"s_w{i}"), 0] for i in range(RING)]
        st = {"loaded": 0, "used": 0, "split": 0, "hl": {}, "tok": {}, "ahead": 1, "pool": False}

        def source(n):
            name, u = order[n]
            return t[name][:, u, :] if name == "ev" else t[name][u]

        def load_next(*w):
            n = st["loaded"]
            if n >= NUNITS:
                return
            slot = n % RING
            Y.wait(*w)
            s_, v_ = ring_sem[slot]
            Y.q.append((sp.dma_start, (ringt[:, slot, :], source), {"unit": n}, (s_, 16)))
            ring_sem[slot][1] += 16
            st["tok"][n] = (s_, v_ + 16)
            WHEN[(s_, v_ + 16)] = Y.t + 4000
            st["loaded"] += 1

        for _ in range(RING):
            load_next()
        x_tok = Y.dma(sp.dma_start, xT[:, :, :], t["xT"].rearrange("(k p) s -> p k s", p=128), s_x)

        def unit(name, u):
            n = st["used"]
            assert n == st["split"], "split ahead"
            order.append((name, u))
            st["used"] += 1
            st["split"] += 1
            return ringt[:, n % RING, :].rearrange("p (k m) -> p k m", m=128), st["tok"][n]

        def split_next():
            n = st["split"]
            if n >= NUNITS:
                return
            hl = wsl[0].take()
            raw = ringt[:, n % RING, :]
            a = A(act.activation, hl[0][:, 0, :], raw, ACT.Copy, w=[st["tok"][n], hl[1]])
            E, e = (G, pool) if st["pool"] else (V, dve)
            v = E(e.tensor_tensor, hl[0][:, 1, :], raw, hl[0][:, 0, :].bitcast(F32), ALU.subtract, w=[a])
            load_next(a, v)
            st["hl"][n] = (hl, v)
            st["split"] += 1

        def unit_hl(name, u, nxt=True):
            n = st["used"]
            if st["split"] == n:
                split_next()
            order.append((name, u))
            st["used"] += 1
            while nxt and st["split"] <= n + st["ahead"] and st["split"] not in UNSPLIT:
                split_next()
            hl, v = st["hl"].pop(n)
            return hl, hl[0].rearrange("p a (k m) -> p a k m", m=128), v

        def mm3(out, W, R, first=True, last=True, inc=True):
            T(pe.matmul, out, W[0], R[0], start=first, stop=False, inc=False)
            T(pe.matmul, out, W[0], R[1], start=False, stop=False, inc=False)
            return T(pe.matmul, out, W[1], R[0], start=False, stop=last, inc=inc)

        def split(src, hi, lo, w):
            a = A(act.activation, hi, src, ACT.Copy, w=w)
            return V(dve.tensor_tensor, lo, src, hi.bitcast(F32), ALU.subtract, w=[a])

        def proj_steps(name, u, rhs, out):
            while len(wsl[0].free) < 1 + (st["split"] == st["used"]):
                yield "blocked"
            hl, W, tok = unit_hl(name, u)
            b = banks.take()
            T.wait(tok, b[1])
            for k in range(8):
                r = mm3(b[0], (W[:, 0, k, :], W[:, 1, k, :]), (rhs[:, 0, k, :], rhs[:, 1, k, :]),
                        first=(k == 0), last=(k == 7), inc=(k == 7))
                if k in (1, 3, 5):
                    yield
            wsl[0].give(hl, r)
            out[:] = [b, r]

        def proj(name, u, rhs, w=(), first=True, last=True, bank=None, nxt=True, wk=None):
            hl, W, tok = unit_hl(name, u, nxt)
            b = bank or banks.take()
            T.wait(tok, *w, *([b[1]] if first else []))
            for k in range(8):
                if wk:
                    T.wait(wk[k])
                r = mm3(b[0], (W[:, 0, k, :], W[:, 1, k, :]), (rhs[:, 0, k, :], rhs[:, 1, k, :]),
                        first=first and k == 0, last=last and k == 7, inc=(k == 7))
            wsl[0].give(hl, r)
            return b, r

        def rsqrt(ap, w):
            a = A(act.activation, ap, ap, ACT.Sqrt, w=[w])
            return V(dve.reciprocal, ap, ap, w=[a])

        def norm_stat(src, w):
            b = banks.take()
            for k in range(KT):
                q = tmp.take()
                a = A(act.activation, q[0], src[:, k, :], ACT.Square, w=[w[k], q[1]])
                r = T(pe.matmul, b[0], ones[:, :], q[0], start=(k == 0), stop=(k == 7), w=[a, b[1], c_tok])
                tmp.give(q, r)
            m = msum[:, :]
            v = V(dve.tensor_scalar, m, b[0], 1.0 / D, 1e-6, ALU.mult, ALU.add, w=[r])
            banks.give(b, v)
            return m, rsqrt(m, v)

        def norm_T(src, dst, g, shift=None, w=(), stat=None):
            m, v = stat or norm_stat(src, w)
            h_free = T.last()
            toks, late = [], []
            if dst is None:
                for k in range(KT):
                    toks.append(V(dve.scalar_tensor_tensor, out=src[:, k, :], in0=src[:, k, :],
                                  scalar=g[:, k:k + 1], in1=m, op0=ALU.mult, op1=ALU.mult, w=[v, w[k]]))
                return toks

            def low(k, x, a):
                if shift is None:
                    E, e = (G, pool) if k % 2 else (V, dve)
                    v2 = E(e.tensor_tensor, dst[:, 1, k, :], x[0], dst[:, 0, k, :].bitcast(F32),
                           ALU.subtract, w=[a])
                else:
                    v2 = V(dve.scalar_tensor_tensor, out=dst[:, 1, k, :], in0=x[0], scalar=shift[:, k:k + 1],
                           in1=dst[:, 0, k, :].bitcast(F32), op0=ALU.add, op1=ALU.subtract, w=[a])
                tmp.give(x, v2)
                toks.append(v2)

            for k in range(KT):
                x = tmp.take()
                v2 = V(dve.scalar_tensor_tensor, out=x[0], in0=src[:, k, :], scalar=g[:, k:k + 1],
                       in1=m, op0=ALU.mult, op1=ALU.mult, w=[v, w[k] if w else None, x[1]])
                if shift is None:
                    a = A(act.activation, dst[:, 0, k, :], x[0], ACT.Copy, w=[v2, h_free])
                else:
                    a = A(act.activation, dst[:, 0, k, :], x[0], ACT.Identity, bias=shift[:, k:k + 1],
                          w=[v2, h_free])
                late.append((k, x, a))
                if k >= 2:
                    low(*late.pop(0))
            for z in late:
                low(*z)
            return toks

        def split_all(src, w, free, dst=hT):
            a = [A(act.activation, dst[:, 0, k, :], src[:, k, :], ACT.Copy, w=[w[k], free]) for k in range(8)]
            return [V(dve.tensor_tensor, dst[:, 1, k, :], src[:, k, :], dst[:, 0, k, :].bitcast(F32), ALU.subtract,
                      w=[a[k]]) for k in range(8)]

        def residual(b, r, m, gate=None):
            if gate is None:
                v = V(dve.tensor_tensor, xT[:, m, :], b[0], xT[:, m, :], ALU.add, w=[r])
            else:
                v = V(dve.scalar_tensor_tensor, out=xT[:, m, :], in0=b[0], scalar=gate,
                      in1=xT[:, m, :], op0=ALU.mult, op1=ALU.add, w=[r])
            banks.give(b, v)
            return v

        mod_toks = {0: [], 1: []}

        def mod_part(l, g):
            b = banks.take()
            T.wait(cond_tok, b[1])
            for kp in range(4):
                hl, _, tok = unit_hl("ada", 24 * l + 4 * g + kp, nxt=False)
                W = hl[0].rearrange("p a (i n) -> p a i n", i=2)
                T.wait(tok)
                for i in range(2):
                    k = 2 * kp + i
                    r = mm3(b[0][0:1, :], (condh[:, 0, k:k + 1], condh[:, 1, k:k + 1]), (W[:, 0, i, :], W[:, 1, i, :]),
                            first=(k == 0), last=(k == 7), inc=(i == 1))
                wsl[0].give(hl, r)
                if st["split"] == st["used"] and st["split"] not in UNSPLIT:
                    split_next()
                if kp < 3:
                    yield
            row = tmp.take()
            a = A(act.activation, row[0][0:1, :], b[0][0:1, :], ACT.Copy, w=[r, row[1]])
            banks.give(b, a)
            b = banks.take()
            T.wait(a, b[1])
            for i in range(4):
                r = T(pe.matmul, b[0][:, i:i + 1], row[0][0:1, i * 128:(i + 1) * 128], ones[0:1, 0:1],
                      start=True, stop=True, inc=(i == 3))
            tmp.give(row, r)
            o = VOFF[f"ada_b{l}"][0] + 4 * g
            v = V(dve.tensor_tensor, mod[:, l, 4 * g:4 * g + 4], b[0][:, 0:4], vec[:, o:o + 4], ALU.add,
                  w=[r, c_tok])
            banks.give(b, v)
            if g == 3:
                o = VOFF[f"norm_g{l}"][0]
                v = V(dve.scalar_tensor_tensor, out=gsc[:, l, :], in0=mod[:, l, 8:16], scalar=1.0,
                      in1=vec[:, o:o + 8], op0=ALU.add, op1=ALU.mult, w=[v])
            mod_toks[l].append(v)
            yield

        cond_tok = A(act.activation, cond[:, :], vec[:, 0:8], ACT.Silu, w=[c_tok])
        condh = sb("condh", [128, 2, 8], F32R)
        a = A(act.activation, condh[:, 0, :], cond[:, :], ACT.Copy, w=[cond_tok])
        cond_tok = V(dve.tensor_tensor, condh[:, 1, :], cond[:, :], condh[:, 0, :].bitcast(F32), ALU.subtract,
                     w=[a])
        oka = VOFF["k_a"][0]
        V(dve.tensor_scalar, omka[:, :], vec[:, oka:oka + 8], -1.0, 1.0, ALU.mult, ALU.add, w=[c_tok])

        ar = Phase(11)
        ar.temps()
        for _ in mod_part(0, 0):
            pass
        stat = norm_stat(xT, [x_tok] * 8)
        for g in range(1, 4):
            for _ in mod_part(0, g):
                pass
        h_toks = norm_T(xT, hT, gsc[:, 0, :], mod[:, 0, 0:8], w=[mod_toks[0]] * 8, stat=stat)

        us = Slots([ar(S + TAPS - 1) for _ in range(2)])
        zs = Slots([ar(S + 1) for _ in range(2)])
        ycs = Slots([(ar(512), [sem(f"s_yc{i}"), 0]) for i in range(2)])
        wl = ar(512)
        lup = ar(1024)
        msk = ar(512, mybir.dt.uint8)
        lvl = ar(128).rearrange("p (l n) -> p l n", l=1)
        lvh = ar(6 * 64).rearrange("p (l n) -> p l n", l=6)
        PP = ar(CH * 129).rearrange("p (c n) -> p c n", c=CH)
        d1 = ar(512)

        def chunked(ap):
            return ap.rearrange("p (c n) -> p c n", c=CH)

        Bes, Khs = Slots([ar(512)]), Slots([ar(512)])
        bons = Slots([ar(512) for _ in range(3)])
        sets = Slots([{"KR": ar(1024).rearrange("p (c a n) -> p c a n", c=CH, a=2), "dd": ar(CH),
                       "Vt": chunked(ar(512)), "Bt": chunked(ar(512)), "Kt": chunked(ar(512))}
                      for _ in range(3)])
        xf = xT[:, :, :].rearrange("p k s -> p (k s)")
        abk = [ar(4096), xf]
        mats = Slots([tuple(z[:, i * 2048:(i + 1) * 2048].rearrange("p (e c a n) -> p e c a n", e=2, c=CH, a=2)
                            for i in range(2)) + (ar(1024).rearrange("p (e c n) -> p e c n", e=2, c=CH),)
                      for z in abk])
        X = ar(1024).rearrange("p (e c n) -> p e c n", e=2, c=CH)
        p1 = msum[:, :]
        P1 = p1.rearrange("p (e c n) -> p e c n", e=2, c=CH)
        Sbd, Su, x1n, SA = (small[:, 2 * i:2 * i + 2, :].rearrange("p a n -> p (a n)") for i in range(4))
        s_rc = [sem("s_rc"), 0]
        Y.dma(sp.dma_start, lup, t["lup"][:, :], s_rc)
        Y.dma(sp.dma_start, lvh.rearrange("p l n -> p (l n)"), t["lvh"][:, :], s_rc)
        Y.dma(sp.dma_start, lvl.rearrange("p l n -> p (l n)"), t["lvl"][:, :], s_rc)
        rc_tok = Y.dma(sp.dma_start, p1.bitcast(U32), t["msk"][:, :], s_rc, w=[h_toks])
        msk_tok = V(dve.tensor_copy, msk, p1.bitcast(U32), w=[rc_tok])
        V(dve.memset, abk[0], 0.0)
        V(dve.memset, abk[1], 0.0, w=[h_toks])
        z0 = ([V(dve.memset, d1, 0.0)] + [V(dve.memset, z[0][:, 0:1], 0.0) for z in zs.free]
              + [V(dve.memset, u[0][:, 0:TAPS - 1], 0.0) for u in us.free])
        y_toks = []

        def conv_in(m, out):
            o = []
            yield from proj_steps("ein", m, hT, o)
            bv, rv = o
            yield
            yield from proj_steps("ein", 8 + m, hT, o)
            bg, rg = o
            s = tmp.take()
            a = A(act.activation, s[0], bg[0], ACT.Sigmoid, w=[rg, s[1]])
            banks.give(bg, a)
            u = us.take()
            v = V(dve.tensor_tensor, u[0][:, TAPS - 1:], bv[0], s[0], ALU.mult, w=[rv, a, u[1], z0])
            banks.give(bv, v)
            tmp.give(s, v)
            out[m] = (u, v)

        def conv(m, inp):
            u, v = inp[m]
            ys = ycs.take()
            yt = ys[0][0]
            cw = lambda k: col("conv_w", m * TAPS + k)
            v = V(dve.tensor_scalar, yt, u[0][:, 0:S], cw(0), col("conv_b", m),
                  ALU.mult, ALU.add, w=[v, ys[1]])
            for k in range(1, TAPS):
                v = V(dve.scalar_tensor_tensor, out=yt, in0=u[0][:, k:k + S], scalar=cw(k),
                      in1=yt, op0=ALU.mult, op1=ALU.add, w=[v])
                yield
            us.give(u, v)
            tk = Y.dma(sp.dma_start, t["yd"][m], yt, ys[0][1], w=[v])
            ycs.give(ys, tk)
            y_toks.append(tk)

        def shifted(name, u, mu_col, out, res, w=()):
            o = []
            yield from proj_steps(name, u, hT, o)
            b, r = o
            z = zs.take()
            a = A(act.activation, z[0][:, 1:], b[0], ACT.Copy, w=[r, z[1], z0])
            banks.give(b, a)
            d = tmp.take()
            g = G(pool.tensor_tensor, d[0], z[0][:, 0:S], z[0][:, 1:], ALU.subtract, w=[a, d[1]])
            v = V(dve.scalar_tensor_tensor, out=out, in0=d[0], scalar=mu_col, in1=z[0][:, 1:],
                  op0=ALU.mult, op1=ALU.add, w=[g, w])
            tmp.give(d, v)
            zs.give(z, v)
            res.append(v)

        T.wait(h_toks)
        res = []
        for _ in shifted("ein", 48, col("mu_l"), wl, res):
            pass
        v = res[0]
        wl_tok = A(act.activation, wl[0:64, :], wl[0:64, :], ACT.Tanh, w=[v])

        def prep(c, out):
            s = sets.take()
            d = s[0]
            out["s"] = s
            sw = s[1]
            k = tmp.take()
            r_ = tmp.take()
            v_ = tmp.take()
            res = []
            yield from shifted("ein", 24 + c, col("mu_r", c), r_[0], res, w=[r_[1]])
            tr = res[0]
            yield
            res = []
            yield from shifted("ein", 32 + c, col("mu_k", c), k[0], res, w=[k[1]])
            tk = res[0]
            yield
            res = []
            yield from shifted("ein", 40 + c, col("mu_v", c), v_[0], res, w=[v_[1]])
            tv = res[0]
            yield
            b1 = banks.take()
            r1 = T(pe.matmul, b1[0], lup[0:64, c * 128:(c + 1) * 128], wl[0:64, :], start=True, stop=True,
                   w=[b1[1], wl_tok, rc_tok])
            b2 = banks.take()
            r2 = T(pe.matmul, b2[0], lup[64:128, c * 128:(c + 1) * 128], wl[64:128, :], start=True, stop=True,
                   w=[b2[1]])
            wd = tmp.take()
            aa = tmp.take()
            a = A(act.activation, wd[0], b1[0], ACT.Sigmoid, bias=col("w0", c), w=[r1, wd[1]])
            banks.give(b1, a)
            ta = A(act.activation, aa[0], b2[0], ACT.Sigmoid, bias=col("a0", c), w=[r2, aa[1]])
            banks.give(b2, ta)
            sq = tmp.take()
            a2 = A(act.activation, sq[0], k[0], ACT.Square, scale=col("k_k", c), w=[tk, sq[1]])
            b = banks.take()
            r = T(pe.matmul, b[0], bones[:, :], sq[0], start=True, stop=True, w=[a2, b[1]])
            tw = A(act.activation, wd[0], wd[0], ACT.Exp, scale=-math.exp(-0.5), w=[a])
            yield
            v = V(dve.tensor_scalar, sq[0], b[0], 1e-24, None, ALU.max, w=[r])
            banks.give(b, v)
            vr = A(act.activation, sq[0], sq[0], ACT.Sqrt, w=[v])
            for i in range(CH):
                v = V(dve.reciprocal, chunked(sq[0])[:, i, :], chunked(sq[0])[:, i, :], w=[vr])
                yield
            kk = tmp.take()
            v = V(dve.scalar_tensor_tensor, out=kk[0], in0=k[0], scalar=col("k_k", c), in1=sq[0],
                  op0=ALU.mult, op1=ALU.mult, w=[v, kk[1]])
            tmp.give(sq, v)
            tkk = v
            k2 = tmp.take()
            v = V(dve.tensor_scalar, k2[0], aa[0], col("k_a", c), omka[:, c:c + 1], ALU.mult, ALU.add,
                  w=[ta, k2[1]])
            tk2 = V(dve.tensor_tensor, k2[0], k2[0], k[0], ALU.mult, w=[v])
            tmp.give(k, tk2)
            tb = G(pool.tensor_tensor, aa[0], aa[0], kk[0], ALU.mult, w=[tkk, v])
            yield
            w4 = wd[0].rearrange("p (c n) -> p c n", c=CH)
            v = V(dve.tensor_copy, d1.rearrange("p (c n) -> p c n", c=CH)[:, :, 0:1], w4[:, :, 0:1], w=[tw, z0])
            v = V(dve.memset, w4[:, :, 0:1], 0.0, w=[v])
            pw = tmp.take()
            v = V(dve.tensor_tensor_scan, pw[0], wd[0], d1, 0.0, ALU.mult, ALU.add, w=[v, pw[1]])
            tmp.give(wd, v)
            p4 = pw[0].rearrange("p (c n) -> p c n", c=CH)
            v2 = V(dve.reciprocal, PP[:, :, 0:1], p4[:, :, 63:64], w=[v])
            v = V(dve.tensor_tensor, PP[:, :, 1:129], p4, PP[:, :, 0:1].broadcast_to([128, CH, 128]), ALU.mult,
                  w=[v2])
            vd = V(dve.tensor_tensor, d["dd"][:, 0:3], PP[:, 0:3, 128:129].rearrange("p c n -> p (c n)"),
                   p4[:, 1:4, 63:64].rearrange("p c n -> p (c n)"), ALU.mult, w=[v, sw])
            pi4 = pw[0].rearrange("p (c n) -> p c n", c=CH)
            for q in range(CH):
                vi = V(dve.reciprocal, pi4[:, q, :], PP[:, q, 1:129], w=[vd])
                yield
            KR = d["KR"]
            f4 = lambda ap: ap.rearrange("p (c n) -> p c n", c=CH)
            g1 = G(pool.tensor_tensor, KR[:, :, 0, :], f4(kk[0]), PP[:, :, 0:128], ALU.mult, w=[v, tkk, sw])
            g2 = V(dve.tensor_tensor, KR[:, :, 1, :], f4(r_[0]), PP[:, :, 1:129], ALU.mult, w=[v, tr, sw])
            tmp.give(kk, g1)
            out["PPfree"] = [g1, g2]
            V.wait(g1)
            Be, Kh, bon = Bes.take(), Khs.take(), bons.take()
            out["b"] = (Be, Kh, bon)
            vB = V(dve.tensor_tensor, Be[0], aa[0], pw[0], ALU.mult, w=[tb, vi, Be[1]])
            vK = V(dve.tensor_tensor, Kh[0], k2[0], pw[0], ALU.mult, w=[tk2, vi, Kh[1]])
            tmp.give(aa, vB)
            tmp.give(pw, vK)
            v = V(dve.scalar_tensor_tensor, out=r_[0], in0=r_[0], scalar=col("r_k", c), in1=k2[0],
                  op0=ALU.mult, op1=ALU.mult, w=[g2])
            tmp.give(k2, v)
            b = banks.take()
            r = T(pe.matmul, b[0], bones[:, :], r_[0], start=True, stop=True, w=[v, b[1]])
            yield
            tmp.give(r_, r)
            vb = V(dve.tensor_tensor, bon[0], b[0], v_[0], ALU.mult, w=[r, tv, bon[1]])
            banks.give(b, vb)
            tt = []
            for src, dst, tk_ in ((v_[0], "Vt", tv), (Be[0], "Bt", vB), (Kh[0], "Kt", vK)):
                b = banks.take()
                T.wait(tk_, b[1])
                for q in range(CH):
                    r = T(pe.transpose, b[0][:, q * 128:(q + 1) * 128], src[:, q * 128:(q + 1) * 128],
                          ident[:, :], inc=(q == 3))
                a = A(act.activation, d[dst].rearrange("p c n -> p (c n)"), b[0], ACT.Copy, w=[r, sw])
                banks.give(b, a)
                if dst == "Vt":
                    tmp.give(v_, r, vb)
                tt.append(a)
                yield
            out["tok"] = [g1, g2, vB, vK, vd] + tt
            out["bon"] = vb

        st2 = {"y": [rc_tok]}

        def invert(c, inp):
            d = inp["s"][0]
            KR = d["KR"]
            sBe, sKh, bon = inp["b"]
            Be, Kh = sBe[0], sKh[0]
            mt = inp["m"] = mats.take()
            AB, AK, XT = mt[0]
            free = mt[1]
            T.wait(inp["tok"])
            ev = []
            for e in range(2):
                p = slice(64 * e, 64 * e + 64)
                for dst, lhs in ((AB, Be), (AK, Kh)):
                    for cc in range(0, CH, 2):
                        b = banks.take()
                        T.wait(b[1])
                        for q in range(2):
                            r = T(pe.matmul, b[0][:, q * 256:(q + 1) * 256],
                                  lhs[p, (cc + q) * 128:(cc + q + 1) * 128],
                                  KR[p, cc + q, :, :].rearrange("p a n -> p (a n)"),
                                  start=True, stop=True, inc=(q == 1))
                        v = V(dve.copy_predicated, dst[:, e, cc:cc + 2, :, :].rearrange("p c a n -> p (c a n)"),
                              msk, b[0], w=[r, msk_tok, free])
                        banks.give(b, v)
                        ev.append(v)
                    yield
            Bes.give(sBe, r)
            Khs.give(sKh, r)
            toks = {}

            def turn(e, w):
                b = banks.take()
                T.wait(b[1], w)
                for q in range(CH):
                    r = T(pe.transpose, b[0][:, q * 128:(q + 1) * 128], src[:, e, q, :], ident[:, :], inc=(q == 3))
                a = A(act.activation, dst[:, e, :, :].rearrange("p c n -> p (c n)"), b[0], ACT.Copy, w=[r])
                banks.give(b, a)
                return a

            src, dst = XT, X
            for e in range(2):
                g = G(pool.tensor_tensor, XT[:, e, :, :], AB[:, e, :, 0, :],
                      lvl[:, 0:1, :].broadcast_to([128, CH, 128]), ALU.mult, w=[ev, free])
                g = G(pool.tensor_tensor, XT[:, e, :, :], XT[:, e, :, :],
                      ident[:, :].rearrange("p (o n) -> p o n", o=1).broadcast_to([128, CH, 128]), ALU.add, w=[g])
                toks[e] = g
            yield
            for e in range(2):
                toks[e] = [toks[e], turn(e, toks[e])]
            yield
            src, dst = X, XT
            for l in range(1, 7):
                n = 1 << l
                even = lambda ap: ap.rearrange("p c (b two s) -> p c b two s", two=2, s=n)[:, :, :, 0, :]
                p1 = {}
                for e in range(2):
                    b = banks.take()
                    T.wait(b[1], toks[e], ev)
                    for q in range(CH):
                        r = T(pe.matmul, b[0][:, q * 64:(q + 1) * 64], AB[:, e, q, 0, :],
                              even(X[:, e, q:q + 1, :]).rearrange("p o b s -> p (o b) s"),
                              start=True, stop=True, inc=(q == 3))
                    v = V(dve.tensor_tensor, P1[:, e, :, :], b[0][:, 0:256].rearrange("p (c n) -> p c n", c=CH),
                          lvh[:, l - 1:l, :].broadcast_to([128, CH, 64]), ALU.mult, w=[r])
                    banks.give(b, v)
                    p1[e] = v
                yield
                for e in range(2):
                    b = banks.take()
                    T.wait(b[1], p1[e])
                    for q in range(CH):
                        r = T(pe.matmul, b[0][:, q * 64:(q + 1) * 64], XT[:, e, q, :], P1[:, e, q, :],
                              start=True, stop=True, inc=(q == 3))
                    for q in range(CH):
                        xe = even(X[:, e, q:q + 1, :]).rearrange("p o b s -> p (o b) s")
                        v = V(dve.tensor_tensor, xe, xe,
                              b[0][:, q * 64:(q + 1) * 64].rearrange("p (b s) -> p b s", s=n), ALU.subtract, w=[r])
                    banks.give(b, v)
                    p1[e] = v
                yield
                for e in range(2):
                    toks[e] = [turn(e, p1[e])]
                yield
            inp["inv"] = [toks, ev]

        def solve(c, inp):
            s = inp["s"]
            d = s[0]
            KR = d["KR"]
            bon = inp["b"][2]
            AB, AK, XT = inp["m"][0]
            toks, ev = inp["inv"]
            T.wait(ev)
            ts = V(dve.memset, Sbd, 0.0, w=[st2["y"]])
            by = banks.take()
            T.wait(by[1])
            for q in range(CH):
                b = banks.take()
                T.wait(b[1], ts, toks[0], toks[1])
                for e in range(2):
                    xe = b[0][:, 64 * e:64 * e + 64]
                    T(pe.matmul, xe, KR[:, q, 0, :], Sbd[:, 64 * e:64 * e + 64], start=True, stop=False, inc=False)
                    r = T(pe.matmul, xe, AK[:, e, q, 0, :], d["Vt"][:, q, 64 * e:64 * e + 64],
                          start=False, stop=True, inc=(e == 1))
                a = A(act.activation, x1n, b[0][:, 0:128], ACT.Copy, scale=-1.0, w=[r, st2["y"]])
                banks.give(b, a)
                yield
                b = banks.take()
                T.wait(b[1], a)
                for e in range(2):
                    r = T(pe.matmul, b[0][:, 64 * e:64 * e + 64], XT[:, e, q, :], x1n[:, 64 * e:64 * e + 64],
                          start=True, stop=True, inc=(e == 1))
                a = A(act.activation, SA, b[0][:, 0:128], ACT.Copy, w=[r, st2["y"]])
                banks.give(b, a)
                yield
                yo = by[0][:, q * 128:(q + 1) * 128]
                T.wait(a)
                b = None
                if q < CH - 1:
                    b = banks.take()
                    T.wait(b[1])
                    T(pe.matmul, b[0][:, 0:128], d["Bt"][:, q, :], SA, start=True, stop=False, inc=False)
                    r = T(pe.matmul, b[0][:, 0:128], d["Kt"][:, q, :], d["Vt"][:, q, :], start=False, stop=True)
                    v = V(dve.tensor_tensor, Su, b[0][:, 0:128], Sbd, ALU.add, w=[r, ts])
                    banks.give(b, v)
                for e in range(2):
                    ye = yo[64 * e:64 * e + 64, :]
                    T(pe.matmul, ye, Sbd[:, 64 * e:64 * e + 64], KR[:, q, 1, :], start=True, stop=False, inc=False)
                    T(pe.matmul, ye, SA[:, 64 * e:64 * e + 64], AB[:, e, q, 1, :], start=False, stop=False,
                      inc=False)
                    ry = T(pe.matmul, ye, d["Vt"][:, q, 64 * e:64 * e + 64], AK[:, e, q, 1, :], start=False,
                           stop=True, inc=(e == 1))
                st2["y"] = [ry]
                if q < CH - 1:
                    ts = V(dve.scalar_tensor_tensor, out=Sbd, in0=Su, scalar=d["dd"][:, q:q + 1], in1=bones[:, :],
                           op0=ALU.mult, op1=ALU.mult, w=[v, ry])
                yield
            mats.give(inp["m"], ry)
            y = tmp.take()
            a = A(act.activation, y[0], by[0], ACT.Copy, w=[ry, y[1]])
            banks.give(by, a)
            b = banks.take()
            r = T(pe.matmul, b[0], bones[:, :], y[0], start=True, stop=True, w=[a, b[1]])
            v = V(dve.scalar_tensor_tensor, out=y[0], in0=b[0], scalar=-1.0 / 64, in1=y[0], op0=ALU.mult,
                  op1=ALU.add, w=[r])
            banks.give(b, v)
            yield
            q = tmp.take()
            a = A(act.activation, q[0], y[0], ACT.Square, w=[v, q[1]])
            b = banks.take()
            r = T(pe.matmul, b[0], bones[:, :], q[0], start=True, stop=True, w=[a, b[1]])
            gs = tmp.take()
            o = []
            yield from proj_steps("ein", 49 + c, hT, o)
            bg, rg = o
            tg = A(act.activation, gs[0], bg[0], ACT.Silu, w=[rg, gs[1]])
            banks.give(bg, tg)
            yield
            v = V(dve.tensor_scalar, q[0], b[0], 1.0 / 64, 64e-5, ALU.mult, ALU.add, w=[r])
            banks.give(b, v)
            vr = A(act.activation, q[0], q[0], ACT.Sqrt, w=[v])
            for i in range(CH):
                v = V(dve.reciprocal, chunked(q[0])[:, i, :], chunked(q[0])[:, i, :], w=[vr])
                yield
            v = V(dve.scalar_tensor_tensor, out=y[0], in0=y[0], scalar=col("gn_w", c), in1=q[0], op0=ALU.mult,
                  op1=ALU.mult, w=[v])
            v = V(dve.scalar_tensor_tensor, out=y[0], in0=y[0], scalar=col("gn_b", c), in1=bon[0], op0=ALU.add,
                  op1=ALU.add, w=[v, inp["bon"]])
            bons.give(bon, v)
            g = V(dve.tensor_tensor, gs[0], y[0], gs[0], ALU.mult, w=[v, tg])
            tk = Y.dma(sp.dma_start, t["yd"][8 + c], gs[0], s_yb[c], w=[g])
            tmp.give(gs, tk)
            tmp.give(y, g)
            tmp.give(q, v)
            yb_toks.append(tk)
            sets.give(s, ry, g, v)

        yb_toks = []
        s_yb = [[sem(f"s_yb{i}"), 0] for i in range(8)]

        def weave(*gens):
            live = [[g[2], 0.0, g] for g in gens]
            while live:
                x = min(live, key=lambda y: y[0] + PATIENCE * max(0.0, y[1] - T.t))
                EST["latest"] = 0.0
                try:
                    if next(x[2][0]) == "blocked":
                        x[1] = T.t + 1500
                    else:
                        x[1] = EST["latest"]
                    x[0] += (x[2][3] - x[2][2]) / x[2][1]
                except StopIteration:
                    live.remove(x)

        def run(*gens):
            live = [[g[2] if len(g) > 2 else 0.0, i, g] for i, g in enumerate(gens)]
            while live:
                x = min(live, key=lambda y: y[:2])
                g = x[2]
                try:
                    next(g[0])
                    x[0] += ((g[3] - g[2]) if len(g) > 2 else 1.0) / g[1]
                except StopIteration:
                    live.remove(x)

        st["pool"] = True
        ui = {}
        o = [{} for _ in range(8)]
        ag_toks = []
        s_ag = [[sem(f"s_ag{i}"), 0] for i in range(8)]

        def conv_gate(tiles):
            for m in tiles:
                o = []
                yield from proj_steps("ein", 16 + m, hT, o)
                b, r = o
                x = tmp.take()
                a = A(act.activation, x[0], b[0], ACT.Silu, w=[r, x[1]])
                banks.give(b, a)
                tk = Y.dma(sp.dma_start, t["yd"][16 + m], x[0], s_ag[m], w=[a])
                tmp.give(x, tk)
                ag_toks.append(tk)
                yield

        mods = itertools.chain(*(mod_part(l, g) for l, g in ((0, 4), (0, 5), *((1, g) for g in range(6)))))

        run((prep(0, o[0]), 26), (conv_in(0, ui), 8))
        for i in range(1, 10):
            gens = []
            if i >= 2:
                gens.append((solve(i - 2, o[i - 2]), 24, 0.059, 1.0))
            if i <= 8:
                gens += [(invert(i - 1, o[i - 1]), 24, 0, 1.0), (conv(i - 1, ui), 31, 0.079, 0.689)]
            if i <= 7:
                gens += [(prep(i, o[i]), 26, 0, 0.9), (conv_in(i, ui), 8, 0.499, 0.841)]
            if i == 8:
                gens.append((conv_gate(range(3)), 12, 0.1, 1.0))
            if i == 9:
                gens.append((conv_gate(range(3, 8)), 20, 0.0, 1.0))
            if i <= 8:
                gens.append((itertools.islice(mods, 4), 4, 0.193, 0.943))
            weave(*gens)
        st["pool"] = False
        ar.leave()
        ar_t = Phase(0)
        posf, pcol, pcr, cidr = ar_t(512), ar_t(4), ar_t(4), ar_t(512)
        tab = {"128": (ar_t(512), ar_t(512)), "64": (ar_t(512), ar_t(512))}
        ar = Phase(4)
        ar.temps()
        xr = ar(4096).rearrange("p (k s) -> p k s", k=8)
        yc = ar(4096).rearrange("p (k s) -> p k s", k=8)
        yb = ar(4096).rearrange("p (k s) -> p k s", k=8)
        ag = ar(4096).rearrange("p (k s) -> p k s", k=8)
        ya = ar(8192, F32R).rearrange("p (a k s) -> p a k s", a=2, k=8)
        s_yr = [[sem(f"s_yr{i}"), 0] for i in range(6)]
        Y.wait(y_toks, yb_toks, ag_toks)
        yb_toks = [Y.dma(sp.dma_start, yb[:, 2 * i:2 * i + 2, :],
                         t["yd"][8 + 2 * i:10 + 2 * i].rearrange("k p s -> p k s"), s_yr[(1, 3, 4, 5)[i]])
                   for i in range(4)]
        y_tok = Y.dma(sp.dma_start, yc, t["yd"][0:8].rearrange("k p s -> p k s"), s_yr[0])
        x_tok = Y.dma(sp.dma_start, xr, t["xT"].rearrange("(k p) s -> p k s", p=128), s_x)
        ag_tok = Y.dma(sp.dma_start, ag, t["yd"][16:24].rearrange("k p s -> p k s"), s_yr[2])

        tabs = {}
        cid = []

        def rope_tables():
            posi = tmp.take()
            s_p = [sem("s_p"), 0]
            ptok = Y.dma(sp.dma_start, posi[0].bitcast(I32), t["positions"].partition_broadcast(128), s_p,
                         w=[posi[1]])
            ptok2 = Y.dma(sp.dma_start, pcr.bitcast(I32), t["pcol"][:, :], s_p)
            v = V(dve.tensor_copy, posf, posi[0].bitcast(I32), w=[ptok2])
            C1 = 6.28125
            C2 = float(np.float32(np.round((TWO_PI - C1) * 2 ** 21) / 2 ** 21))
            C3 = float(TWO_PI - C1 - C2)
            for nm, inv, sgn in (("128", "inv128", "sgn128"), ("64", "inv64", "sgn64")):
                ang, n = tmp.take(), tmp.take()
                cosT, sinT = tab[nm]
                v = V(dve.tensor_scalar, ang[0], posf, col(inv), None, ALU.mult, w=[v, ang[1]])
                v = V(dve.tensor_scalar, n[0], ang[0], 1.0 / TWO_PI, None, ALU.mult, w=[v, n[1]])
                v = V(dve.tensor_scalar, n[0], n[0], MAGIC, None, ALU.add, w=[v])
                v = V(dve.tensor_scalar, n[0], n[0], -MAGIC, None, ALU.add, w=[v])
                yield
                for cst in (C1, C2, C3):
                    v = V(dve.scalar_tensor_tensor, out=ang[0], in0=n[0], scalar=-cst, in1=ang[0],
                          op0=ALU.mult, op1=ALU.add, w=[v])
                v = V(dve.tensor_scalar, ang[0], ang[0], 3.1415925, -3.1415925, ALU.min, ALU.max, w=[v])
                yield
                a = A(act.activation, sinT, ang[0], ACT.Sin, w=[v])
                vs = V(dve.tensor_scalar, sinT, sinT, col(sgn), None, ALU.mult, w=[a])
                v = V(dve.tensor_scalar, ang[0], ang[0], math.pi / 2, None, ALU.add, w=[a])
                yield
                v = V(dve.tensor_scalar, n[0], ang[0], math.pi, -TWO_PI, ALU.is_gt, ALU.mult, w=[v])
                v = V(dve.tensor_tensor, ang[0], ang[0], n[0], ALU.add, w=[v])
                v = V(dve.tensor_scalar, ang[0], ang[0], 3.1415925, -3.1415925, ALU.min, ALU.max, w=[v])
                a = A(act.activation, cosT, ang[0], ACT.Sin, w=[v])
                tmp.give(ang, a)
                tmp.give(n, v)
                tabs[nm] = (cosT, sinT, [a, vs])
            v = V(dve.tensor_scalar, posi[0].bitcast(I32), posi[0].bitcast(I32), 6, None,
                  ALU.arith_shift_right, w=[v])
            v = V(dve.tensor_copy, cidr, posi[0].bitcast(I32), w=[v])
            tmp.give(posi, v)
            v = V(dve.tensor_scalar, pcr.bitcast(I32), pcr.bitcast(I32), 6, None, ALU.arith_shift_right, w=[v, ptok2])
            cid.append(V(dve.tensor_copy, pcol, pcr.bitcast(I32), w=[v]))

        h_toks = split_all(yb, [yb_toks[k // 2] for k in range(8)], T.last())

        def eout_b(m):
            b, r = proj("eout", 2 * m + 1, hT, wk=h_toks)
            v = V(dve.scalar_tensor_tensor, out=xr[:, m, :], in0=b[0], scalar=mod[:, 0, 16 + m:17 + m],
                  in1=xr[:, m, :], op0=ALU.mult, op1=ALU.add, w=[r, x_tok, mod_toks[0]])
            banks.give(b, v)
            return r

        eout_b(0)
        b = banks.take()
        for m in range(8):
            r = T(pe.matmul, b[0], ones[:, :], yc[:, m, :], start=(m == 0), stop=(m == 7), w=[y_tok, b[1]])
        mu = tmp.take()
        a = A(act.activation, mu[0], b[0], ACT.Copy, scale=1.0 / D, w=[r, mu[1]])
        banks.give(b, a)
        vs = [V(dve.tensor_tensor, yc[:, m, :], yc[:, m, :], mu[0], ALU.subtract, w=[a, y_tok]) for m in range(8)]
        eout_b(1)
        eout_b(2)
        b = banks.take()
        for m in range(8):
            q = tmp.take()
            a2 = A(act.activation, q[0], yc[:, m, :], ACT.Square, w=[vs[m], q[1]])
            r = T(pe.matmul, b[0], ones[:, :], q[0], start=(m == 0), stop=(m == 7), w=[a2, b[1]])
            tmp.give(q, r)
        v = V(dve.tensor_scalar, mu[0], b[0], 1.0 / D, 1e-5, ALU.mult, ALU.add, w=[r, vs])
        banks.give(b, v)
        vr = rsqrt(mu[0], v)
        ya_toks = []
        for m in range(8):
            if m < 5:
                eout_b(3 + m)
            v = V(dve.tensor_tensor, yc[:, m, :], yc[:, m, :], mu[0], ALU.mult, w=[vr])
            a = A(act.activation, yc[:, m, :], yc[:, m, :], ACT.Silu, scale=col("ln_w", m),
                  bias=col("ln_b", m), w=[v])
            ya_toks.append(G(pool.tensor_tensor, yc[:, m, :], yc[:, m, :], ag[:, m, :], ALU.mult, w=[a, ag_tok]))
        tmp.give(mu, v)
        h_toks = split_all(yc, ya_toks, [], ya)
        rt = rope_tables()
        x_toks = []
        for m in range(8):
            b, r = proj("eout", 2 * m, ya, wk=h_toks)
            st["pool"] = True
            v = V(dve.scalar_tensor_tensor, out=xT[:, m, :], in0=b[0], scalar=mod[:, 0, 16 + m:17 + m],
                  in1=xr[:, m, :], op0=ALU.mult, op1=ALU.add, w=[r])
            banks.give(b, v)
            x_toks.append(v)
            if m < 7:
                next(rt, None)
        for _ in rt:
            pass
        st["pool"] = False

        x_toks = [[x, mod_toks[1]] for x in x_toks]
        stat = norm_stat(xT, x_toks)
        ar.leave()
        ar = Phase(14)
        ar.temps()
        h_toks = norm_T(xT, hT, gsc[:, 1, :], mod[:, 1, 0:8], w=x_toks, stat=stat)
        og = ar(8192).rearrange("p (k s) -> p k s", k=16)
        ar_a = Phase(0)
        def rope(b, r, tab, out, w=()):
            cosT, sinT, tt = tabs[tab]
            h = int(tab) // 2
            m, n = tmp.take(), tmp.take()
            v1 = V(dve.tensor_tensor, m[0], b[0], cosT, ALU.mult, w=[r, m[1], tt])
            V.wait(n[1])
            for p in range(0, 128, h):
                q = p + h if (p // h) % 2 == 0 else p - h
                v2 = V(dve.tensor_tensor, n[0][p:p + h, :], b[0][q:q + h, :], sinT[q:q + h, :], ALU.mult)
            banks.give(b, v2)
            E, e = (V, dve) if st["pool"] else (G, pool)
            g = E(e.tensor_tensor, out, m[0], n[0], ALU.add, w=[v1, v2, w])
            tmp.give(m, g)
            tmp.give(n, g)
            return g

        kiT = ar_a(512)
        b, r = proj("oin", 22, hT, wk=h_toks)
        ki_tok = rope(b, r, "64", kiT)
        hl, W, tok = unit_hl("oin", 23)
        b = banks.take()
        T.wait(tok, b[1])
        for q in range(4):
            for k in range(8):
                r = mm3(b[0][:, q * 8:q * 8 + 8],
                        [hT[:, i, k, q * 128:(q + 1) * 128] for i in range(2)], [W[:, i, k, 0:8] for i in range(2)],
                        first=(k == 0), last=(k == 7), inc=(k == 7))
        wsl[0].give(hl, r)
        wi = ar_a(32)
        wi_tok = A(act.activation, wi, b[0][:, 0:32], ACT.Copy, scale=8.0 ** -0.5, w=[r])
        banks.give(b, wi_tok)
        qi = ar_a(2048).rearrange("p (k s) -> p k s", k=4)
        qi_toks = []
        for m in range(4):
            b, r = proj("oin", 18 + m, hT)
            qi_toks.append(rope(b, r, "64", qi[:, m, :]))
        kT = ar_a(512)
        Vs = ar_a(512).rearrange("p (s n) -> p s n", s=4)
        kv = {}

        def key_part():
            b, r = proj("oin", 16, hT)
            kv["k"] = rope(b, r, "128", kT)

        def value_part():
            hl, W, tok = unit_hl("oin", 17)
            b = banks.take()
            T.wait(tok, b[1])
            for q in range(4):
                for k in range(8):
                    r = mm3(b[0][:, q * 128:(q + 1) * 128],
                            [hT[:, i, k, q * 128:(q + 1) * 128] for i in range(2)],
                            [W[:, i, k, :] for i in range(2)],
                            first=(k == 0), last=(k == 7), inc=(k == 7))
            wsl[0].give(hl, r)
            kv["v"] = A(act.activation, Vs.rearrange("p s n -> p (s n)"), b[0], ACT.Copy, w=[r])
            banks.give(b, kv["v"])

        selb = ar_a(2048).rearrange("p (b s) -> p b s", b=4)
        m8 = ar_a(8)
        sel_toks = []
        og_toks = {}

        def gate_proj(m):
            b, r = proj("oin", 24 + m, hT)
            og_toks[m] = A(act.activation, og[:, m, :], b[0], ACT.Silu, w=[r])
            banks.give(b, og_toks[m])

        qTs = Slots([ar_a(512) for _ in range(2)])
        nxt = {}

        def q_part(h, out):
            b, r = proj("oin", h, hT)
            qT = qTs.take()
            out["q"] = (qT, rope(b, r, "128", qT[0], w=[qT[1]]))

        fill = [key_part, value_part, *(lambda m=m: gate_proj(m) for m in range(16)), lambda: q_part(0, nxt)]
        m8_free = []
        fill.pop(0)()
        fill.pop(0)()
        st["pool"] = True
        for blk in range(4):
            acc, val = tmp.take(), tmp.take()
            v = None
            for h in range(8):
                e = h % 2
                b = banks.take()
                r = T(pe.matmul, b[0], qi[64 * e:64 * e + 64, h // 2, blk * 128:(blk + 1) * 128],
                      kiT[64 * e:64 * e + 64, :], start=True, stop=True, w=[b[1], qi_toks, ki_tok])
                x = tmp.take()
                a = A(act.activation, x[0], b[0], ACT.Relu, scale=0.125, w=[r, x[1]])
                banks.give(b, a)
                wc = wi[:, blk * 8 + h:blk * 8 + h + 1]
                if h == 0:
                    v = V(dve.tensor_scalar, acc[0], x[0], wc, None, ALU.mult, w=[a, wi_tok, acc[1]])
                else:
                    v = V(dve.scalar_tensor_tensor, out=acc[0], in0=x[0], scalar=wc, in1=acc[0],
                          op0=ALU.mult, op1=ALU.add, w=[a, v])
                tmp.give(x, v)
            v2 = V(dve.tensor_scalar, val[0], cidr, pcol[:, blk:blk + 1], None, ALU.is_le, w=[cid, val[1]])
            v = V(dve.tensor_tensor, acc[0], acc[0], val[0], ALU.mult, w=[v, v2])
            x = tmp.take()
            v2 = V(dve.tensor_scalar, x[0], val[0], -1.0, -NEG, ALU.add, ALU.mult, w=[v2, x[1]])
            v = V(dve.tensor_tensor, acc[0], acc[0], x[0], ALU.add, w=[v, v2])
            if blk == 3:
                fill.pop()()
            cur = acc[0]
            for i in range(16):
                v = V(dve.max, m8, cur, w=[v, m8_free])
                v = V(dve.match_replace, x[0], m8, cur, -3e38, w=[v])
                cur = x[0]
            v = V(dve.tensor_tensor, x[0], x[0], acc[0], ALU.not_equal, w=[v])
            v = V(dve.tensor_tensor, x[0], x[0], val[0], ALU.mult, w=[v])
            v = V(dve.tensor_scalar, selb[:, blk, :], x[0], -1.0, -NEG, ALU.add, ALU.mult, w=[v])
            sel_toks.append(v)
            tmp.give(acc, v)
            tmp.give(val, v)
            tmp.give(x, v)
            for _ in range(4):
                fill.pop(0)()

        SC = 128 ** -0.5
        PTs = Slots([ar_a(2048).rearrange("p (s q) -> p s q", s=4) for _ in range(2)])
        sms = Slots([small[:, i, 0:4] for i in range(8)])

        def attend(h, inp):
            qT, q_tok = inp["q"]
            PT = PTs.take()
            evs = []
            Ps = []
            ready = []

            def normed(x):
                p, c4, a = x
                v = V(dve.reciprocal, c4[0][:, 3:4], c4[0][:, 2:3], w=[a])
                ready.append(A(act.activation, p[0], p[0], ACT.Copy, scale=c4[0][:, 3:4], w=[v]))
                sms.give(c4, ready[-1])

            for blk in range(4):
                b = banks.take()
                r = T(pe.matmul, b[0], qT[0][:, blk * 128:(blk + 1) * 128], kT, start=True, stop=True,
                      w=[b[1], q_tok, kv["k"]])
                p, c4 = tmp.take(), sms.take()
                v = V(dve.tensor_tensor_reduce, out=p[0], in0=b[0], in1=selb[:, blk, :], scale=1.0,
                      scalar=-3e38, op0=ALU.add, op1=ALU.max, accum_out=c4[0][:, 0:1],
                      w=[r, p[1], c4[1], sel_toks[blk]])
                banks.give(b, v)
                v = V(dve.tensor_scalar, c4[0][:, 1:2], c4[0][:, 0:1], -SC, None, ALU.mult, w=[v])
                a = A(act.activation, p[0], p[0], ACT.Exp, scale=SC, bias=c4[0][:, 1:2],
                      accum_out=c4[0][:, 2:3], w=[v])
                Ps.append((p, c4, a))
                if blk:
                    normed(Ps[blk - 1])
            normed(Ps[3])
            qTs.give(qT, r)
            yield
            for blk in range(4):
                p = Ps[blk][0]
                g = ready[blk]
                b = banks.take()
                T.wait(b[1], g)
                for s in range(4):
                    r = T(pe.transpose, b[0][:, s * 128:(s + 1) * 128], p[0][:, s * 128:(s + 1) * 128],
                          ident[:, :], inc=(s == 3))
                tmp.give(p, r)
                dst = PT[0][:, :, blk * 128:(blk + 1) * 128]
                srcb = b[0].rearrange("p (s q) -> p s q", s=4)
                if blk % 2:
                    e = V(dve.tensor_copy, dst, srcb, w=[r, PT[1]])
                else:
                    e = A(act.activation, dst, srcb, ACT.Copy, w=[r, PT[1]])
                banks.give(b, e)
                evs.append(e)
            yield
            b = banks.take()
            T.wait(b[1], evs, kv["v"])
            for s in range(4):
                r = T(pe.matmul, b[0], Vs[:, s, :], PT[0][:, s, :], start=(s == 0), stop=(s == 3), inc=(s == 3))
            PTs.give(PT, r)
            v = V(dve.tensor_tensor, og[:, h, :], b[0], og[:, h, :], ALU.mult, w=[r, og_toks[h]])
            banks.give(b, v)
            og_toks[h] = v

        old = None
        for h in range(16):
            g = attend(h, nxt)
            next(g)
            if old:
                next(old)
            nxt = {}
            if h < 15:
                q_part(h + 1, nxt)
            if old:
                next(old, None)
            old = g
        next(old)
        next(old, None)
        st["pool"] = False
        for half in range(2):
            if half:
                rhs, h_toks = h2, h2_toks
            else:
                h_toks = split_all(og[:, 0:8, :], [og_toks[k] for k in range(8)], T.last())
                rhs = hT
                ar_a.leave()
                ar_a = Phase(0)
                h2 = ar_a(8192, F32R).rearrange("p (a k s) -> p a k s", a=2, k=8)
                h2_toks = split_all(og[:, 8:16, :], [og_toks[8 + k] for k in range(8)], [], h2)
            x_toks = []
            for m in range(8):
                b, r = proj("oout", 2 * m + half, rhs, wk=h_toks)
                x_toks.append(residual(b, r, m, gate=mod[:, 1, 16 + m:17 + m]))
        fgm = gsc[:, 0, :]
        of, om = VOFF["final_g"][0], VOFF["g_mix"][0]
        V(dve.tensor_tensor, fgm, vec[:, of:of + 8], vec[:, om:om + 8], ALU.mult)
        b, b2 = banks.take(), banks.take()
        for k in range(KT):
            q, q2 = tmp.take(), tmp.take()
            a = A(act.activation, q[0], xT[:, k, :], ACT.Square, w=[x_toks[k], q[1]])
            a2 = A(act.activation, q2[0], xT[:, k, :], ACT.Square, scale=vec[:, of + k:of + k + 1],
                   w=[x_toks[k], q2[1]])
            r = T(pe.matmul, b[0], ones[:, :], q[0], start=(k == 0), stop=(k == 7), w=[a, b[1]])
            r2 = T(pe.matmul, b2[0], ones[:, :], q2[0], start=(k == 0), stop=(k == 7), w=[a2, b2[1]])
            tmp.give(q, r)
            tmp.give(q2, r2)
        m2 = small[:, :, :].rearrange("p a n -> p (a n)")
        v = V(dve.tensor_scalar, msum[:, :], b[0], 1.0 / D, 1e-6, ALU.mult, ALU.add, w=[r])
        banks.give(b, v)
        v2 = V(dve.tensor_scalar, m2, b2[0], 1.0 / D, None, ALU.mult, w=[r2])
        banks.give(b2, v2)
        v2 = V(dve.scalar_tensor_tensor, out=m2, in0=msum[:, :], scalar=1e-6, in1=m2, op0=ALU.mult,
               op1=ALU.add, w=[v, v2])
        v2 = rsqrt(m2, v2)
        fence()
        ar_a.leave(False)
        ar.leave(False)
        ar_t.leave(False)
        ar = Phase(14)
        ar.temps()

        h_toks = norm_T(xT, hT, fgm, stat=(m2, v2))
        v = rsqrt(msum[:, :], v)
        f_toks = norm_T(xT, None, vec[:, of:of + 8], w=[h_toks[k] for k in range(8)], stat=(msum[:, :], v))
        ym = ar(4096).rearrange("p (k s) -> p k s", k=8)
        PADL = 16
        zp = [ar(S + 2 * PADL) for _ in range(3)]
        icnt = ar(2048).rearrange("p (g s) -> p g s", g=4)
        s_ic = [sem("s_ic"), 0]
        ic_tok = Y.dma(sp.dma_start, icnt, t["icnt"].rearrange("g s -> (g s)").partition_broadcast(128), s_ic)
        v = None
        for z in zp:
            v = V(dve.memset, z, 0.0, w=[v])
        zt = v
        ymt = {}
        cc = {}
        xg = {}
        pl = []
        v = zt
        for g in range(4):
            w = 2 << g
            b, r = proj("win", 12 + g, hT, wk=h_toks)
            z, z2 = zp[1], zp[2]
            u = tmp.take()
            v = V(dve.tensor_copy, z[:, PADL:PADL + S], b[0], w=[r, v])
            a = A(act.activation, u[0], b[0], ACT.Copy, w=[v, u[1]])
            banks.give(b, v, a)
            src, dst, n = z, z2, 1
            while n < w:
                L = S + 2 * PADL
                v = V(dve.tensor_tensor, dst[:, n:L], src[:, n:L], src[:, 0:L - n], ALU.add, w=[v])
                v = V(dve.tensor_copy, dst[:, 0:n], src[:, 0:n], w=[v])
                src, dst, n = dst, src, 2 * n
            o = PADL + w // 2 - 1
            p = tmp.take()
            v = V(dve.tensor_tensor, p[0], src[:, o:o + S], icnt[:, g, :], ALU.mult, w=[v, ic_tok, p[1]])
            pt = V(dve.tensor_tensor, p[0], p[0], u[0], ALU.subtract, w=[v, a])
            tmp.give(u, pt)
            v = V(dve.memset, z, 0.0, w=[pt])
            v = V(dve.memset, z2, 0.0, w=[v])
            pl.append((p, pt))
        for m in range(4):
            b, r = proj("win", m, hT)
            a = A(act.activation, ym[:, m, :], b[0], ACT.Copy, w=[r])
            banks.give(b, a)
            ymt[m] = a
        for m in range(4):
            cc[m] = tmp.take()
            b, r = proj("win", 4 + m, hT)
            a = A(act.activation, cc[m][0], b[0], ACT.Copy, w=[r, cc[m][1]])
            banks.give(b, a)
            cc[m] = (cc[m], a)
        for m in range(4):
            b, r = proj("win", 8 + m, hT)
            z = zp[0]
            cs, a = cc[m]
            v = V(dve.tensor_tensor, z[:, 1:S + 1], b[0], cs[0], ALU.mult, w=[r, a, zt])
            banks.give(b, v)
            w3 = lambda i: col("conv_w2", m * 3 + i)
            v = V(dve.tensor_scalar, cs[0], z[:, 0:S], w3(0), None, ALU.mult, w=[v])
            v = V(dve.scalar_tensor_tensor, out=cs[0], in0=z[:, 1:S + 1], scalar=w3(1), in1=cs[0],
                  op0=ALU.mult, op1=ALU.add, w=[v])
            zt = v = V(dve.scalar_tensor_tensor, out=cs[0], in0=z[:, 2:S + 2], scalar=w3(2), in1=cs[0],
                       op0=ALU.mult, op1=ALU.add, w=[v])
            ymt[m] = V(dve.tensor_tensor, ym[:, m, :], ym[:, m, :], cs[0], ALU.mult, w=[v, ymt[m]])
            tmp.give(cs, ymt[m])
        W, tok = unit("pool", 0)
        for g in range(4):
            p, pt = pl[g]
            b = banks.take()
            r = T(pe.matmul, b[0], W[:, g, :], p[0], start=True, stop=True, w=[tok, pt, b[1]])
            tmp.give(p, r)
            ymt[4 + g] = A(act.activation, ym[:, 4 + g, :], b[0], ACT.Copy, scale=col("pool_s", g), w=[r])
            banks.give(b, ymt[4 + g])
        load_next(r)
        h_toks = split_all(ym, ymt, r)
        x_toks = []
        for m in range(8):
            b, r = proj("wo", m, hT, wk=h_toks)
            x_toks.append(residual(b, r, m))
        stat = norm_stat(xT, x_toks)
        ar.leave()

        ar0 = Phase(0)
        gT, rT = ar0(512), msum[:, :]
        ixT = [ar0(512, BF16) for _ in range(5)]
        s_zd = [[sem(f"s_zd{i}"), 0] for i in range(2)]
        pre = []

        def pre_z(xs):
            j = len(pre)
            if j >= NPRE * JC:
                return
            b, r = proj("eu", j, hT, wk=h_toks)
            x = xs.take()
            a = A(act.activation, x[0][0], b[0], ACT.Gelu_apprx_tanh, w=[r, x[1]])
            banks.give(b, a)
            tk = Y.dma(sp.dma_start, t["zd"][j], x[0][0], x[0][1], w=[a])
            xs.give(x, tk)
            pre.append(tk)

        ar = Phase(5)
        ar.temps()
        o = VOFF["g_ffn"][0]
        h_toks = norm_T(xT, hT, vec[:, o:o + 8], w=x_toks, stat=stat)
        xs = Slots([(ar(512), s_zd[i]) for i in range(2)])
        ksb = ar(2048).rearrange("p (u k m) -> p u k m", u=2, k=8)
        s_ks = [sem("s_ks"), 0]
        ks_tok = Y.dma(sp.dma_start, ksb.rearrange("p u k m -> p u (k m)"), t["keys"].rearrange("u p n -> p u n"), s_ks)
        cand = ar(2048)
        cand2 = ar(2048)
        gcand2 = []
        sv_ = ar(1024).rearrange("p (b h k) -> p b h k", b=4, k=16)
        sx_ = ar(1024, U32).rearrange("p (b h k) -> p b h k", b=4, k=16)
        sxf = ar(256).rearrange("p (h k) -> p h k", k=16)
        tv = ar(128).rearrange("p (h k) -> p h k", k=16)
        px = ar(128, U32).rearrange("p (h k) -> p h k", k=16)
        ph = ar(128, U32)
        hif = ar(128)
        lof = ar(128)
        ijg = ar(384)
        io16 = ar(16)
        s16 = ar(256)
        io_tok = Y.dma(sp.dma_start, io16, t["iota16"].partition_broadcast(128), s_ic)
        v = None
        fin, gcand = [], []
        def top16(n, src, vals, idx, w, beside=lambda: None):
            a, b = slice(0, 8), slice(8, 16)
            one = [V(dve.max, vals[:, i, a], src(i), w=w) for i in range(n)]
            beside()
            for i in range(n):
                V(dve.max_index, idx[:, i, a], vals[:, i, a], src(i), w=[one[i]])
            beside()
            one = [V(dve.match_replace, src(i), vals[:, i, a], src(i), -3e38, w=[V.last()] if not i else [])
                   for i in range(n)]
            beside()
            one = [V(dve.max, vals[:, i, b], src(i), w=[one[i]]) for i in range(n)]
            for i in range(n):
                v = V(dve.max_index, idx[:, i, b], vals[:, i, b], src(i), w=[one[i]])
            return v

        for hp in range(16):
            b, r = proj("wq", hp, hT, wk=h_toks)
            q = tmp.take()
            a = A(act.activation, q[0], b[0], ACT.Copy, w=[r, q[1]])
            banks.give(b, a)
            b = banks.take()
            T.wait(a, b[1], ks_tok)
            for blk in range(4):
                r = T(pe.matmul, b[0][:, blk * 128:(blk + 1) * 128], q[0][:, blk * 128:(blk + 1) * 128],
                      ksb[:, hp // 8, hp % 8, :], start=True, stop=True, inc=(blk == 3))
            tmp.give(q, r)
            x = tmp.take()
            a = A(act.activation, x[0], b[0], ACT.Copy, w=[r, x[1]])
            banks.give(b, a)
            v = top16(4, lambda i: x[0][:, i * 128:(i + 1) * 128], sv_[:, :, hp, :], sx_[:, :, hp, :], [a])
            tmp.give(x, v)
        for blk in range(4):
            pre_z(xs)
            sv, sx = sv_[:, blk, :, :], sx_[:, blk, :, :]
            v = V(dve.tensor_copy, sxf, sx, w=[v])
            sv4 = sv.rearrange("p (h two) k -> p h two k", two=2)
            sx4 = sxf.rearrange("p (h two) k -> p h two k", two=2)
            c4 = cand.rearrange("p (h a b) -> p h a b", h=8, a=16)
            for h in range(8):
                v = V(dve.tensor_tensor, c4[:, h, :, :],
                      sv4[:, h, 0, :].rearrange("p (a o) -> p a o", o=1).broadcast_to([128, 16, 16]),
                      sv4[:, h, 1:2, :].broadcast_to([128, 16, 16]), ALU.add, w=[gcand])
            pre_z(xs)
            v = top16(8, lambda i: cand[:, i * 256:(i + 1) * 256], tv, px, [v], lambda: pre_z(xs))
            pxf = px.rearrange("p h k -> p (h k)")
            v = V(dve.tensor_scalar, ph, pxf, 4, None, ALU.logical_shift_right, w=[v])
            v = V(dve.tensor_copy, hif, ph, w=[v])
            v = V(dve.tensor_scalar, ph, pxf, 15, None, ALU.bitwise_and, w=[v])
            v = V(dve.tensor_copy, lof, ph, w=[v])
            for half, src in ((1, lof), (0, hif)):
                E, e_, buf, gw = (G, pool, cand2, gcand2) if half else (V, dve, cand, [])
                oh = buf.rearrange("p (n a) -> p n a", a=16)
                if half:
                    v1 = v
                v = V(dve.tensor_tensor, oh, src.rearrange("p (n o) -> p n o", o=1).broadcast_to([128, 128, 16]),
                      io16.rearrange("p (o a) -> p o a", o=1).broadcast_to([128, 128, 16]), ALU.is_equal,
                      w=[v1, io_tok, gw])
                oh4 = buf.rearrange("p (h k a) -> p h k a", h=8, k=16)
                v0 = v
                for h in range(8):
                    v = E(e_.tensor_tensor, oh4[:, h, :, :], oh4[:, h, :, :],
                          sx4[:, h, half:half + 1, :].broadcast_to([128, 16, 16]), ALU.mult, w=[v0])
                pre_z(xs)
                if half:
                    gp_ = v
                    continue
                v = V(dve.tensor_reduce, ijg[:, 0:128], oh, AX.X, ALU.add, w=[v, fin])
                v = gcand2 = V(dve.tensor_reduce, ijg[:, 128:256], cand2.rearrange("p (n a) -> p n a", a=16),
                               AX.X, ALU.add, w=[gp_])
            pre_z(xs)
            gt = ijg[:, 256:384].rearrange("p (h k) -> p h k", k=16)
            v = V(dve.tensor_tensor, gt, tv, tv[:, :, 0:1].broadcast_to([128, 8, 16]), ALU.subtract, w=[v])
            a = A(act.activation, gt, gt, ACT.Exp, w=[v])
            s8 = s16[:, 0:8]
            v = V(dve.tensor_reduce, s8, gt, AX.X, ALU.add, w=[a])
            v = V(dve.reciprocal, s8, s8, w=[v])
            v = V(dve.tensor_tensor, gt, gt, s8.rearrange("p (h o) -> p h o", o=1).broadcast_to([128, 8, 16]),
                  ALU.mult, w=[v])
            b = banks.take()
            T.wait(b[1], v)
            for i in range(3):
                r = T(pe.transpose, b[0][:, i * 128:(i + 1) * 128], ijg[:, i * 128:(i + 1) * 128], ident[:, :],
                      inc=(i == 2))
            fin = [r]
            for i, o in enumerate((ixT[0], ixT[1], gT)):
                a = A(act.activation, o[:, blk * 128:(blk + 1) * 128], b[0][:, i * 128:(i + 1) * 128],
                      ACT.Copy, w=[r])
            banks.give(b, a)
        v = V(dve.tensor_copy, ixT[2], gT, w=[a, v])
        v = V(dve.tensor_tensor, rT, gT, ixT[2], ALU.subtract, w=[v])
        v = V(dve.tensor_copy, ixT[3], rT, w=[v])
        v = V(dve.tensor_tensor, rT, rT, ixT[3], ALU.subtract, w=[v])
        split_tok = V(dve.tensor_copy, ixT[4], rT, w=[v])
        ar.leave()
        st["pool"] = True
        ar = Phase(0)
        TB = 16
        iom = ar(128 * TB, BF16).rearrange("p (n t) -> p n t", t=TB)
        s_io = [sem("s_io"), 0]
        io_tok = Y.dma(sp.dma_start, iom.rearrange("p n t -> p (n t)"), t["iom"].partition_broadcast(128), s_io)
        oj = ar(128 * TB, BF16).rearrange("p (n t) -> p n t", t=TB)
        ohs = Slots([[ar(128 * TB, BF16).rearrange("p (n t) -> p n t", t=TB) for _ in range(4)] for _ in range(2)])
        xs = Slots([(ar(512), s_zd[i]) for i in range(2)])
        stages = Slots([(ar(128 * TG), [sem(f"s_st{i}"), 0]) for i in range(2)])
        gd_toks = []
        vg = None

        def spread(ix, t0):
            return ix[:, t0:t0 + TB].rearrange("p (o t) -> p o t", o=1).broadcast_to([128, 128, TB])

        for blk in range(S // TG):
            stg = stages.take()
            sview = stg[0][0].rearrange("p (j t) -> p j t", t=TG)
            for tb in range(TG // TB):
                t0 = blk * TG + tb * TB
                o = ohs.take()
                oi, g1, g2, g3 = o[0]
                if tb % 2 == 0:
                    pre_z(xs)
                V(dve.tensor_tensor, oi, iom, spread(ixT[0], t0), ALU.is_equal, w=[o[1], split_tok, io_tok])
                v = V(dve.tensor_tensor, oj, iom, spread(ixT[1], t0), ALU.is_equal, w=[vg])
                v1 = V(dve.tensor_tensor, g1, oj, spread(ixT[2], t0), ALU.mult, w=[v])
                V(dve.tensor_tensor, g2, oj, spread(ixT[3], t0), ALU.mult)
                vg = v = V(dve.tensor_tensor, g3, oj, spread(ixT[4], t0), ALU.mult)
                T.wait(v)
                for t4 in range(TB // 4):
                    b = banks.take()
                    T.wait(b[1])
                    for q in range(4):
                        tk = t4 * 4 + q
                        for m, gm in enumerate((g1, g2, g3)):
                            r = T(pe.matmul, b[0][:, q * 128:(q + 1) * 128], oi[:, :, tk], gm[:, :, tk],
                                  start=(m == 0), stop=(m == 2), inc=(m == 2))
                    at_ = tb * TB + t4 * 4
                    e = A(act.activation, sview[:, :, at_:at_ + 4].rearrange("p j t -> p t j"),
                          b[0].rearrange("p (t j) -> p t j", t=4), ACT.Copy, w=[r, stg[1]])
                    banks.give(b, e)
                ohs.give(o, r)
            tk = Y.dma(sp.dma_start, t["gd"][:, blk, :, :].rearrange("c p n -> p c n"),
                       stg[0][0].rearrange("p (c n) -> p c n", n=JC * TG), stg[0][1], w=[e])
            gd_toks.append(tk)
            stages.give(stg, tk)
        ar.leave()
        ar0.leave(False)
        st["pool"] = False
        ar = Phase(5)
        ar.temps()
        more = ar(5 * 2048, F32R).rearrange("p (i a n) -> p i a n", i=5, a=2)
        keep = wsl[0].free
        wsl[0].free = keep + [(more[:, i, :, :], []) for i in range(5)]
        NC = 128 // JC
        gch = [(ar(JC * S), [sem(f"s_g{i}"), 0]) for i in range(2)]
        agb = [ar(2 * JC * S, F32R).rearrange("p (a j s) -> p a j s", a=2, j=JC) for _ in range(2)]
        gfree = [[], []]
        afree = [[], []]
        gl = {}
        zch = [(ar(JC * S).rearrange("p (j s) -> p j s", j=JC), [sem(f"s_z{i}"), 0]) for i in range(2)]
        zl = {}

        def load_g(c):
            g, sm_ = gch[c % 2]
            gl[c] = Y.dma(sp.dma_start, g.rearrange("p (b n) -> p b n", n=JC * TG),
                          t["gd"][c].rearrange("b p n -> p b n"), sm_, w=[gfree[c % 2], gd_toks])
            if c < NPRE:
                z, sm_ = zch[c % 2]
                zl[c] = Y.dma(sp.dma_start, z, t["zd"][c * JC:(c + 1) * JC].rearrange("j p n -> p j n"), sm_,
                              w=[pre[c * JC:(c + 1) * JC]])

        xs = Slots([(tmp.take()[0], s_zd[i]) for i in range(2)])
        pre_z(xs)
        pre_z(xs)
        pre_z(xs)
        load_g(0)
        pre_z(xs)
        assert len(pre) == NPRE * JC
        load_g(1)
        for _ in range(2):
            x = xs.take()
            tmp.give((x[0][0],), x[1])
        st["ahead"] = 4
        ag_t = {}

        def z_part(c):
            g = gch[c % 2][0].rearrange("p (b j t) -> p j b t", j=JC, t=TG)
            toks = []
            for j in range(JC):
                y = tmp.take()
                if c < NPRE:
                    x, a = (zch[c % 2][0][:, j, :], None), zl[c]
                else:
                    b, r = proj("eu", c * JC + j, hT)
                    x = tmp.take()
                    a = A(act.activation, x[0], b[0], ACT.Gelu_apprx_tanh, w=[r, x[1]])
                    banks.give(b, a)
                v = V(dve.tensor_tensor, y[0].rearrange("p (b t) -> p b t", t=TG),
                      x[0].rearrange("p (b t) -> p b t", t=TG), g[:, j, :, :], ALU.mult, w=[a, gl[c], y[1]])
                if c >= NPRE:
                    tmp.give(x, v)
                hi, lo = agb[c % 2][:, 0, j, :], agb[c % 2][:, 1, j, :]
                a = A(act.activation, hi, y[0], ACT.Copy, w=[v, afree[c % 2]])
                p = G(pool.tensor_tensor, lo, y[0], hi.bitcast(F32), ALU.subtract, w=[a])
                tmp.give(y, p)
                toks.append(p)
                yield
            gfree[c % 2] = [v]
            ag_t[c] = toks

        def v_part(c):
            us_ = []
            for j in range(JC):
                us_.append(unit_hl("ev", c * JC + j, nxt=False))
            x_toks = []
            for dt in range(8):
                b = banks.take()
                T.wait(b[1])
                for j in range(JC):
                    T.wait(us_[j][2], ag_t[c][j])
                    W = us_[j][1]
                    r = mm3(b[0], (W[:, 0, dt, :], W[:, 1, dt, :]),
                            (agb[c % 2][:, 0, j, :], agb[c % 2][:, 1, j, :]),
                            first=(j == 0), last=(j == JC - 1), inc=(j == JC - 1))
                x_toks.append(residual(b, r, dt))
                if dt % 2 == 0 and c < NC - 1 and st["split"] < st["used"] + 4:
                    split_next()
            for j in range(JC):
                wsl[0].give(us_[j][0], r)
            afree[c % 2] = [r]
            return x_toks

        run((z_part(0), 4))
        for c in range(NC):
            if c + 1 < NC:
                run((z_part(c + 1), 4))
                if c + 2 < NC:
                    load_g(c + 2)
            vlast = v_part(c)

        st["ahead"] = 1
        o = VOFF["g_ple"][0]
        stat = norm_stat(xT, vlast)
        gp = [z[0][:, j, :] for z in zch for j in range(JC)]
        pT = gch[0][0][:, 0:1024].rearrange("p (k s) -> p k s", k=2)
        p_tok = Y.dma(sp.dma_start, pT, t["pT"].rearrange("(k p) s -> p k s", p=128), s_ic, w=[gfree[0]])
        pj = []
        for u in range(2):
            W, tok = unit("plep", u)
            for i in range(4):
                b = banks.take()
                T.wait(tok, b[1], p_tok)
                for k in range(2):
                    r = T(pe.matmul, b[0], W[:, 2 * i + k, :], pT[:, k, :], start=(k == 0), stop=(k == 1),
                          inc=(k == 1))
                a = A(act.activation, gp[4 * u + i], b[0], ACT.Copy, w=[r])
                banks.give(b, a)
                pj.append(a)
            load_next(r)
        h_toks = norm_T(xT, hT, vec[:, o:o + 8], w=vlast, stat=stat)
        x_toks = []
        for m in range(8):
            b, r = proj("pleg", m, hT, wk=h_toks)
            y = tmp.take()
            a = A(act.activation, y[0], b[0], ACT.Sigmoid, w=[r, y[1]])
            banks.give(b, a)
            v = V(dve.tensor_tensor, gp[m], gp[m], y[0], ALU.mult, w=[a, pj[m]])
            tmp.give(y, v)
            x_toks.append(V(dve.tensor_tensor, xT[:, m, :], xT[:, m, :], gp[m], ALU.add, w=[v]))
        o = VOFF["g_final"][0]
        f_toks = norm_T(xT, None, vec[:, o:o + 8], w=x_toks)
        s_out = [sem("s_out"), 0]
        for m in range(4):
            o_tok = Y.dma(sp.dma_start, t["out"].rearrange("(k p) s -> p k s", p=128)[:, 2 * m:2 * m + 2, :],
                          xT[:, 2 * m:2 * m + 2, :], s_out, w=[f_toks[2 * m + 1]])
        Y.wait(o_tok)
        assert st["used"] == len(order)

        ctx.callback(ar.ctx.close)
        block = ctx.enter_context(nc.Block())

        @block.sync
        def _(eng):
            Y.play(eng)

        @block.scalar
        def _(eng):
            A.play(eng)

        @block.vector
        def _(eng):
            V.play(eng)

        @block.gpsimd
        def _(eng):
            G.play(eng)

        @block.tensor
        def _(eng):
            T.play(eng)


def _cols(v):
    return np.ascontiguousarray(np.asarray(v).reshape(-1, 128).T)


def _units(w, starts=None):
    w = np.asarray(w)
    K, N = w.shape
    starts = range(0, N, 128) if starts is None else starts
    out = []
    for s in starts:
        for kh in range(0, K, 1024):
            out.append(w[kh:kh + 1024, s:s + 128].reshape(8, 128, 128).transpose(1, 0, 2).reshape(128, 1024))
    return np.ascontiguousarray(np.stack(out))


def _constants():
    i = np.arange(128)
    strict = (i[:, None] < i[None, :])
    incl = (i[:, None] <= i[None, :])
    m = np.concatenate([strict, incl], 1).astype(np.uint32)
    lvl = np.zeros((7, 128, 128), np.float32)
    for l in range(7):
        s = 1 << l
        lvl[l] = ((i[:, None] // s) % 2 == 1) & (i[None, :] // s == i[:, None] // s - 1)
    lvh = np.concatenate([lvl[l].reshape(128, -1, 2, 1 << l)[:, :, 0, :].reshape(128, 64) for l in range(1, 7)], 1)
    lvl = -lvl[0].T
    icnt = np.zeros((4, S), np.float32)
    tt = np.arange(S)
    for g, w in enumerate((2, 4, 8, 16)):
        icnt[g] = 1.0 / (np.clip(tt + w // 2, 0, S) - np.clip(tt - w // 2, 0, S))
    return {
        "ident": np.eye(128, dtype=np.float32), "ones": np.ones((128, 128), np.float32),
        "bones": np.kron(np.eye(2), np.ones((64, 64))).astype(np.float32),
        "msk": np.concatenate([m, m], 1), "lvl": np.ascontiguousarray(lvl), "lvh": np.ascontiguousarray(lvh), "icnt": icnt,
        "iota16": np.arange(16, dtype=np.float32),
    }


def kernel(x, c, positions, ada_w, ada_b, norm_g, final_g, even_w_in, even_w_out, conv_w, conv_vec,
           rwkv_mu_rkv, rwkv_mu_lora, rwkv_vec, rwkv_w_up, rwkv_a_up, rwkv_r_k, odd_w_in, odd_w_out,
           p_2, g_mix_2, w_in_2, conv_w_2, pool_w_2, pool_scale_2, w_o_2, g_ffn_2, w_q_2, sub_keys_2,
           expert_u_2, expert_v_2, g_ple_2, w_ple_gate_2, w_ple_proj_2, g_final_2):
    import ml_dtypes
    import concourse.bacc as bacc
    from concourse.bass_utils import run_bass_kernel_spmd

    a = np.asarray
    f = {}
    f.update(_constants())
    f["iom"] = np.repeat(np.arange(128), 16).astype(ml_dtypes.bfloat16)
    f["xT"] = np.ascontiguousarray(a(x)[0].T)
    f["positions"] = np.ascontiguousarray(a(positions)[0])
    f["pcol"] = np.ascontiguousarray(a(positions)[0].reshape(4, 128).T)
    q = np.arange(128)
    inv = lambda d: (np.float32(10000.0) ** (-np.arange(0, d, 2, dtype=np.float32) / np.float32(d))).astype(np.float32)
    v = {
        "c": _cols(c), "norm_g0": _cols(a(norm_g)[0]), "norm_g1": _cols(a(norm_g)[1]), "final_g": _cols(final_g),
        "ada_b0": _cols(a(ada_b)[0]), "ada_b1": _cols(a(ada_b)[1]),
        "conv_b": _cols(a(conv_vec)[0, 0]), "ln_w": _cols(a(conv_vec)[0, 1]), "ln_b": _cols(a(conv_vec)[0, 2]),
        "mu_r": _cols(a(rwkv_mu_rkv)[0, 0]), "mu_k": _cols(a(rwkv_mu_rkv)[0, 1]), "mu_v": _cols(a(rwkv_mu_rkv)[0, 2]),
        "mu_l": a(rwkv_mu_lora)[0].reshape(128, 1), "r_k": _cols(a(rwkv_r_k)[0]),
        "conv_w": a(conv_w)[0, :, 0, :].reshape(TAPS, 8, 128).transpose(2, 1, 0).reshape(128, 8 * TAPS),
        "g_mix": _cols(a(g_mix_2)[0]), "g_ffn": _cols(a(g_ffn_2)[0]), "g_ple": _cols(a(g_ple_2)[0]),
        "g_final": _cols(g_final_2), "pool_s": _cols(a(pool_scale_2)[0]),
        "conv_w2": a(conv_w_2)[0].reshape(3, 4, 128).transpose(2, 1, 0).reshape(128, 12),
        "inv128": inv(128)[q % 64][:, None], "inv64": inv(64)[q % 32][:, None],
        "sgn128": np.where(q % 128 < 64, 1.0, -1.0).astype(np.float32)[:, None],
        "sgn64": np.where(q % 64 < 32, 1.0, -1.0).astype(np.float32)[:, None],
    }
    for i, n in enumerate(("w0", "a0", "k_k", "k_a", "gn_w", "gn_b")):
        v[n] = _cols(a(rwkv_vec)[0, i])
    f["vec"] = np.ascontiguousarray(np.concatenate([v[n] for n, _ in VECS], 1))
    f["lup"] = np.ascontiguousarray(np.concatenate([a(rwkv_w_up)[0], a(rwkv_a_up)[0]], 0))
    f["ada"] = np.ascontiguousarray(
        a(ada_w).reshape(2, 4, 2, 128, 6, 512).transpose(0, 4, 1, 3, 2, 5)).reshape(48, 128, 1024)
    f["ein"] = _units(a(even_w_in)[0])
    f["eout"] = _units(a(even_w_out)[0])
    w = a(odd_w_in)[0]
    ki, wi = w[:, 2816:2880], w[:, 2880:2888]
    pad = np.zeros((D, 120), w.dtype)
    f["oin"] = _units(np.concatenate([w[:, 0:2816], ki, ki, wi, pad, w[:, 2888:]], 1))
    f["oout"] = _units(a(odd_w_out)[0])
    f["win"] = _units(a(w_in_2)[0])
    pw = a(pool_w_2)[0].transpose(1, 0, 2).reshape(128, 512)
    f["pool"] = np.ascontiguousarray(np.concatenate([pw, np.zeros_like(pw)], 1))[None]
    f["wo"] = _units(a(w_o_2)[0])
    f["wq"] = _units(a(w_q_2)[0])
    sk = a(sub_keys_2)[0].reshape(2, 8, 128, 128)
    f["keys"] = np.ascontiguousarray(sk.transpose(0, 3, 1, 2).reshape(2, 128, 1024))
    f["eu"] = np.ascontiguousarray(
        a(expert_u_2)[0].reshape(128, 128, 8, 128).transpose(1, 3, 2, 0)).reshape(128, 128, 1024)
    f["ev"] = np.ascontiguousarray(a(expert_v_2)[0]).reshape(128, 128, 1024)
    f["pleg"] = _units(a(w_ple_gate_2)[0])
    wp = a(w_ple_proj_2)[0].reshape(2, 128, 2, 4, 128)
    f["plep"] = np.ascontiguousarray(wp.transpose(2, 1, 3, 0, 4)).reshape(2, 128, 1024)
    f["pT"] = np.ascontiguousarray(a(p_2)[0, 0].T)

    nc = bacc.Bacc("TRN2", target_bir_lowering=False, num_devices=1)
    t = {k: nc.dram_tensor(f"in_{k}", list(z.shape), mybir.dt.from_np(z.dtype), kind="ExternalInput").ap()
         for k, z in f.items()}
    t["zd"] = nc.dram_tensor("zd", [NPRE * JC, 128, 512], F32, kind="Internal").ap()
    t["yd"] = nc.dram_tensor("yd", [24, 128, 512], F32, kind="Internal").ap()
    t["out"] = nc.dram_tensor("out_0", [D, S], F32, kind="ExternalOutput").ap()
    t["gd"] = nc.dram_tensor("gd", [128 // JC, S // TG, 128, JC * TG], F32, kind="Internal").ap()
    build(nc, t)
    r = run_bass_kernel_spmd(nc, [{f"in_{k}": z for k, z in f.items()}], core_ids=[0])
    return np.ascontiguousarray(r.results[0]["out_0"].T)[None]
```
